# Optimizing a Trainium2 kernel written in Bass

```python
import jax, jax.numpy as jnp
from jax import lax
import numpy as np

D_MODEL = 1024
BATCH = 1
SEQ = 1024
DEPTH = 1
DEC_BATCH = 8
DEC_SEQ = 4
PAST_LEN = 2048
PAGE_SIZE = 128

GLA_HEADS = 4
GLA_DK = D_MODEL // 8
GLA_DV = D_MODEL // 4
GLA_RANK = 16
GLA_TAU = 16.0
GLA_CHUNK = 64
DIL_GROUPS = ((128, 1), (512, 4), (2048, 16))
N_DIL = 3
DIL_HEADS = 4
DIL_HD = D_MODEL // 8
MEM_LEN = 256
MEM_HEADS = 4
MEM_HD = D_MODEL // 8
ROPE_THETA = 10000.0
PEER_HEADS = 8
PEER_NKEYS = 128
PEER_N = PEER_NKEYS * PEER_NKEYS
PEER_DKEY = D_MODEL // 4
PEER_TOPK = 16
PEER_BLOCK = 128
N_BRANCH = 3
EPS = 1e-6
NEG = -1e30
IN_SIZES = (GLA_HEADS * GLA_DK, GLA_HEADS * GLA_DK, GLA_HEADS * GLA_DV, GLA_HEADS * GLA_DV,
            GLA_RANK, N_DIL * 3 * DIL_HEADS * DIL_HD, MEM_HEADS * MEM_HD, N_BRANCH * D_MODEL)
W_IN_COLS = sum(IN_SIZES)

kernel_name = "hybrid_gla_dilated_peer_step"

def rms_norm(x, g):
    xf = x.astype(jnp.float32)
    y = xf * lax.rsqrt(jnp.mean(xf * xf, axis=-1, keepdims=True) + EPS)
    return (y * g.astype(jnp.float32)).astype(x.dtype)

def rope(x, pos):
    hd = x.shape[-1]
    half = hd // 2
    inv = ROPE_THETA ** (-jnp.arange(half, dtype=jnp.float32) / half)
    ang = pos.astype(jnp.float32)[:, None] * inv[None, :]
    shp = (1, pos.shape[0]) + (1,) * (x.ndim - 3) + (half,)
    cos = jnp.cos(ang).reshape(shp)
    sin = jnp.sin(ang).reshape(shp)
    xf = x.astype(jnp.float32)
    x1, x2 = xf[..., :half], xf[..., half:]
    return jnp.concatenate([x1 * cos - x2 * sin, x2 * cos + x1 * sin], axis=-1).astype(x.dtype)

def masked_softmax(s, mask):
    s = jnp.where(mask, s, NEG)
    m = jnp.max(s, axis=-1, keepdims=True)
    e = jnp.exp(s - m)
    den = jnp.sum(e, axis=-1, keepdims=True)
    return e / den, (m + jnp.log(den))[..., 0]

def split_cols(z):
    idx, acc = [], 0
    for sz in IN_SIZES[:-1]:
        acc += sz
        idx.append(acc)
    return jnp.split(z, idx, axis=-1)

def gla_chunked(q, k, v, g, s0, chunk):
    B, S, H, dk = q.shape
    dv = v.shape[-1]
    nc = S // chunk

    def to_chunks(a):
        return a.reshape(B, nc, chunk, H, a.shape[-1]).transpose(1, 0, 3, 2, 4)

    tri = (jnp.arange(chunk)[:, None] >= jnp.arange(chunk)[None, :])[..., None]

    def step(st, inp):
        qc, kc, vc, gc = inp
        b = jnp.cumsum(gc.astype(jnp.float32), axis=2)
        diff = b[:, :, :, None, :] - b[:, :, None, :, :]
        decay = jnp.exp(jnp.where(tri, diff, 0.0)) * tri
        a = jnp.einsum('bhtd,bhsd,bhtsd->bhts', qc, kc, decay)
        o = (jnp.einsum('bhtd,bhde->bhte', qc * jnp.exp(b), st)
             + jnp.einsum('bhts,bhse->bhte', a, vc))
        bl = b[:, :, -1:, :]
        st_new = (jnp.exp(bl[:, :, 0, :])[..., None] * st
                  + jnp.einsum('bhsd,bhse->bhde', kc * jnp.exp(bl - b), vc))
        return st_new.astype(s0.dtype), o.astype(v.dtype)

    s_fin, o = lax.scan(step, s0, (to_chunks(q), to_chunks(k), to_chunks(v), to_chunks(g)))
    o = o.transpose(1, 0, 3, 2, 4).reshape(B, S, H, dv)
    return o, s_fin

def dilated_band(q, k, v, r, span):
    B, S, H, d = q.shape
    L = S // r
    nb = -(-L // span)
    Lp = nb * span

    def fold(a):
        a = a.reshape(B, L, r, H, d).transpose(0, 2, 1, 3, 4).reshape(B * r, L, H, d)
        a = jnp.pad(a, ((0, 0), (0, Lp - L), (0, 0), (0, 0)))
        return a.reshape(B * r, nb, span, H, d)

    def prev(a):
        return jnp.pad(a, ((0, 0), (1, 0), (0, 0), (0, 0), (0, 0)))[:, :-1]

    qb, kb, vb = fold(q), fold(k), fold(v)
    kk = jnp.concatenate([prev(kb), kb], axis=2)
    vv = jnp.concatenate([prev(vb), vb], axis=2)
    s = jnp.einsum('nbqhd,nbkhd->nbhqk', qb, kk).astype(jnp.float32) * (d ** -0.5)
    mq = jnp.arange(span)[:, None]
    mk = jnp.arange(2 * span)[None, :]
    dist = mq + span - mk
    band = (dist >= 0) & (dist <= span)
    blk = jnp.arange(nb)[:, None, None]
    mask = band[None] & ((blk > 0) | (mk >= span)[None])
    p, lse = masked_softmax(s, mask[None, :, None])
    o = jnp.einsum('nbhqk,nbkhd->nbqhd', p.astype(v.dtype), vv)
    o = o.reshape(B, r, Lp, H, d)[:, :, :L].transpose(0, 2, 1, 3, 4).reshape(B, S, H, d)
    lse = lse.transpose(0, 1, 3, 2).reshape(B, r, Lp, H)[:, :, :L].transpose(0, 2, 1, 3).reshape(B, S, H)
    return o, lse

def dilated_gather(q, k_buf, v_buf, k_new, v_new, r, span, window):
    Bd, T, H, d = q.shape
    wb = k_buf.shape[1]
    kk = jnp.concatenate([k_buf, k_new], axis=1)
    vv = jnp.concatenate([v_buf, v_new], axis=1)
    idx = wb + jnp.arange(T)[:, None] - r * jnp.arange(span + 1)[None, :]
    valid = idx >= 0
    idxc = jnp.maximum(idx, 0)
    kg = kk[:, idxc]
    vg = vv[:, idxc]
    s = jnp.einsum('bthd,btjhd->bhtj', q, kg).astype(jnp.float32) * (d ** -0.5)
    p, lse = masked_softmax(s, valid[None, None])
    o = jnp.einsum('bhtj,btjhd->bthd', p.astype(v_new.dtype), vg)
    keep = min(window, wb + T)
    return o, lse.transpose(0, 2, 1), kk[:, -keep:], vv[:, -keep:]

def peer(n, wq, keys, u_tab, v_tab):
    T, D = n.shape
    nblk = -(-T // PEER_BLOCK)
    xp = jnp.pad(n, ((0, nblk * PEER_BLOCK - T), (0, 0))).reshape(nblk, PEER_BLOCK, D)

    def blk(xb):
        qh = (xb @ wq).reshape(PEER_BLOCK, PEER_HEADS, 2, PEER_DKEY // 2)
        s = jnp.einsum('thcd,hckd->thck', qh, keys).astype(jnp.float32)
        sv, si = lax.top_k(s, PEER_TOPK)
        cand = (sv[:, :, 0, :, None] + sv[:, :, 1, None, :]).reshape(PEER_BLOCK, PEER_HEADS, -1)
        cidx = (si[:, :, 0, :, None] * PEER_NKEYS + si[:, :, 1, None, :]).reshape(PEER_BLOCK, PEER_HEADS, -1)
        sc, pos = lax.top_k(cand, PEER_TOPK)
        eidx = jnp.take_along_axis(cidx, pos, axis=-1)
        gw = jax.nn.softmax(sc, axis=-1)
        hpre = jnp.einsum('td,thkd->thk', xb, u_tab[eidx])
        act = (jax.nn.gelu(hpre.astype(jnp.float32), approximate=False) * gw).astype(xb.dtype)
        return jnp.einsum('thk,thkd->td', act, v_tab[eidx])

    out = lax.map(blk, xp).reshape(nblk * PEER_BLOCK, D)
    return out[:T]

def mem_kv(mem, mem_norm_g, w_mem_kv, mem_kn_g):
    B, M, _ = mem.shape
    kv = rms_norm(mem, mem_norm_g) @ w_mem_kv
    k, v = jnp.split(kv, 2, axis=-1)
    k = rms_norm(k.reshape(B, M, MEM_HEADS, MEM_HD), mem_kn_g)
    return k, v.reshape(B, M, MEM_HEADS, MEM_HD)

def layer(x, pos, mem_k, mem_v, gla_s0, gla_chunk, dil_bufs, w):
    (ln1_g, w_in, gla_wg2, gla_bg, gla_onorm_g, dil_qn_g, dil_kn_g, mem_qn_g,
     w_br_gla, w_br_dil, w_br_mem, w_out, ln2_g, peer_wq, peer_keys, peer_u, peer_v) = w
    B, S, D = x.shape
    n = rms_norm(x, ln1_g)
    q_g, k_g, v_g, r_g, a_g, dil_qkv, q_m, gates = split_cols(n @ w_in)

    qg = q_g.reshape(B, S, GLA_HEADS, GLA_DK) * (GLA_DK ** -0.5)
    kg = k_g.reshape(B, S, GLA_HEADS, GLA_DK)
    vg = v_g.reshape(B, S, GLA_HEADS, GLA_DV)
    lg = jax.nn.log_sigmoid((a_g @ gla_wg2 + gla_bg).astype(jnp.float32)) / GLA_TAU
    lg = lg.reshape(B, S, GLA_HEADS, GLA_DK)
    og, gla_state = gla_chunked(qg, kg, vg, lg, gla_s0, gla_chunk)
    og = rms_norm(og, gla_onorm_g) * jax.nn.silu(r_g.reshape(B, S, GLA_HEADS, GLA_DV))
    br_gla = og.reshape(B, S, -1) @ w_br_gla

    dq = dil_qkv.reshape(B, S, N_DIL, 3, DIL_HEADS, DIL_HD)
    qd = rope(rms_norm(dq[:, :, :, 0], dil_qn_g), pos)
    kd = rope(rms_norm(dq[:, :, :, 1], dil_kn_g), pos)
    vd = dq[:, :, :, 2]
    outs, lses, new_bufs = [], [], []
    for gi, (wd, r) in enumerate(DIL_GROUPS):
        span = wd // r
        qi, ki, vi = qd[:, :, gi], kd[:, :, gi], vd[:, :, gi]
        if dil_bufs is None:
            o, l = dilated_band(qi, ki, vi, r, span)
            keep = min(wd, S)
            nk, nv = ki[:, -keep:], vi[:, -keep:]
        else:
            kb, vb = dil_bufs[gi]
            o, l, nk, nv = dilated_gather(qi, kb, vb, ki, vi, r, span, wd)
        outs.append(o)
        lses.append(l)
        new_bufs.append((nk, nv))
    wts = jax.nn.softmax(jnp.stack(lses, axis=0), axis=0)
    od = jnp.sum(wts[..., None] * jnp.stack(outs, axis=0).astype(jnp.float32), axis=0).astype(x.dtype)
    br_dil = od.reshape(B, S, -1) @ w_br_dil

    qm = rms_norm(q_m.reshape(B, S, MEM_HEADS, MEM_HD), mem_qn_g)
    sm = jnp.einsum('bshd,bmhd->bhsm', qm, mem_k).astype(jnp.float32) * (MEM_HD ** -0.5)
    pm = jax.nn.softmax(sm, axis=-1).astype(x.dtype)
    om = jnp.einsum('bhsm,bmhd->bshd', pm, mem_v)
    br_mem = om.reshape(B, S, -1) @ w_br_mem

    gt = jax.nn.sigmoid(gates.reshape(B, S, N_BRANCH, D))
    merged = gt[:, :, 0] * br_gla + gt[:, :, 1] * br_dil + gt[:, :, 2] * br_mem
    h = x + merged @ w_out

    n2 = rms_norm(h, ln2_g)
    y = h + peer(n2.reshape(B * S, D), peer_wq, peer_keys, peer_u, peer_v).reshape(B, S, D)
    return y, gla_state, new_bufs

def setup_inputs(seed: int = 0) -> dict:
    key = jax.random.key(seed)
    ks = iter(jax.random.split(key, 64))
    f32 = jnp.float32

    def nrm(shape, scale=1.0):
        return jax.random.normal(next(ks), shape, f32) * scale

    def gain(dim):
        return 1.0 + 0.02 * jax.random.normal(next(ks), (dim,), f32)

    d = D_MODEL
    inp = {}
    inp["x_prompt"] = nrm((BATCH, SEQ, d))
    inp["x_sample"] = nrm((DEC_BATCH, DEC_SEQ, d))
    inp["mem_prompt"] = nrm((BATCH, MEM_LEN, d))
    inp["state_gla"] = nrm((DEC_BATCH, GLA_HEADS, GLA_DK, GLA_DV))
    for gi, (wd, r) in enumerate(DIL_GROUPS):
        wb = min(wd, PAST_LEN)
        inp["cache_dil_k%d" % gi] = nrm((DEC_BATCH, wb, DIL_HEADS, DIL_HD))
        inp["cache_dil_v%d" % gi] = nrm((DEC_BATCH, wb, DIL_HEADS, DIL_HD))
    inp["cache_mem_k"] = nrm((DEC_BATCH, MEM_LEN, MEM_HEADS, MEM_HD))
    inp["cache_mem_v"] = nrm((DEC_BATCH, MEM_LEN, MEM_HEADS, MEM_HD))
    inp["ln1_g"] = gain(d)
    inp["w_in"] = nrm((d, W_IN_COLS), d ** -0.5)
    inp["gla_wg2"] = nrm((GLA_RANK, GLA_HEADS * GLA_DK), GLA_RANK ** -0.5)
    inp["gla_bg"] = nrm((GLA_HEADS * GLA_DK,), 0.1)
    inp["gla_onorm_g"] = gain(GLA_DV)
    inp["dil_qn_g"] = gain(DIL_HD)
    inp["dil_kn_g"] = gain(DIL_HD)
    inp["mem_norm_g"] = gain(d)
    inp["w_mem_kv"] = nrm((d, 2 * MEM_HEADS * MEM_HD), d ** -0.5)
    inp["mem_qn_g"] = gain(MEM_HD)
    inp["mem_kn_g"] = gain(MEM_HD)
    inp["w_br_gla"] = nrm((GLA_HEADS * GLA_DV, d), (GLA_HEADS * GLA_DV) ** -0.5)
    inp["w_br_dil"] = nrm((DIL_HEADS * DIL_HD, d), (DIL_HEADS * DIL_HD) ** -0.5)
    inp["w_br_mem"] = nrm((MEM_HEADS * MEM_HD, d), (MEM_HEADS * MEM_HD) ** -0.5)
    inp["w_out"] = nrm((d, d), d ** -0.5)
    inp["ln2_g"] = gain(d)
    inp["peer_wq"] = nrm((d, PEER_HEADS * PEER_DKEY), d ** -0.5)
    inp["peer_keys"] = nrm((PEER_HEADS, 2, PEER_NKEYS, PEER_DKEY // 2), (PEER_DKEY // 2) ** -0.5)
    inp["peer_u"] = nrm((PEER_N, d), d ** -0.5)
    inp["peer_v"] = nrm((PEER_N, d), 0.5)
    return inp

def reference(x_prompt, x_sample, mem_prompt, state_gla,
              cache_dil_k0, cache_dil_v0, cache_dil_k1, cache_dil_v1, cache_dil_k2, cache_dil_v2,
              cache_mem_k, cache_mem_v,
              ln1_g, w_in, gla_wg2, gla_bg, gla_onorm_g, dil_qn_g, dil_kn_g,
              mem_norm_g, w_mem_kv, mem_qn_g, mem_kn_g,
              w_br_gla, w_br_dil, w_br_mem, w_out, ln2_g,
              peer_wq, peer_keys, peer_u, peer_v):
    w = (ln1_g, w_in, gla_wg2, gla_bg, gla_onorm_g, dil_qn_g, dil_kn_g, mem_qn_g,
         w_br_gla, w_br_dil, w_br_mem, w_out, ln2_g, peer_wq, peer_keys, peer_u, peer_v)
    B, S, _ = x_prompt.shape
    Bd, T, _ = x_sample.shape

    mem_k_p, mem_v_p = mem_kv(mem_prompt, mem_norm_g, w_mem_kv, mem_kn_g)
    s0 = jnp.zeros((B, GLA_HEADS, GLA_DK, GLA_DV), x_prompt.dtype)
    y_prompt = x_prompt
    for _ in range(DEPTH):
        y_prompt, gla_state_p, bufs_p = layer(y_prompt, jnp.arange(S, dtype=jnp.int32), mem_k_p, mem_v_p,
                                              s0, min(GLA_CHUNK, S), None, w)
    (dk0_p, dv0_p), (dk1_p, dv1_p), (dk2_p, dv2_p) = bufs_p

    bufs_in = ((cache_dil_k0, cache_dil_v0), (cache_dil_k1, cache_dil_v1), (cache_dil_k2, cache_dil_v2))
    pos_s = PAST_LEN + jnp.arange(T, dtype=jnp.int32)
    y_sample = x_sample
    for _ in range(DEPTH):
        y_sample, gla_state_s, bufs_s = layer(y_sample, pos_s, cache_mem_k, cache_mem_v,
                                              state_gla, T, bufs_in, w)
    (dk0_s, dv0_s), (dk1_s, dv1_s), (dk2_s, dv2_s) = bufs_s

    return (y_prompt, y_sample,
            gla_state_p, dk0_p, dv0_p, dk1_p, dv1_p, dk2_p, dv2_p, mem_k_p, mem_v_p,
            gla_state_s, dk0_s, dv0_s, dk1_s, dv1_s, dk2_s, dv2_s)


_drawn_inputs = setup_inputs


def setup_inputs(seed=0):
    import zlib

    import numpy as np

    out = dict(_drawn_inputs(seed))
    spreads = {}
    factors = {'gla_onorm_g': 7.258,
     'dil_qn_g': 21.159,
     'dil_kn_g': 9.018,
     'mem_norm_g': 2.828,
     'mem_qn_g': 6.124,
     'mem_kn_g': 3.298,
     'ln2_g': 4.059}
    for name, (base, spread) in spreads.items():
        noise = np.random.default_rng([zlib.crc32(name.encode()), seed]).standard_normal(out[name].shape)
        drawn = base * np.exp(spread * noise) if base else spread * noise
        out[name] = __import__('jax').numpy.asarray(drawn.astype(out[name].dtype))
    for name, factor in factors.items():
        out[name] = (out[name] * factor).astype(out[name].dtype)
    return out
```

```python
P = 128
D = 1024
KD = D // P
SEQ, DEC_B, DEC_T = 1024, 8, 4
NS = DEC_B * DEC_T
NT = SEQ // P
ROWS = SEQ + NS
H = 4
DK, DV, RANK = 128, 256, 16
NG = 3
MEM = 256
C_Q, C_K, C_V, C_R, C_A = 0, 512, 1024, 2048, 3072
C_DIL = C_A + RANK
C_QM = C_DIL + NG * 3 * 512
C_GATE = C_QM + 512
COLS = C_GATE + 3 * D
WINDOWS = ((128, 1), (512, 4), (2048, 16))
CACHES = [(f"d{kv}{g}", WINDOWS[g][0], g) for g in range(NG) for kv in "kv"]
PH, NKEY, TOPK, NEXP = 8, 128, 16, 128
EPS = 1e-6
NEG = -1e30
TABLES = "natural_log_exp_and_others"


def stage_semaphores(nc, ctx, tag):
    taken = []

    def sem(name):
        taken.append(nc.alloc_semaphore(tag + name))
        return taken[-1]

    def give_back():
        nc.clear_and_free_semaphores(taken)
        nc.all_engine_barrier()

    ctx.callback(give_back)
    return sem


def project(nc, d):
    import concourse.bass as bass
    from concourse import mybir
    from contextlib import ExitStack
    fp32, ACT, ALU = mybir.dt.float32, mybir.ActivationFunctionType, mybir.AluOpType

    CW = 470
    CHUNKS = COLS // CW
    tiles = [(P * t, P, False) for t in range(NT)] + [(SEQ, NS, False)] + [(P * t, P, True) for t in range(2)]
    XT = NT + 1
    BANKS = 6
    STEPS = 2 * XT
    USES = STEPS // BANKS
    MW = 512

    with ExitStack() as ctx:
        sb = lambda n, s: ctx.enter_context(nc.sbuf_tensor("pj_" + n, s, fp32))
        sem = stage_semaphores(nc, ctx, "pj_")
        xin = sb("xin", [P, 2, D])
        sq = sb("sq", [P, D])
        xn = sb("xn", [P, 2, D])
        g1, gm = sb("g1", [P, D]), sb("gm", [P, D])
        ident = sb("ident", [P, P])
        stat = sb("stat", [P, 3, len(tiles)])
        eps = sb("eps", [P, 1])
        nT = sb("nT", [P, KD, ROWS])
        nmT = sb("nmT", [P, KD, MEM])
        w = sb("w", [P, 2, KD, CW])
        wm = sb("wm", [P, KD, MW])
        zo = sb("zo", [P, BANKS, MW])
        ps = ctx.enter_context(nc.psum_tensor("pj_ps", [P, 8, 512], fp32))
        consts_in, eps_set = sem("consts_in"), sem("eps_set")
        x_in = [sem(f"x_in{i}") for i in range(2)]
        square_done, log_done, rms_done, xn_done = sem("square"), sem("log"), sem("rms"), sem("xn_done")
        halves_done, halves_out = sem("halves_done"), sem("halves_out")
        w_in = [sem(f"w_in{i}") for i in range(2)]
        w_used = sem("w_used")
        product_done = sem("product_done")
        bank_out = [sem(f"bank_out{i}") for i in range(BANKS)]
        stored = [sem(f"stored{i}") for i in range(BANKS)]
        cache_moved = sem("cache_moved")
        wm_in, wm_used = sem("wm_in"), sem("wm_used")

        block = ctx.enter_context(nc.Block())
        w_dram = d["w_in"].rearrange("(k p) n -> p k n", p=P)
        wm_dram = d["w_mem_kv"].rearrange("(k p) n -> p k n", p=P)

        @block.sync
        def _(sp):
            sp.dma_start(g1[:], d["ln1_g"].partition_broadcast(P)).then_inc(consts_in, 16)
            sp.dma_start(gm[:], d["mem_norm_g"].partition_broadcast(P)).then_inc(consts_in, 16)
            sp.dma_start(ident[:], d["ident"]).then_inc(consts_in, 16)
            for s in stored:
                sp.sem_inc(s, 16)
            for t, (row, n, mem) in enumerate(tiles):
                if t >= 2:
                    sp.wait_ge(xn_done, t - 1)
                src = d["mem_prompt"][row:row + n, :] if mem else d["x"][0][row:row + n, :] if row < SEQ else d["x"][1]
                sp.dma_start(xin[0:n, t % 2, :], src).then_inc(x_in[t % 2], 16)
            with sp.Fori(0, CHUNKS // 2) as i:
                for s in range(STEPS):
                    c, t = divmod(s, XT)
                    row, n, _ = tiles[t]
                    sp.wait_ge(bank_out[s % BANKS], i * USES + s // BANKS + 2)
                    sp.dma_start(d["z"][row:row + n, bass.ds(i * 2 * CW + c * CW, CW)],
                                 zo[0:n, s % BANKS, 0:CW]).then_inc(stored[s % BANKS], 16)
            for s in range(4):
                c, t = divmod(s, 2)
                sp.wait_ge(bank_out[s], USES * CHUNKS // 2 + 2)
                sp.dma_start(d["zm"][P * t:P * t + P, c * MW:(c + 1) * MW], zo[:, s, :]).then_inc(stored[s], 16)
            for s in range(BANKS):
                sp.wait_ge(stored[s], 16 * (1 + USES * CHUNKS // 2 + (s < 4)))

        @block.gpsimd
        def _(pool):
            pool.sem_inc(w_used, 2)
            with pool.Fori(0, CHUNKS // 2) as i:
                for c in range(2):
                    pool.wait_ge(w_used, i * 2 + c + 1)
                    pool.dma_start(w[:, c], w_dram[:, :, bass.ds(i * 2 * CW + c * CW, CW)]).then_inc(w_in[c], 16)
            for c in range(2):
                if c:
                    pool.wait_ge(wm_used, 1)
                pool.dma_start(wm[:], wm_dram[:, :, c * MW:(c + 1) * MW]).then_inc(wm_in, 16)

        def evacuate(act, t):
            row, n, mem = tiles[t]
            dst = nmT[:, :, row:row + n] if mem else nT[:, :, row:row + n]
            for h in range(2):
                act.wait_ge(halves_done, 2 * t + h + 1)
                src = ps[:, 6 + h, :].rearrange("p (k t) -> p k t", k=4)[:, :, 0:n]
                nc.scalar.copy(dst[:, 4 * h:4 * h + 4, :], src).then_inc(halves_out, 1)

        @block.scalar
        def _(act):
            for name, wd, _ in CACHES:
                for b in range(DEC_B):
                    old = d[f"cache_{name[:-1].replace('d', 'dil_')}{name[-1]}"][b]
                    kept = old[DEC_T:wd, :].rearrange("w n -> (w n)").rearrange("(s x) -> s x", s=P)
                    new = d[f"{name}_s"][b][0:wd - DEC_T, :].rearrange("w n -> (w n)").rearrange("(s x) -> s x", s=P)
                    act.dma_start(new, kept).then_inc(cache_moved, 16)
            nc.scalar.preload_act_table_set(TABLES)
            act.wait_ge(eps_set, 1)
            for t, (row, n, mem) in enumerate(tiles):
                act.wait_ge(x_in[t % 2], 16 * (t // 2 + 1))
                if t:
                    act.wait_ge(square_done, t)
                nc.scalar.activation(sq[0:n, :], xin[0:n, t % 2, :], ACT.Square,
                                     accum_out=stat[0:n, 0, t:t + 1]).then_inc(square_done, 1)
                act.wait_ge(square_done, t + 1)
                nc.scalar.activation(stat[0:n, 1, t:t + 1], stat[0:n, 0, t:t + 1], ACT.Ln,
                                     bias=eps[0:n, :], scale=1.0 / D).then_inc(log_done, 1)
                act.wait_ge(log_done, t + 1)
                nc.scalar.activation(stat[0:n, 2, t:t + 1], stat[0:n, 1, t:t + 1], ACT.Exp,
                                     scale=-0.5).then_inc(rms_done, 1)
                if t:
                    evacuate(act, t - 1)
            evacuate(act, len(tiles) - 1)
            for b in range(0, BANKS, 2):
                act.sem_inc(bank_out[b], 1)
            with act.Fori(0, CHUNKS // 2) as i:
                for s in range(0, STEPS, 2):
                    n = tiles[s % XT][1]
                    act.wait_ge(product_done, i * STEPS + s + 1)
                    act.wait_ge(stored[s % BANKS], i * (16 * USES) + 16 * (s // BANKS + 1))
                    nc.scalar.copy(zo[0:n, s % BANKS, 0:CW], ps[0:n, s % BANKS, 0:CW]).then_inc(bank_out[s % BANKS], 1)
            for s in (0, 2):
                act.wait_ge(product_done, STEPS * CHUNKS // 2 + s + 1)
                act.wait_ge(stored[s], 16 * (1 + USES * CHUNKS // 2))
                nc.scalar.copy(zo[:, s, :], ps[:, s, :]).then_inc(bank_out[s], 1)
            act.wait_ge(cache_moved, 16 * DEC_B * len(CACHES))

        @block.vector
        def _(dve):
            nc.vector.memset(eps[:], EPS).then_inc(eps_set, 1)
            dve.wait_ge(consts_in, 48)
            for t, (row, n, mem) in enumerate(tiles):
                dve.wait_ge(rms_done, t + 1)
                if t >= 2:
                    dve.wait_ge(halves_done, 2 * (t - 1))
                gain = gm if mem else g1
                nc.vector.scalar_tensor_tensor(out=xn[0:n, t % 2, :], in0=xin[0:n, t % 2, :],
                                               scalar=stat[0:n, 2, t:t + 1], in1=gain[0:n, :],
                                               op0=ALU.mult, op1=ALU.mult).then_inc(xn_done, 1)
            for b in range(1, BANKS, 2):
                dve.sem_inc(bank_out[b], 1)
            with dve.Fori(0, CHUNKS // 2) as i:
                for s in range(1, STEPS, 2):
                    n = tiles[s % XT][1]
                    dve.wait_ge(product_done, i * STEPS + s + 1)
                    dve.wait_ge(stored[s % BANKS], i * (16 * USES) + 16 * (s // BANKS + 1))
                    nc.vector.tensor_copy(zo[0:n, s % BANKS, 0:CW], ps[0:n, s % BANKS, 0:CW]).then_inc(bank_out[s % BANKS], 1)
            for s in (1, 3):
                dve.wait_ge(product_done, STEPS * CHUNKS // 2 + s + 1)
                dve.wait_ge(stored[s], 16 * (1 + USES * CHUNKS // 2))
                nc.vector.tensor_copy(zo[:, s, :], ps[:, s, :]).then_inc(bank_out[s], 1)

        @block.tensor
        def _(pe):
            pe.wait_ge(consts_in, 48)
            for t, (row, n, mem) in enumerate(tiles):
                pe.wait_ge(xn_done, t + 1)
                for h in range(2):
                    if t:
                        pe.wait_ge(halves_out, 2 * t - 1 + h)
                    for k in range(4):
                        last = nc.tensor.transpose(ps[:, 6 + h, P * k:P * k + n],
                                                   xn[0:n, t % 2, P * (4 * h + k):P * (4 * h + k + 1)],
                                                   ident[0:n, 0:n])
                    last.then_inc(halves_done, 1)
            pe.wait_ge(halves_out, 2 * len(tiles))
            with pe.Fori(0, CHUNKS // 2) as i:
                for s in range(STEPS):
                    c, t = divmod(s, XT)
                    row, n, _ = tiles[t]
                    if t == 0:
                        pe.wait_ge(w_in[c], i * 16 + 16)
                    pe.wait_ge(bank_out[s % BANKS], i * USES + s // BANKS + 1)
                    for k in range(KD):
                        last = nc.tensor.matmul(ps[0:n, s % BANKS, 0:CW], nT[:, k, row:row + n], w[:, c, k, :],
                                                start=(k == 0), stop=(k == KD - 1))
                    last.then_inc(product_done, 1)
                    if t == XT - 1:
                        pe.wait_ge(product_done, i * STEPS + s + 1)
                        pe.sem_inc(w_used, 1)
            for s in range(4):
                c, t = divmod(s, 2)
                if t == 0:
                    pe.wait_ge(wm_in, 16 * (c + 1))
                pe.wait_ge(bank_out[s], USES * CHUNKS // 2 + 1)
                for k in range(KD):
                    last = nc.tensor.matmul(ps[:, s, :], nmT[:, k, P * t:P * t + P], wm[:, k, :],
                                            start=(k == 0), stop=(k == KD - 1))
                last.then_inc(product_done, 1)
                if s == 1:
                    pe.wait_ge(product_done, STEPS * CHUNKS // 2 + 2)
                    pe.sem_inc(wm_used, 1)


class Signal:

    def __init__(self, sem, per=1):
        self.sem, self.per = sem, per

    def prime(self, eng):
        eng.sem_inc(self.sem, 2 * self.per)

    def at(self, turn, done=None, back=0):
        return turn * self.per + (2 - back) * self.per + (self.per if done is None else done)


def gla(nc, d):
    import concourse.bass as bass
    from concourse import mybir
    from contextlib import ExitStack
    fp32, ACT, ALU = mybir.dt.float32, mybir.ActivationFunctionType, mybir.AluOpType
    SUB = 16
    NSUB = P // SUB
    TAU = 16.0
    CAP = 70.0 * TAU

    with ExitStack() as ctx:
        sb = lambda n, s: ctx.enter_context(nc.sbuf_tensor("gl_" + n, s, fp32))
        pb = lambda n, s: ctx.enter_context(nc.psum_tensor("gl_" + n, s, fp32))
        sem = stage_semaphores(nc, ctx, "gl_")
        signals = []

        def signal(n, per=1):
            signals.append(Signal(sem(n), per))
            return signals[-1]

        ident, causal = sb("ident", [P, P]), sb("causal", [P, P])
        wg2, bg = sb("wg2", [RANK, 512]), sb("bg", [P, H])
        gn = sb("gn", [P, DV])
        eps, ones = sb("eps", [P, 1]), sb("ones", [P, P])
        qk, v = sb("qk", [P, 2, 2 * H, DK]), sb("v", [P, 2, H, DV])
        r, a = sb("r", [P, 2, H * DV]), sb("a", [P, 2, RANK])
        aT = sb("aT", [RANK, P])
        qkT = sb("qkT", [P, 2 * H, P])
        x0, x1, x2 = sb("x0", [P, H, P]), sb("x1", [P, H, P]), sb("x2", [P, H, P])
        b = sb("b", [P, H, P])
        ref = sb("ref", [P, H, NSUB])
        eb, eq, ek = sb("eb", [P, H, P]), sb("eq", [P, H, P]), sb("ek", [P, H, P])
        qs, qin, kin = sb("qs", [P, H, P]), sb("qin", [P, H, P]), sb("kin", [P, H, P])
        kinT = sb("kinT", [P, H, DK])
        kx = sb("kx", [P, 2, NSUB, P])
        A = sb("A", [P, H, P])
        S = sb("S", [P, H, DV])
        sq, stat = sb("sq", [P, H, DV]), sb("stat", [P, 3, H])
        er, u = sb("er", [P, H * DV]), sb("u", [P, H * DV])
        og = sb("og", [P, 2, H * DV])
        ps_t, ps_g, ps_a = pb("ps_t", [P, 2 * H, P]), pb("ps_g", [P, H, P]), pb("ps_a", [P, H, P])
        ps_k, ps_o = pb("ps_k", [P, H, P]), pb("ps_o", [P, H, DV])
        ps_kv = ps_t[:, :, :].rearrange("p (h two) t -> p h (two t)", two=2)

        consts_in, set_up = sem("consts_in"), sem("set_up")
        z_in = [sem(f"z_in{i}") for i in range(2)]
        stored = [sem(f"stored{i}") for i in range(2)]
        a_t, a_out, gate = signal("a_t"), signal("a_out"), signal("gate")
        qk_t, qk_out = signal("qk_t"), signal("qk_out", 2)
        x0_done, neg_done, abs_done = signal("x0_done"), signal("neg_done"), signal("abs_done")
        exp_done, ln_done, lg_done = signal("exp_done"), signal("ln_done"), signal("lg_done")
        b_done, ref_done, dq_done, dk_done = signal("b_done"), signal("ref_done"), signal("dq_done"), signal("dk_done")
        eb_done, eq_done, ek_done = signal("eb_done"), signal("eq_done"), signal("ek_done")
        qs_done, qin_done, kin_done = signal("qs_done"), signal("qin_done"), signal("kin_done")
        kx_sub, kx_min, kx_exp = signal("kx_sub", H), signal("kx_min", H), signal("kx_exp", H)
        kx_done, scores, A_done = signal("kx_done", H), signal("scores", H), signal("A_done")
        kin_t, kinT_out = signal("kin_t"), signal("kinT_out")
        o_done, kv_done, S_done = signal("o_done"), signal("kv_done"), signal("S_done")
        sq_done, lnv_done, rms_done, u_done = signal("sq_done"), signal("lnv_done"), signal("rms_done"), signal("u_done")
        er_done, er1_done, sig_done = signal("er_done"), signal("er1_done"), signal("sig_done")
        swish_done, og_done = signal("swish_done"), signal("og_done")

        block = ctx.enter_context(nc.Block())
        z = d["z"]

        def turns(eng):
            with eng.Fori(0, NT // 2) as i:
                for j in range(2):
                    yield i * 2 + j, i, j

        @block.sync
        def _(sp):
            for dst, src in ((ident[:], d["ident"]), (causal[:], d["causal"]), (wg2[:], d["gla_wg2"]),
                             (gn[:], d["gla_onorm_g"].partition_broadcast(P))):
                sp.dma_start(dst, src).then_inc(consts_in, 16)
            with nc.allow_non_contiguous_dma(reason="a bias of 512 numbers, once"):
                sp.dma_start(bg[:], d["gla_bg"].rearrange("(h p) -> p h", p=P)).then_inc(consts_in, 16)
            for s in stored:
                sp.sem_inc(s, 16)
            for s in signals:
                s.prime(sp)

            def load(i, j):
                rows, turn = bass.ds(i * 2 * P + j * P, P), i * 2 + j
                sp.wait_ge(kv_done.sem, kv_done.at(turn, back=2))
                sp.wait_ge(swish_done.sem, swish_done.at(turn, back=2))
                sp.wait_ge(er_done.sem, er_done.at(turn, back=2))
                sp.dma_start(a[:, j, :], z[rows, C_A:C_A + RANK]).then_inc(z_in[j], 16)
                sp.dma_start(qk[:, j, :, :], z[rows, C_Q:C_Q + 2 * H * DK].rearrange("t (h e) -> t h e", e=DK)).then_inc(z_in[j], 16)
                sp.dma_start(v[:, j, :, :], z[rows, C_V:C_V + H * DV].rearrange("t (h e) -> t h e", e=DV)).then_inc(z_in[j], 16)
                sp.dma_start(r[:, j, :], z[rows, C_R:C_R + H * DV]).then_inc(z_in[j], 16)

            def store(i, j):
                sp.wait_ge(og_done.sem, og_done.at(i * 2 + j))
                sp.dma_start(d["acts"][bass.ds(i * 2 * P + j * P, P), 0:H * DV], og[:, j, :]).then_inc(stored[j], 16)

            load(0, 0)
            load(0, 1)
            with sp.Fori(0, NT // 2 - 1) as i:
                for j in range(2):
                    store(i, j)
                    load(i + 1, j)
            for j in range(2):
                store(NT // 2 - 1, j)
                sp.wait_ge(stored[j], 16 * (NT // 2 + 1))
            sp.wait_ge(S_done.sem, NT + 2)
            sp.dma_start(d["gla_state_p"].rearrange("h p e -> p h e"), S[:]).then_inc(consts_in, 16)
            sp.wait_ge(consts_in, 6 * 16)

        @block.gpsimd
        def _(pool):
            for turn, i, j in turns(pool):
                pool.wait_ge(qk_out.sem, qk_out.at(turn))
                pool.wait_ge(eq_done.sem, eq_done.at(turn))
                pool.wait_ge(scores.sem, scores.at(turn, back=1))
                nc.gpsimd.tensor_tensor(qs[:], qkT[:, 0:H, :], eq[:], ALU.mult).then_inc(qs_done.sem, 1)
                for h in range(H):
                    pool.wait_ge(kx_exp.sem, kx_exp.at(turn, h + 1))
                    nc.gpsimd.tensor_tensor(kx[:, h % 2], kx[:, h % 2],
                                            qkT[:, H + h, :].unsqueeze(1).to_broadcast([P, NSUB, P]),
                                            ALU.mult).then_inc(kx_done.sem, 1)
                pool.wait_ge(eb_done.sem, eb_done.at(turn))
                pool.wait_ge(o_done.sem, o_done.at(turn, back=1))
                nc.gpsimd.tensor_tensor(qin[:], qkT[:, 0:H, :], eb[:], ALU.mult).then_inc(qin_done.sem, 1)
                pool.wait_ge(ek_done.sem, ek_done.at(turn))
                pool.wait_ge(kin_t.sem, kin_t.at(turn, back=1))
                nc.gpsimd.tensor_tensor(kin[:], qkT[:, H:, :], ek[:], ALU.mult).then_inc(kin_done.sem, 1)
                pool.wait_ge(sig_done.sem, sig_done.at(turn))
                nc.gpsimd.tensor_tensor(er[:], r[:, j, :], er[:], ALU.mult).then_inc(swish_done.sem, 1)
                pool.wait_ge(swish_done.sem, swish_done.at(turn))
                pool.wait_ge(u_done.sem, u_done.at(turn))
                pool.wait_ge(stored[j], i * 16 + 16)
                nc.gpsimd.tensor_tensor(og[:, j, :], u[:], er[:], ALU.mult).then_inc(og_done.sem, 1)

        @block.scalar
        def _(act):
            nc.scalar.preload_act_table_set(TABLES)
            act.wait_ge(set_up, 3)
            for turn, i, j in turns(act):
                act.wait_ge(a_t.sem, a_t.at(turn))
                nc.scalar.copy(aT[:], ps_g[0:RANK, 0, :]).then_inc(a_out.sem, 1)
                act.wait_ge(qk_t.sem, qk_t.at(turn))
                act.wait_ge(kin_done.sem, kin_done.at(turn, back=1))
                nc.scalar.mul(qkT[:, 0:H, :], ps_t[:, 0:H, :], DK ** -0.5).then_inc(qk_out.sem, 1)
                nc.scalar.copy(qkT[:, H:, :], ps_t[:, H:, :]).then_inc(qk_out.sem, 1)
                act.wait_ge(x0_done.sem, x0_done.at(turn))
                nc.scalar.activation(x1[:], x0[:], ACT.Abs).then_inc(abs_done.sem, 1)
                act.wait_ge(abs_done.sem, abs_done.at(turn))
                nc.scalar.activation(x1[:], x1[:], ACT.Exp, scale=-1.0).then_inc(exp_done.sem, 1)
                act.wait_ge(exp_done.sem, exp_done.at(turn))
                nc.scalar.activation(x1[:], x1[:], ACT.Ln, bias=1.0).then_inc(ln_done.sem, 1)
                act.wait_ge(dq_done.sem, dq_done.at(turn))
                nc.scalar.activation(eq[:], eq[:], ACT.Exp, scale=1.0 / TAU).then_inc(eq_done.sem, 1)
                for h in range(H):
                    act.wait_ge(kx_min.sem, kx_min.at(turn, h + 1))
                    nc.scalar.activation(kx[:, h % 2], kx[:, h % 2], ACT.Exp, scale=1.0 / TAU).then_inc(kx_exp.sem, 1)
                act.wait_ge(b_done.sem, b_done.at(turn))
                act.wait_ge(qin_done.sem, qin_done.at(turn, back=1))
                act.wait_ge(S_done.sem, S_done.at(turn, back=1))
                nc.scalar.activation(eb[:], b[:], ACT.Exp, scale=1.0 / TAU).then_inc(eb_done.sem, 1)
                act.wait_ge(dk_done.sem, dk_done.at(turn))
                nc.scalar.activation(ek[:], ek[:], ACT.Exp, scale=1.0 / TAU).then_inc(ek_done.sem, 1)
                act.wait_ge(z_in[j], i * 64 + 64)
                act.wait_ge(og_done.sem, og_done.at(turn, back=1))
                nc.scalar.activation(er[:], r[:, j, :], ACT.Exp, scale=-1.0).then_inc(er_done.sem, 1)
                act.wait_ge(kin_t.sem, kin_t.at(turn))
                nc.scalar.copy(kinT[:], ps_k[:]).then_inc(kinT_out.sem, 1)
                act.wait_ge(o_done.sem, o_done.at(turn))
                for h in range(H):
                    last = nc.scalar.activation(sq[:, h, :], ps_o[:, h, :], ACT.Square, accum_out=stat[:, 0, h:h + 1])
                last.then_inc(sq_done.sem, 1)
                act.wait_ge(sq_done.sem, sq_done.at(turn))
                nc.scalar.activation(stat[:, 1, :], stat[:, 0, :], ACT.Ln, bias=eps[:], scale=1.0 / DV).then_inc(lnv_done.sem, 1)
                act.wait_ge(lnv_done.sem, lnv_done.at(turn))
                act.wait_ge(u_done.sem, u_done.at(turn, back=1))
                nc.scalar.activation(stat[:, 2, :], stat[:, 1, :], ACT.Exp, scale=-0.5).then_inc(rms_done.sem, 1)

        @block.vector
        def _(dve):
            nc.vector.memset(ref[:], 0.0).then_inc(set_up, 1)
            nc.vector.memset(ones[:], 1.0).then_inc(set_up, 1)
            nc.vector.memset(eps[:], EPS).then_inc(set_up, 1)
            nc.vector.memset(S[:], 0.0).then_inc(set_up, 1)
            dve.wait_ge(set_up, 4)
            dve.wait_ge(consts_in, 5 * 16)
            for turn, i, j in turns(dve):
                dve.wait_ge(gate.sem, gate.at(turn))
                nc.vector.tensor_tensor(x0[:], ps_g[:], bg[:].unsqueeze(2).to_broadcast([P, H, P]), ALU.add).then_inc(x0_done.sem, 1)
                dve.wait_ge(x0_done.sem, x0_done.at(turn))
                nc.vector.tensor_scalar(x2[:], x0[:], 0.0, None, ALU.min).then_inc(neg_done.sem, 1)
                dve.wait_ge(neg_done.sem, neg_done.at(turn))
                dve.wait_ge(ln_done.sem, ln_done.at(turn))
                nc.vector.tensor_tensor(x2[:], x2[:], x1[:], ALU.subtract).then_inc(lg_done.sem, 1)
                dve.wait_ge(lg_done.sem, lg_done.at(turn))
                dve.wait_ge(eb_done.sem, eb_done.at(turn, back=1))
                for h in range(H):
                    last = nc.vector.tensor_tensor_scan(b[:, h, :], ones[:], x2[:, h, :], 0.0, ALU.mult, ALU.add)
                last.then_inc(b_done.sem, 1)
                dve.wait_ge(b_done.sem, b_done.at(turn))
                nc.vector.tensor_copy(ref[:, :, 1:NSUB], b[:, :, SUB - 1:P - 1:SUB]).then_inc(ref_done.sem, 1)
                dve.wait_ge(ref_done.sem, ref_done.at(turn))
                dve.wait_ge(qs_done.sem, qs_done.at(turn, back=1))
                nc.vector.tensor_tensor(eq[:].rearrange("p h (s t) -> p (h s) t", t=SUB),
                                        b[:].rearrange("p h (s t) -> p (h s) t", t=SUB),
                                        ref[:].rearrange("p h s -> p (h s)").unsqueeze(2).to_broadcast([P, H * NSUB, SUB]),
                                        ALU.subtract).then_inc(dq_done.sem, 1)
                for h in range(H):
                    if h < 2:
                        dve.wait_ge(scores.sem, scores.at(turn, h + 3, back=1))
                    else:
                        dve.wait_ge(scores.sem, scores.at(turn, h - 1))
                    nc.vector.tensor_tensor(kx[:, h % 2], ref[:, h, :].unsqueeze(2).to_broadcast([P, NSUB, P]),
                                            b[:, h, :].unsqueeze(1).to_broadcast([P, NSUB, P]),
                                            ALU.subtract).then_inc(kx_sub.sem, 1)
                    dve.wait_ge(kx_sub.sem, kx_sub.at(turn, h + 1))
                    nc.vector.tensor_scalar(kx[:, h % 2], kx[:, h % 2], CAP, None, ALU.min).then_inc(kx_min.sem, 1)
                    if h == 0:
                        dve.wait_ge(kin_done.sem, kin_done.at(turn, back=1))
                        nc.vector.tensor_tensor(ek[:], b[:, :, P - 1:P].to_broadcast([P, H, P]), b[:],
                                                ALU.subtract).then_inc(dk_done.sem, 1)
                dve.wait_ge(scores.sem, scores.at(turn))
                dve.wait_ge(o_done.sem, o_done.at(turn, back=1))
                nc.vector.tensor_tensor(A[:], ps_a[:], causal[:].unsqueeze(1).to_broadcast([P, H, P]), ALU.mult).then_inc(A_done.sem, 1)
                dve.wait_ge(er_done.sem, er_done.at(turn))
                nc.vector.tensor_scalar(er[:], er[:], 1.0, None, ALU.add).then_inc(er1_done.sem, 1)
                dve.wait_ge(er1_done.sem, er1_done.at(turn))
                nc.vector.reciprocal(er[:], er[:]).then_inc(sig_done.sem, 1)
                dve.wait_ge(kv_done.sem, kv_done.at(turn))
                dve.wait_ge(o_done.sem, o_done.at(turn))
                for h in range(H):
                    last = nc.vector.scalar_tensor_tensor(out=S[:, h, :], in0=S[:, h, :], scalar=eb[:, h, P - 1:P],
                                                          in1=ps_kv[:, h, :], op0=ALU.mult, op1=ALU.add)
                last.then_inc(S_done.sem, 1)
                dve.wait_ge(rms_done.sem, rms_done.at(turn))
                dve.wait_ge(og_done.sem, og_done.at(turn, back=1))
                for h in range(H):
                    last = nc.vector.scalar_tensor_tensor(out=u[:, h * DV:(h + 1) * DV], in0=ps_o[:, h, :],
                                                          scalar=stat[:, 2, h:h + 1], in1=gn[:], op0=ALU.mult, op1=ALU.mult)
                last.then_inc(u_done.sem, 1)

        @block.tensor
        def _(pe):
            pe.wait_ge(consts_in, 5 * 16)
            pe.wait_ge(set_up, 4)
            for turn, i, j in turns(pe):
                pe.wait_ge(z_in[j], i * 64 + 64)
                pe.wait_ge(x0_done.sem, x0_done.at(turn, back=1))
                nc.tensor.transpose(ps_g[0:RANK, 0, :], a[:, j, :], ident[:]).then_inc(a_t.sem, 1)
                pe.wait_ge(S_done.sem, S_done.at(turn, back=1))
                for h in range(2 * H):
                    last = nc.tensor.transpose(ps_t[:, h, :], qk[:, j, h, :], ident[:])
                last.then_inc(qk_t.sem, 1)
                pe.wait_ge(a_out.sem, a_out.at(turn))
                for h in range(H):
                    last = nc.tensor.matmul(ps_g[:, h, :], wg2[:, h * DK:(h + 1) * DK], aT[:], start=True, stop=True)
                last.then_inc(gate.sem, 1)
                pe.wait_ge(qs_done.sem, qs_done.at(turn))
                pe.wait_ge(A_done.sem, A_done.at(turn, back=1))
                for h in range(H):
                    pe.wait_ge(kx_done.sem, kx_done.at(turn, h + 1))
                    for s in range(NSUB):
                        last = nc.tensor.matmul(ps_a[:, h, s * SUB:(s + 1) * SUB], kx[:, h % 2, s, :],
                                                qs[:, h, s * SUB:(s + 1) * SUB], start=True, stop=True)
                    last.then_inc(scores.sem, 1)
                pe.wait_ge(kin_done.sem, kin_done.at(turn))
                pe.wait_ge(kinT_out.sem, kinT_out.at(turn, back=1))
                for h in range(H):
                    last = nc.tensor.transpose(ps_k[:, h, :], kin[:, h, :], ident[:])
                last.then_inc(kin_t.sem, 1)
                pe.wait_ge(A_done.sem, A_done.at(turn))
                pe.wait_ge(qin_done.sem, qin_done.at(turn))
                pe.wait_ge(u_done.sem, u_done.at(turn, back=1))
                for h in range(H):
                    nc.tensor.matmul(ps_o[:, h, :], A[:, h, :], v[:, j, h, :], start=True, stop=False)
                    last = nc.tensor.matmul(ps_o[:, h, :], qin[:, h, :], S[:, h, :], start=False, stop=True)
                last.then_inc(o_done.sem, 1)
                pe.wait_ge(kinT_out.sem, kinT_out.at(turn))
                pe.wait_ge(qk_out.sem, qk_out.at(turn))
                for h in range(H):
                    last = nc.tensor.matmul(ps_kv[:, h, :], kinT[:, h, :], v[:, j, h, :], start=True, stop=True)
                last.then_inc(kv_done.sem, 1)


def gla_sample(nc, d):
    from concourse import mybir
    from contextlib import ExitStack
    fp32, ACT, ALU = mybir.dt.float32, mybir.ActivationFunctionType, mybir.AluOpType
    TAU = 16.0
    CAP = 70.0 * TAU
    B, T = DEC_B, DEC_T
    HC = 2 * H

    with ExitStack() as ctx:
        sb = lambda n, s: ctx.enter_context(nc.sbuf_tensor("gs_" + n, s, fp32))
        pb = lambda n, s: ctx.enter_context(nc.psum_tensor("gs_" + n, s, fp32))
        sem = stage_semaphores(nc, ctx, "gs_")
        ident, restart = sb("ident", [P, P]), sb("restart", [P, NS])
        own, own_causal = sb("own", [NS, B]), sb("own_causal", [NS, NS])
        wg2, bg, gn = sb("wg2", [RANK, 512]), sb("bg", [P, H]), sb("gn", [NS, DV])
        eps = sb("eps", [P, 1])
        qk, v = sb("qk", [NS, 2 * H, DK]), sb("v", [NS, H, DV])
        r, a = sb("r", [NS, H * DV]), sb("a", [NS, RANK])
        S = sb("S", [P, B, H, DV])
        aT, qkT = sb("aT", [RANK, NS]), sb("qkT", [P, HC, NS])
        x0, x1, x2 = sb("x0", [P, H, NS]), sb("x1", [P, H, NS]), sb("x2", [P, H, NS])
        b, eb, ei, ek = sb("b", [P, H, NS]), sb("eb", [P, H, NS]), sb("ei", [P, H, NS]), sb("ek", [P, H, NS])
        qin, kx, kin = sb("qin", [P, H, NS]), sb("kx", [P, H, NS]), sb("kin", [P, H, NS])
        A, kinT, own_k = sb("A", [NS, H, NS]), sb("kinT", [NS, H, DK]), sb("own_k", [NS, B, H, DK])
        oT, sq, stat = sb("oT", [P, HC, NS]), sb("sq", [NS, H, DV]), sb("stat", [NS, 3, H])
        er, u, og = sb("er", [NS, H * DV]), sb("u", [NS, H * DV]), sb("og", [NS, H * DV])
        ps_a, ps_t = pb("ps_a", [P, 512]), pb("ps_t", [P, HC, NS])
        ps_o, ps_kv = pb("ps_o", [NS, H, DV]), pb("ps_kv", [P, 2, H, DV])
        a_v = ps_a[0:RANK, 0:NS]
        gate_v = ps_a[:, 128:256].rearrange("p (h t) -> p h t", h=H)
        A_v = ps_a[0:NS, 256:384].rearrange("p (h t) -> p h t", h=H)
        kinT_v = ps_kv[0:NS, 0, 0:2, :].rearrange("p x (h e) -> p (x h) e", e=DK)

        consts_in, z_in, S_in, set_up = sem("consts_in"), sem("z_in"), sem("S_in"), sem("set_up")
        a_t, a_out, qk_t, qk_out, gate = sem("a_t"), sem("a_out"), sem("qk_t"), sem("qk_out"), sem("gate")
        x0_done, neg_done, abs_done, exp_done, ln_done = sem("x0"), sem("neg"), sem("abs"), sem("exp"), sem("ln")
        lg_done, b_done, eb_done, ni_done, ei_done = sem("lg"), sem("b"), sem("eb"), sem("ni"), sem("ei")
        dk_done, ek_done, prod_done, scores, A_done = sem("dk"), sem("ek"), sem("prod"), sem("scores"), sem("A")
        kin_t, kinT_out, ownk_done = sem("kin_t"), sem("kinT_out"), sem("ownk")
        oT_done, oT_out, o_t = sem("oT"), sem("oT_out"), sem("o_t")
        kv_done, S_done, stored = sem("kv"), sem("S"), sem("stored")
        sq_done, lnv_done, rms_done, u_done = sem("sq"), sem("lnv"), sem("rms"), sem("u")
        er_done, er1_done, sig_done, swish_done, og_done = sem("er"), sem("er1"), sem("sig"), sem("swish"), sem("og")

        block = ctx.enter_context(nc.Block())
        z = d["z"]
        rows = slice(SEQ, ROWS)

        @block.sync
        def _(sp):
            sp.dma_start(a[:], z[rows, C_A:C_A + RANK]).then_inc(z_in, 16)
            sp.dma_start(qk[:], z[rows, C_Q:C_Q + 2 * H * DK].rearrange("t (h e) -> t h e", e=DK)).then_inc(z_in, 16)
            sp.dma_start(v[:], z[rows, C_V:C_V + H * DV].rearrange("t (h e) -> t h e", e=DV)).then_inc(z_in, 16)
            sp.dma_start(r[:], z[rows, C_R:C_R + H * DV]).then_inc(z_in, 16)
            for q in range(B):
                sp.dma_start(S[:, q], d["state_gla"][q].rearrange("h p e -> p h e")).then_inc(S_in, 16)
            sp.wait_ge(og_done, 1)
            sp.dma_start(d["acts"][rows, 0:H * DV], og[:]).then_inc(stored, 16)
            for q in range(B):
                sp.wait_ge(S_done, q + 1)
                sp.dma_start(d["gla_state_s"][q].rearrange("h p e -> p h e"), S[:, q]).then_inc(stored, 16)
            sp.wait_ge(stored, 16 * (B + 1))

        @block.gpsimd
        def _(pool):
            for dst, src in ((ident[:], d["ident"]), (restart[:], d["restart"]), (own[:], d["own"]),
                             (own_causal[:], d["own_causal"]), (wg2[:], d["gla_wg2"]),
                             (gn[:], d["gla_onorm_g"].partition_broadcast(NS))):
                pool.dma_start(dst, src).then_inc(consts_in, 16)
            with nc.allow_non_contiguous_dma(reason="a bias of 512 numbers, once"):
                pool.dma_start(bg[:], d["gla_bg"].rearrange("(h p) -> p h", p=P)).then_inc(consts_in, 16)
            pool.wait_ge(qk_out, 2)
            pool.wait_ge(eb_done, 1)
            nc.gpsimd.tensor_tensor(qin[:], qkT[:, 0:H, :], eb[:], ALU.mult).then_inc(prod_done, 1)
            pool.wait_ge(ei_done, 1)
            nc.gpsimd.tensor_tensor(kx[:], qkT[:, H:, :], ei[:], ALU.mult).then_inc(prod_done, 1)
            pool.wait_ge(ek_done, 1)
            nc.gpsimd.tensor_tensor(kin[:], qkT[:, H:, :], ek[:], ALU.mult).then_inc(prod_done, 1)
            pool.wait_ge(sig_done, 1)
            nc.gpsimd.tensor_tensor(er[:], r[:], er[:], ALU.mult).then_inc(swish_done, 1)
            pool.wait_ge(swish_done, 1)
            pool.wait_ge(u_done, 1)
            nc.gpsimd.tensor_tensor(og[:], u[:], er[:], ALU.mult).then_inc(og_done, 1)

        @block.scalar
        def _(act):
            nc.scalar.preload_act_table_set(TABLES)
            act.wait_ge(a_t, 1)
            nc.scalar.copy(aT[:], a_v).then_inc(a_out, 1)
            act.wait_ge(qk_t, 1)
            nc.scalar.mul(qkT[:, 0:H, :], ps_t[:, 0:H, :], DK ** -0.5).then_inc(qk_out, 1)
            nc.scalar.copy(qkT[:, H:, :], ps_t[:, H:, :]).then_inc(qk_out, 1)
            act.wait_ge(x0_done, 1)
            nc.scalar.activation(x1[:], x0[:], ACT.Abs).then_inc(abs_done, 1)
            act.wait_ge(abs_done, 1)
            nc.scalar.activation(x1[:], x1[:], ACT.Exp, scale=-1.0).then_inc(exp_done, 1)
            act.wait_ge(exp_done, 1)
            nc.scalar.activation(x1[:], x1[:], ACT.Ln, bias=1.0).then_inc(ln_done, 1)
            act.wait_ge(b_done, 1)
            nc.scalar.activation(eb[:], b[:], ACT.Exp, scale=1.0 / TAU).then_inc(eb_done, 1)
            act.wait_ge(ni_done, 1)
            nc.scalar.activation(ei[:], ei[:], ACT.Exp, scale=1.0 / TAU).then_inc(ei_done, 1)
            act.wait_ge(dk_done, 1)
            nc.scalar.activation(ek[:], ek[:], ACT.Exp, scale=1.0 / TAU).then_inc(ek_done, 1)
            act.wait_ge(z_in, 64)
            nc.scalar.activation(er[:], r[:], ACT.Exp, scale=-1.0).then_inc(er_done, 1)
            act.wait_ge(kin_t, 1)
            nc.scalar.copy(kinT[:], kinT_v).then_inc(kinT_out, 1)
            act.wait_ge(oT_done, 1)
            nc.scalar.copy(oT[:], ps_t[:]).then_inc(oT_out, 1)
            act.wait_ge(o_t, 1)
            act.wait_ge(set_up, 1)
            for h in range(H):
                last = nc.scalar.activation(sq[:, h, :], ps_o[:, h, :], ACT.Square, accum_out=stat[:, 0, h:h + 1])
            last.then_inc(sq_done, 1)
            act.wait_ge(sq_done, 1)
            nc.scalar.activation(stat[:, 1, :], stat[:, 0, :], ACT.Ln, bias=eps[0:NS, :], scale=1.0 / DV).then_inc(lnv_done, 1)
            act.wait_ge(lnv_done, 1)
            nc.scalar.activation(stat[:, 2, :], stat[:, 1, :], ACT.Exp, scale=-0.5).then_inc(rms_done, 1)

        @block.vector
        def _(dve):
            nc.vector.memset(eps[:], EPS).then_inc(set_up, 1)
            dve.wait_ge(consts_in, 7 * 16)
            dve.wait_ge(gate, 1)
            nc.vector.tensor_tensor(x0[:], gate_v, bg[:].unsqueeze(2).to_broadcast([P, H, NS]), ALU.add).then_inc(x0_done, 1)
            dve.wait_ge(x0_done, 1)
            nc.vector.tensor_scalar(x2[:], x0[:], 0.0, None, ALU.min).then_inc(neg_done, 1)
            dve.wait_ge(neg_done, 1)
            dve.wait_ge(ln_done, 1)
            nc.vector.tensor_tensor(x2[:], x2[:], x1[:], ALU.subtract).then_inc(lg_done, 1)
            dve.wait_ge(lg_done, 1)
            for h in range(H):
                last = nc.vector.tensor_tensor_scan(b[:, h, :], restart[:], x2[:, h, :], 0.0, ALU.mult, ALU.add)
            last.then_inc(b_done, 1)
            dve.wait_ge(b_done, 1)
            nc.vector.tensor_scalar(ei[:], b[:], -1.0, CAP, ALU.mult, ALU.min).then_inc(ni_done, 1)
            last_b = b[:].rearrange("p h (q t) -> p (h q) t", t=T)
            nc.vector.tensor_tensor(ek[:].rearrange("p h (q t) -> p (h q) t", t=T),
                                    last_b[:, :, T - 1:T].to_broadcast([P, H * B, T]), last_b, ALU.subtract).then_inc(dk_done, 1)
            dve.wait_ge(er_done, 1)
            nc.vector.tensor_scalar(er[:], er[:], 1.0, None, ALU.add).then_inc(er1_done, 1)
            dve.wait_ge(er1_done, 1)
            nc.vector.reciprocal(er[:], er[:]).then_inc(sig_done, 1)
            dve.wait_ge(scores, 1)
            nc.vector.tensor_tensor(A[:], A_v, own_causal[:].unsqueeze(1).to_broadcast([NS, H, NS]), ALU.mult).then_inc(A_done, 1)
            dve.wait_ge(kinT_out, 1)
            for q in range(B):
                nc.vector.tensor_scalar(own_k[:, q], kinT[:], own[:, q:q + 1], None, ALU.mult).then_inc(ownk_done, 1)
            dve.wait_ge(oT_done, 1)
            for q in range(B):
                dve.wait_ge(kv_done, q + 1)
                for h in range(H):
                    last = nc.vector.scalar_tensor_tensor(out=S[:, q, h, :], in0=S[:, q, h, :],
                                                          scalar=eb[:, h, T * q + T - 1:T * q + T],
                                                          in1=ps_kv[:, q % 2, h, :], op0=ALU.mult, op1=ALU.add)
                last.then_inc(S_done, 1)
            dve.wait_ge(rms_done, 1)
            for h in range(H):
                last = nc.vector.scalar_tensor_tensor(out=u[:, h * DV:(h + 1) * DV], in0=ps_o[:, h, :],
                                                      scalar=stat[:, 2, h:h + 1], in1=gn[:], op0=ALU.mult, op1=ALU.mult)
            last.then_inc(u_done, 1)

        @block.tensor
        def _(pe):
            pe.wait_ge(consts_in, 7 * 16)
            pe.wait_ge(z_in, 64)
            nc.tensor.transpose(a_v, a[:], ident[0:NS, 0:NS]).then_inc(a_t, 1)
            for h in range(2 * H):
                last = nc.tensor.transpose(ps_t[:, h, :], qk[:, h, :], ident[0:NS, 0:NS])
            last.then_inc(qk_t, 1)
            pe.wait_ge(a_out, 1)
            for h in range(H):
                last = nc.tensor.matmul(gate_v[:, h, :], wg2[:, h * DK:(h + 1) * DK], aT[:], start=True, stop=True)
            last.then_inc(gate, 1)
            pe.wait_ge(prod_done, 2)
            pe.wait_ge(x0_done, 1)
            for h in range(H):
                last = nc.tensor.matmul(A_v[:, h, :], kx[:, h, :], qin[:, h, :], start=True, stop=True)
            last.then_inc(scores, 1)
            pe.wait_ge(prod_done, 3)
            for h in range(H):
                last = nc.tensor.transpose(kinT_v[:, h, :], kin[:, h, :], ident[:])
            last.then_inc(kin_t, 1)
            pe.wait_ge(A_done, 1)
            pe.wait_ge(S_in, 16 * B)
            pe.wait_ge(qk_out, 2)
            for h in range(H):
                for c in range(2):
                    hc, e = 2 * h + c, slice(c * P, (c + 1) * P)
                    nc.tensor.matmul(ps_t[:, hc, :], v[:, h, e], A[:, h, :], start=True, stop=False)
                    for q in range(B):
                        last = nc.tensor.matmul(ps_t[:, hc, T * q:T * q + T], S[:, q, h, e], qin[:, h, T * q:T * q + T],
                                                start=False, stop=(q == B - 1))
            last.then_inc(oT_done, 1)
            pe.wait_ge(oT_out, 1)
            o_v = ps_o[:].rearrange("t h (c e) -> t (h c) e", c=2)
            for hc in range(HC):
                last = nc.tensor.transpose(o_v[:, hc, :], oT[:, hc, :], ident[:])
            last.then_inc(o_t, 1)
            pe.wait_ge(kinT_out, 1)
            for q in range(B):
                pe.wait_ge(ownk_done, q + 1)
                if q >= 2:
                    pe.wait_ge(S_done, q - 1)
                for h in range(H):
                    last = nc.tensor.matmul(ps_kv[:, q % 2, h, :], own_k[:, q, h, :], v[:, h, :], start=True, stop=True)
                last.then_inc(kv_done, 1)


def attend(nc, d, group):
    import concourse.bass as bass
    from concourse import mybir
    from contextlib import ExitStack
    fp32, ACT, ALU = mybir.dt.float32, mybir.ActivationFunctionType, mybir.AluOpType
    AX = mybir.AxisListType.X
    memory = group == NG
    R = 1 if memory else WINDOWS[group][1]
    NH = H if memory else 2 * H
    SCALE = DK ** -0.5
    CLASS = min(P, SEQ // R)
    col = C_QM if memory else C_DIL + group * 3 * 512

    def tiles(j):
        return (0, 1) if memory or R == 1 or (R == 4 and j == 1) else (1,)

    def rows(t2, i, j):
        if R == 1:
            return [(0, t2[bass.ds(i * 2 * P + j * P, P), :])]
        v = t2.rearrange("(m r) n -> r m n", r=R)
        if R == 4:
            return [(0, v[bass.ds(i, 1), j * P:(j + 1) * P, :].rearrange("a m n -> (a m) n"))]
        return [(c * CLASS, v[bass.ds(i * 4 + j * 2 + c, 1), :, :].rearrange("a m n -> (a m) n")) for c in range(P // CLASS)]

    PARTS = P // CLASS
    tag = f"at{group}_"
    with ExitStack() as ctx:
        sb = lambda n, s: ctx.enter_context(nc.sbuf_tensor(tag + n, s, fp32))
        pb = lambda n, s: ctx.enter_context(nc.psum_tensor(tag + n, s, fp32))
        sem = stage_semaphores(nc, ctx, tag)
        signals = []

        def signal(n, per=1):
            signals.append(Signal(sem(n), per))
            return signals[-1]

        ident, mask, mask_prev = sb("ident", [P, P]), sb("mask", [P, 2, P]), sb("mask_prev", [P, P])
        eps = sb("eps", [P, 1])
        gain = sb("gain", [P, 2, 2, P])
        x, tab = sb("x", [P, 2, NH, P]), sb("tab", [P, 2, 2, P])
        tg = sb("tg", [P, 2, 2, P])
        sq, stat = sb("sq", [P, 2 * H, P]), sb("stat", [P, 3, 2 * H])
        xr, t1, t2 = sb("xr", [P, NH, P]), sb("t1", [P, NH, P]), sb("t2", [P, NH, P])
        y = sb("y", [P, 2, NH, P])
        qT, kT = sb("qT", [P, H, P]), sb("kT", [P, 2, H, P])
        v = sb("v", [P, 2, H, P])
        e, pT = sb("e", [P, H, 2, P]), sb("pT", [P, H, 2, P])
        mx, nm, den, rden, lnd = (sb(n, [P, H]) for n in ("mx", "nm", "den", "rden", "lnd"))
        o, lse = sb("o", [P, 2, H, P]), sb("lse", [P, 2, H])
        zk = sb("zk", [P, H, P]) if memory else None
        ps_t, ps_s = pb("ps_t", [P, 2 * H, P]), pb("ps_s", [P, H, 2, P])
        ps_p, ps_o = pb("ps_p", [P, H, 2, P]), pb("ps_o", [P, H, P])

        zk_in, key_sq, key_ss, key_ln, key_rs = (sem(n) for n in ("zk_in", "key_sq", "key_ss", "key_ln", "key_rs"))
        key_normed, key_gained, key_t, key_out, key_stored = (sem(n) for n in ("key_normed", "key_gained", "key_t", "key_out", "key_stored"))
        consts_in, set_up, masked = sem("consts_in"), sem("set_up"), sem("masked")
        x_in, v_in = [sem(f"x_in{i}") for i in range(2)], [sem(f"v_in{i}") for i in range(2)]
        X_LOADS = PARTS * (1 if memory else 2)
        k_stored, o_stored = [sem(f"k_stored{i}") for i in range(2)], [sem(f"o_stored{i}") for i in range(2)]
        O_STORES = PARTS * (1 if memory else 2)
        tg_done, sq_done, ss_done, ln_done, rs_done = (signal(n) for n in ("tg", "sq", "ss", "ln", "rs"))
        xr_done, t1_done, t2_done, y_done = (signal(n) for n in ("xr", "t1", "t2", "y"))
        t_done, T_out, scores = signal("t"), signal("T_out", 2), signal("scores")
        sm_done, mx_done, nm_done, e_done = (signal(n) for n in ("sm", "mx", "nm", "e"))
        p_t, pT_act, pT_dve, o_done = (signal(n) for n in ("p_t", "pT_act", "pT_dve", "o"))
        rd_done, lnd_done, lse_done, out_done = (signal(n) for n in ("rd", "lnd", "lse", "out"))
        keeps = lambda j: not memory and (R == 16 or (R == 4 and j == 1))

        block = ctx.enter_context(nc.Block())
        z, zm = d["z"][0:SEQ, :], d["zm"]

        def ahead(eng, front, back):
            front(0, 0, 0)
            with eng.Fori(0, NT // 2 - 1) as i:
                front(i * 2 + 1, i, 1)
                back(i * 2, i, 0)
                front(i * 2 + 2, i + 1, 0)
                back(i * 2 + 1, i, 1)
            i = NT // 2 - 1
            front(2 * i + 1, i, 1)
            back(2 * i, i, 0)
            back(2 * i + 1, i, 1)

        @block.sync
        def _(sp):
            for s in signals:
                s.prime(sp)
            for s in k_stored + o_stored:
                sp.sem_inc(s, 16)
            sp.dma_start(ident[:], d["ident"]).then_inc(consts_in, 16)
            gains = [d["mem_qn_g"], d["mem_kn_g"]] if memory else [d["dil_qn_g"], d["dil_kn_g"]]
            for n, g in enumerate(gains):
                sp.dma_start(gain[:, 0, n, :], g.partition_broadcast(P)).then_inc(consts_in, 16)
                for half in range(2):
                    sp.dma_start(gain[:, 1, n, half * 64:half * 64 + 64],
                                 g[64 - half * 64:128 - half * 64].partition_broadcast(P)).then_inc(consts_in, 16)
            if memory:
                for m in range(2):
                    sp.dma_start(v[:, m], zm[m * P:(m + 1) * P, 512:1024].rearrange("t (h e) -> t h e", h=H)).then_inc(v_in[m], 16)
                    if m:
                        sp.wait_ge(key_normed, 1)
                    sp.dma_start(zk[:], zm[m * P:(m + 1) * P, 0:512].rearrange("t (h e) -> t h e", h=H)).then_inc(zk_in, 16)
                    sp.wait_ge(key_gained, m + 1)
                    sp.dma_start(d["mem_k_p"][m * P:(m + 1) * P, :].rearrange("t (h e) -> t h e", h=H), y[:, m]).then_inc(key_stored, 16)
                    sp.wait_ge(key_stored, 16 * (m + 1))
            else:
                own = d["mask_pair"] if R == 16 else d["mask_own"]
                sp.dma_start(mask[:, 1, :], own).then_inc(consts_in, 16)
                sp.dma_start(mask_prev[:], d["mask_prev"]).then_inc(consts_in, 16)

            def load_x(turn, i, j):
                sp.wait_ge(xr_done.sem, xr_done.at(turn, back=2))
                sp.wait_ge(sq_done.sem, sq_done.at(turn, back=2))
                for p0, src in rows(z[:, col:col + NH * P], i, j):
                    sp.dma_start(x[p0:p0 + CLASS, j, :, :], src.rearrange("t (h e) -> t h e", e=P)).then_inc(x_in[j], 16)
                if not memory:
                    sp.wait_ge(tg_done.sem, tg_done.at(turn, back=2))
                    for p0, src in rows(d["rope"][0:SEQ, :], i, j):
                        sp.dma_start(tab[p0:p0 + CLASS, j], src.rearrange("t (c e) -> t c e", c=2)).then_inc(x_in[j], 16)

            def load_v(turn, i, j):
                for p0, src in rows(z[:, col + 1024:col + 1536], i, j):
                    sp.dma_start(v[p0:p0 + CLASS, j], src.rearrange("t (h e) -> t h e", h=H)).then_inc(v_in[j], 16)

            def back(turn, i, j, more_x=True, more_v=True):
                if not memory:
                    sp.wait_ge(y_done.sem, y_done.at(turn))
                    for p0, dst in rows(d["kr"][group], i, j):
                        sp.dma_start(dst.rearrange("t (h e) -> t h e", h=H), y[p0:p0 + CLASS, j, H:, :]).then_inc(k_stored[j], 16)
                if more_x:
                    load_x(turn + 2, i + 1, j)
                sp.wait_ge(o_done.sem, o_done.at(turn))
                if more_v and not memory:
                    load_v(turn + 1, i + j, 1 - j)
                sp.wait_ge(out_done.sem, out_done.at(turn))
                out = d["acts"][0:SEQ, 1536:2048] if memory else d["od"][group]
                for p0, dst in rows(out, i, j):
                    sp.dma_start(dst.rearrange("t (h e) -> t h e", h=H), o[p0:p0 + CLASS, j]).then_inc(o_stored[j], 16)
                if not memory:
                    sp.wait_ge(lse_done.sem, lse_done.at(turn))
                    for p0, dst in rows(d["lse"][group], i, j):
                        sp.dma_start(dst, lse[p0:p0 + CLASS, j, :]).then_inc(o_stored[j], 16)

            load_x(0, 0, 0)
            load_x(1, 0, 1)
            if not memory:
                load_v(0, 0, 0)
            with sp.Fori(0, NT // 2 - 1) as i:
                for j in range(2):
                    back(i * 2 + j, i, j)
            for j in range(2):
                back(NT - 2 + j, NT // 2 - 1, j, more_x=False, more_v=(j == 0))
            for j in range(2):
                if not memory:
                    sp.wait_ge(k_stored[j], 16 + 16 * PARTS * (NT // 2))
                sp.wait_ge(o_stored[j], 16 + 16 * O_STORES * (NT // 2))

        N_CONSTS = 1 + 6 + (0 if memory else 2)

        @block.gpsimd
        def _(pool):
            pool.wait_ge(consts_in, 16 * N_CONSTS)

            def front(turn, i, j):
                pool.wait_ge(x_in[j], i * (16 * X_LOADS) + 16 * X_LOADS)
                if not memory:
                    pool.wait_ge(t1_done.sem, t1_done.at(turn, back=1))
                    pool.wait_ge(t2_done.sem, t2_done.at(turn, back=1))
                    nc.gpsimd.tensor_tensor(tg[:], tab[:, j].unsqueeze(2).to_broadcast([P, 2, 2, P]), gain[:],
                                            ALU.mult).then_inc(tg_done.sem, 1)
                pool.wait_ge(rs_done.sem, rs_done.at(turn))
                pool.wait_ge(t1_done.sem, t1_done.at(turn, back=1))
                nc.gpsimd.tensor_tensor(xr[:], x[:, j], stat[:, 2, 0:NH].unsqueeze(2).to_broadcast([P, NH, P]),
                                        ALU.mult).then_inc(xr_done.sem, 1)
                if not memory:
                    pool.wait_ge(xr_done.sem, xr_done.at(turn))
                    pool.wait_ge(tg_done.sem, tg_done.at(turn))
                    pool.wait_ge(y_done.sem, y_done.at(turn, back=1))
                    for n in range(2):
                        for half in range(2):
                            dst, src = slice(half * 64, half * 64 + 64), slice(64 - half * 64, 128 - half * 64)
                            last = nc.gpsimd.tensor_tensor(t2[:, n * H:(n + 1) * H, dst], xr[:, n * H:(n + 1) * H, src],
                                                           tg[:, 1, n, dst].unsqueeze(1).to_broadcast([P, H, 64]), ALU.mult)
                    last.then_inc(t2_done.sem, 1)

            ahead(pool, front, lambda turn, i, j: None)

        @block.scalar
        def _(act):
            nc.scalar.preload_act_table_set(TABLES)
            act.wait_ge(set_up, 1)
            if memory:
                for m in range(2):
                    act.wait_ge(zk_in, 16 * (m + 1))
                    act.wait_ge(key_ss, m) if m else None
                    nc.scalar.activation(sq[:, 0:H], zk[:], ACT.Square).then_inc(key_sq, 1)
                    act.wait_ge(key_ss, m + 1)
                    nc.scalar.activation(stat[:, 1, 0:H], stat[:, 0, 0:H], ACT.Ln, bias=eps[:], scale=1.0 / DK).then_inc(key_ln, 1)
                    act.wait_ge(key_ln, m + 1)
                    nc.scalar.activation(stat[:, 2, 0:H], stat[:, 1, 0:H], ACT.Exp, scale=-0.5).then_inc(key_rs, 1)
                    act.wait_ge(key_t, m + 1)
                    nc.scalar.copy(kT[:, m], ps_t[:, 0:H]).then_inc(key_out, 1)

            def front(turn, i, j):
                act.wait_ge(x_in[j], i * (16 * X_LOADS) + 16 * X_LOADS)
                act.wait_ge(ss_done.sem, ss_done.at(turn, back=1))
                nc.scalar.activation(sq[:, 0:NH], x[:, j], ACT.Square).then_inc(sq_done.sem, 1)
                act.wait_ge(ss_done.sem, ss_done.at(turn))
                nc.scalar.activation(stat[:, 1, 0:NH], stat[:, 0, 0:NH], ACT.Ln, bias=eps[:], scale=1.0 / DK).then_inc(ln_done.sem, 1)
                act.wait_ge(ln_done.sem, ln_done.at(turn))
                act.wait_ge(xr_done.sem, xr_done.at(turn, back=1))
                nc.scalar.activation(stat[:, 2, 0:NH], stat[:, 1, 0:NH], ACT.Exp, scale=-0.5).then_inc(rs_done.sem, 1)
                act.wait_ge(t_done.sem, t_done.at(turn))
                act.wait_ge(scores.sem, scores.at(turn, back=1))
                nc.scalar.copy(qT[:], ps_t[:, 0:H]).then_inc(T_out.sem, 1)
                if memory:
                    act.sem_inc(T_out.sem, 1)
                else:
                    nc.scalar.copy(kT[:, j], ps_t[:, H:]).then_inc(T_out.sem, 1)

            def back(turn, i, j):
                act.wait_ge(nm_done.sem, nm_done.at(turn))
                act.wait_ge(rd_done.sem, rd_done.at(turn, back=1))
                w = slice(tiles(j)[0], 2)
                for h in range(H):
                    last = nc.scalar.activation(e[:, h, w], e[:, h, w], ACT.Exp, bias=nm[:, h:h + 1], accum_out=den[:, h:h + 1])
                last.then_inc(e_done.sem, 1)
                if not memory:
                    act.wait_ge(e_done.sem, e_done.at(turn))
                    act.wait_ge(lse_done.sem, lse_done.at(turn, back=1))
                    nc.scalar.activation(lnd[:], den[:], ACT.Ln).then_inc(lnd_done.sem, 1)
                act.wait_ge(p_t.sem, p_t.at(turn))
                act.wait_ge(o_done.sem, o_done.at(turn, back=1))
                nc.scalar.copy(pT[:, 0:2, w], ps_p[:, 0:2, w]).then_inc(pT_act.sem, 1)

            ahead(act, front, back)

        @block.vector
        def _(dve):
            nc.vector.memset(eps[:], EPS).then_inc(set_up, 1)
            if memory:
                dve.wait_ge(consts_in, 16 * N_CONSTS)
                for m in range(2):
                    dve.wait_ge(key_sq, m + 1)
                    nc.vector.tensor_reduce(stat[:, 0, 0:H], sq[:, 0:H], axis=AX, op=ALU.add).then_inc(key_ss, 1)
                    dve.wait_ge(key_rs, m + 1)
                    nc.vector.tensor_tensor(xr[:], zk[:], stat[:, 2, 0:H].unsqueeze(2).to_broadcast([P, H, P]), ALU.mult).then_inc(key_normed, 1)
                    dve.wait_ge(key_normed, m + 1)
                    nc.vector.tensor_tensor(y[:, m], xr[:], gain[:, 0, 1, :].unsqueeze(1).to_broadcast([P, H, P]), ALU.mult).then_inc(key_gained, 1)
                dve.wait_ge(key_stored, 32)
            else:
                nc.vector.memset(mask[:, 0, :], NEG).then_inc(masked, 1)
                nc.vector.memset(kT[:], 0.0).then_inc(masked, 1)
                nc.vector.memset(v[:, 1], 0.0).then_inc(masked, 1)
                dve.wait_ge(masked, 3)
            dve.wait_ge(consts_in, 16 * N_CONSTS)
            if R == 4:
                nc.vector.tensor_copy(mask[:, 0, :], mask_prev[:]).then_inc(masked, 1)
                dve.wait_ge(masked, 4)

            def front(turn, i, j):
                dve.wait_ge(sq_done.sem, sq_done.at(turn))
                dve.wait_ge(ln_done.sem, ln_done.at(turn, back=1))
                nc.vector.tensor_reduce(stat[:, 0, 0:NH], sq[:, 0:NH], axis=AX, op=ALU.add).then_inc(ss_done.sem, 1)
                dve.wait_ge(xr_done.sem, xr_done.at(turn))
                dve.wait_ge(t_done.sem, t_done.at(turn, back=2))
                if memory:
                    nc.vector.tensor_tensor(y[:, j], xr[:], gain[:, 0, 0, :].unsqueeze(1).to_broadcast([P, H, P]), ALU.mult).then_inc(y_done.sem, 1)
                    dve.sem_inc(t1_done.sem, 1)
                    return
                dve.wait_ge(k_stored[j], i * (16 * PARTS) + 16)
                dve.wait_ge(tg_done.sem, tg_done.at(turn))
                dve.wait_ge(y_done.sem, y_done.at(turn, back=1))
                nc.vector.tensor_tensor(t1[:].rearrange("p (n h) e -> p n h e", n=2), xr[:].rearrange("p (n h) e -> p n h e", n=2),
                                        tg[:, 0].unsqueeze(2).to_broadcast([P, 2, H, P]), ALU.mult).then_inc(t1_done.sem, 1)
                dve.wait_ge(t1_done.sem, t1_done.at(turn))
                dve.wait_ge(t2_done.sem, t2_done.at(turn))
                nc.vector.tensor_tensor(y[:, j], t1[:], t2[:], ALU.add).then_inc(y_done.sem, 1)

            def back(turn, i, j):
                first = tiles(j)[0]
                n, w = 2 - first, slice(first, 2)
                dve.wait_ge(scores.sem, scores.at(turn))
                dve.wait_ge(p_t.sem, p_t.at(turn, back=1))
                if memory:
                    nc.vector.tensor_scalar(e[:], ps_s[:], SCALE, None, ALU.mult).then_inc(sm_done.sem, 1)
                else:
                    nc.vector.scalar_tensor_tensor(out=e[:, :, w], in0=ps_s[:, :, w], scalar=SCALE,
                                                   in1=mask[:, w].unsqueeze(1).to_broadcast([P, H, n, P]),
                                                   op0=ALU.mult, op1=ALU.add).then_inc(sm_done.sem, 1)
                dve.wait_ge(sm_done.sem, sm_done.at(turn))
                if R == 1 and not memory:
                    nc.vector.tensor_copy(mask[:, 0, :], mask_prev[:]).then_inc(masked, 1)
                dve.wait_ge(lse_done.sem, lse_done.at(turn, back=1)) if not memory else None
                nc.vector.tensor_reduce(mx[:], e[:, :, w].rearrange("p h n k -> p h (n k)"), axis=AX, op=ALU.max).then_inc(mx_done.sem, 1)
                dve.wait_ge(mx_done.sem, mx_done.at(turn))
                dve.wait_ge(e_done.sem, e_done.at(turn, back=1))
                nc.vector.tensor_scalar(nm[:], mx[:], -1.0, None, ALU.mult).then_inc(nm_done.sem, 1)
                dve.wait_ge(e_done.sem, e_done.at(turn))
                nc.vector.reciprocal(rden[:], den[:]).then_inc(rd_done.sem, 1)
                dve.wait_ge(p_t.sem, p_t.at(turn))
                dve.wait_ge(o_done.sem, o_done.at(turn, back=1))
                nc.vector.tensor_copy(pT[:, 2:4, w], ps_p[:, 2:4, w]).then_inc(pT_dve.sem, 1)
                dve.wait_ge(o_stored[j], i * (16 * O_STORES) + 16)
                if not memory:
                    dve.wait_ge(lnd_done.sem, lnd_done.at(turn))
                    nc.vector.tensor_tensor(lse[:, j], lnd[:], mx[:], ALU.add).then_inc(lse_done.sem, 1)
                dve.wait_ge(rd_done.sem, rd_done.at(turn))
                dve.wait_ge(o_done.sem, o_done.at(turn))
                nc.vector.tensor_tensor(o[:, j], ps_o[:], rden[:].unsqueeze(2).to_broadcast([P, H, P]), ALU.mult).then_inc(out_done.sem, 1)

            ahead(dve, front, back)

        @block.tensor
        def _(pe):
            pe.wait_ge(consts_in, 16)
            if memory:
                for m in range(2):
                    pe.wait_ge(key_gained, m + 1)
                    if m:
                        pe.wait_ge(key_out, m)
                    for h in range(H):
                        last = nc.tensor.transpose(ps_t[:, h, :], y[:, m, h, :], ident[:])
                    last.then_inc(key_t, 1)
                pe.wait_ge(key_out, 2)
            else:
                pe.wait_ge(masked, 3)
                pe.wait_ge(consts_in, 16 * N_CONSTS)

            def front(turn, i, j):
                pe.wait_ge(y_done.sem, y_done.at(turn))
                pe.wait_ge(T_out.sem, T_out.at(turn, back=1))
                for h in range(NH):
                    last = nc.tensor.transpose(ps_t[:, h, :], y[:, j, h, :], ident[:])
                last.then_inc(t_done.sem, 1)
                pe.wait_ge(T_out.sem, T_out.at(turn))
                pe.wait_ge(sm_done.sem, sm_done.at(turn, back=1))
                for h in range(H):
                    for n in tiles(j):
                        key = n if memory else (j if n else 1 - j)
                        last = nc.tensor.matmul(ps_s[:, h, n, :], qT[:, h, :], kT[:, key, h, :], start=True, stop=True)
                last.then_inc(scores.sem, 1)

            def back(turn, i, j):
                pe.wait_ge(e_done.sem, e_done.at(turn))
                pe.wait_ge(pT_act.sem, pT_act.at(turn, back=1))
                pe.wait_ge(pT_dve.sem, pT_dve.at(turn, back=1))
                for h in range(H):
                    for n in tiles(j):
                        last = nc.tensor.transpose(ps_p[:, h, n, :], e[:, h, n, :], ident[:])
                last.then_inc(p_t.sem, 1)
                pe.wait_ge(pT_act.sem, pT_act.at(turn))
                pe.wait_ge(pT_dve.sem, pT_dve.at(turn))
                if memory:
                    pe.wait_ge(v_in[0], 16)
                    pe.wait_ge(v_in[1], 16)
                else:
                    pe.wait_ge(v_in[j], i * (16 * PARTS) + 16 * PARTS)
                pe.wait_ge(out_done.sem, out_done.at(turn, back=1))
                for h in range(H):
                    for n in tiles(j):
                        key = n if memory else (j if n else 1 - j)
                        last = nc.tensor.matmul(ps_o[:, h, :], pT[:, h, n, :], v[:, key, h, :],
                                                start=(n == tiles(j)[0]), stop=(n == 1))
                last.then_inc(o_done.sem, 1)

            ahead(pe, front, back)


def decode(nc, d):
    import concourse.bass as bass
    from concourse import mybir
    from contextlib import ExitStack
    fp32, ACT, ALU = mybir.dt.float32, mybir.ActivationFunctionType, mybir.AluOpType
    AX = mybir.AxisListType.X
    B, T = DEC_B, DEC_T
    NH = NG * 2 * H + H
    SCALE = DK ** -0.5
    UNITS = [(0, 0, T)] + [(1, t, 1) for t in range(T)] + [(2, t, 1) for t in range(T)] + [(3, 0, T), (4, 0, T)]
    NU = len(UNITS)
    KEYS = P + NS

    with ExitStack() as ctx:
        sb = lambda n, s: ctx.enter_context(nc.sbuf_tensor("de_" + n, s, fp32))
        pb = lambda n, s: ctx.enter_context(nc.psum_tensor("de_" + n, s, fp32))
        sem = stage_semaphores(nc, ctx, "de_")
        signals = []

        def signal(n, per=1):
            signals.append(Signal(sem(n), per))
            return signals[-1]

        ident, mask, eps = sb("ident", [P, P]), sb("mask", [P, NG, KEYS]), sb("eps", [P, 1])
        gain, tab, tg = sb("gain", [NS, 2, 2, P]), sb("tab", [NS, 2, P]), sb("tg", [NS, 2, 2, P])
        gain_m = sb("gain_m", [NS, P])
        x, sq, xr = sb("x", [NS, NH, P]), sb("sq", [NS, NH, P]), sb("xr", [NS, NH, P])
        stat = sb("stat", [NS, 3, NH])
        t1, t2, y = sb("t1", [NS, NH - H, P]), sb("t2", [NS, NH - H, P]), sb("y", [NS, NH, P])
        vn = sb("vn", [NS, NG, H, P])
        yT = sb("yT", [P, NH, NS])
        kv = sb("kv", [P, 2, NU, 512])
        kT = sb("kT", [P, 2, H, P])
        sT, s, sm, p = sb("sT", [P, 5, P]), sb("s", [P, NG, KEYS]), sb("sm", [P, 2, P]), sb("p", [P, NG, KEYS])
        nm, den, rden = sb("nm", [P, 4]), sb("den", [P, 4]), sb("rden", [P, 4])
        mx, lse, wt, wsum = sb("mx", [P, 4]), sb("lse", [P, NG]), sb("wt", [P, NG]), sb("wsum", [P, 3])
        pT, pnT = sb("pT", [P, 5, P]), sb("pnT", [NS, NG, P])
        oT, o = sb("oT", [P, 2, P]), sb("o", [NS, 2, H, P])
        zero = sb("zero", [P, P])
        ps_t = pb("ps_t", [P, 2, 512])
        ps_sd, ps_sm = pb("ps_sd", [P, NG, P]), pb("ps_sm", [P, 2, P])
        ps_n, ps_x = pb("ps_n", [P, NG, NS]), pb("ps_x", [P, 5, P])
        ps_od, ps_om = ps_sd[:, 0, :], ps_sm[:, 0, :]
        head = lambda g, n, h: (g * 2 + n) * H + h
        query = lambda g, h: head(g, 0, h) if g < NG else NG * 2 * H + h

        steps = {}

        def st(n):
            if n not in steps:
                steps[n] = sem(n)
            return steps[n]

        kv_in = [sem(f"kv_in{i}") for i in range(2)]
        KV_LOADS = 4
        t_done, T_out, used = signal("t", 2 * NU), (signal("T_act", NU), signal("T_dve", NU)), signal("used", 2)
        v_used = signal("v_used", 2)

        block = ctx.enter_context(nc.Block())
        z = d["z"][SEQ:ROWS, :]

        def load(eng, caches, mem, b, j):
            row = lambda a: a[bass.ds(b, 1), :, :].rearrange("a m n -> (a m) n")
            eng.dma_start(kv[:, j, 0, :], row(caches[0])).then_inc(kv_in[j], 16)
            for g in (1, 2):
                src = row(caches[g]).rearrange("(m r) n -> m r n", m=P)[:, 0:T, :]
                eng.dma_start(kv[:, j, 1 + T * (g - 1):1 + T * g, :], src).then_inc(kv_in[j], 16)
            eng.dma_start(kv[:, j, NU - 2:NU, :], row(mem).rearrange("(k m) n -> m k n", k=2)).then_inc(kv_in[j], 16)

        @block.sync
        def _(sp):
            for s_ in signals:
                s_.prime(sp)
            for g in range(NG):
                c = C_DIL + g * 1536
                sp.dma_start(x[:, g * 8:g * 8 + 8, :], z[:, c:c + 1024].rearrange("t (h e) -> t h e", e=P)).then_inc(st("x_in"), 16)
                sp.dma_start(vn[:, g], z[:, c + 1024:c + 1536].rearrange("t (h e) -> t h e", e=P)).then_inc(st("vn_in"), 16)
            sp.dma_start(x[:, 24:28, :], z[:, C_QM:C_QM + 512].rearrange("t (h e) -> t h e", e=P)).then_inc(st("x_in"), 16)
            with sp.Fori(0, B // 2) as i:
                for j in range(2):
                    sp.wait_ge(used.sem, used.at(i, j + 1, back=1))
                    load(sp, [d[f"cache_dil_k{g}"] for g in range(NG)], d["cache_mem_k"], i * 2 + j, j)
            sp.wait_ge(used.sem, used.at(B // 2 - 1))
            with sp.Fori(0, B // 2) as i:
                for j in range(2):
                    sp.wait_ge(v_used.sem, v_used.at(i, j + 1, back=1))
                    load(sp, [d[f"cache_dil_v{g}"] for g in range(NG)], d["cache_mem_v"], i * 2 + j, j)
            sp.wait_ge(st("o_out"), 1)
            for n in range(2):
                sp.dma_start(d["acts"][SEQ:ROWS, 1024 + 512 * n:1536 + 512 * n].rearrange("t (h e) -> t h e", e=P), o[:, n]).then_inc(st("stored"), 16)
            sp.wait_ge(st("stored"), 32)

        @block.gpsimd
        def _(pool):
            consts = [(ident[:], d["ident"]), (mask[:], d["dec_mask"]),
                      (tab[:], d["rope"][SEQ:ROWS, :].rearrange("t (c e) -> t c e", c=2)),
                      (gain_m[:], d["mem_qn_g"].partition_broadcast(NS))]
            for n, g in enumerate((d["dil_qn_g"], d["dil_kn_g"])):
                consts += [(gain[:, 0, n, :], g.partition_broadcast(NS))]
                consts += [(gain[:, 1, n, f:f + 64], g[64 - f:128 - f].partition_broadcast(NS)) for f in (0, 64)]
            for dst, src in consts:
                pool.dma_start(dst, src).then_inc(st("consts_in"), 16)
            pool.wait_ge(st("consts_in"), 16 * len(consts))
            nc.gpsimd.tensor_tensor(tg[:], tab[:].unsqueeze(2).to_broadcast([NS, 2, 2, P]), gain[:], ALU.mult).then_inc(st("tg"), 1)
            pool.wait_ge(st("xr"), 1)
            pool.wait_ge(st("tg"), 1)
            for g in range(NG):
                for n in range(2):
                    hs = slice(head(g, n, 0), head(g, n, H))
                    for f in (0, 64):
                        last = nc.gpsimd.tensor_tensor(t2[:, hs, f:f + 64], xr[:, hs, 64 - f:128 - f],
                                                       tg[:, 1, n, f:f + 64].unsqueeze(1).to_broadcast([NS, H, 64]), ALU.mult)
            last.then_inc(st("t2"), 1)
            pool.wait_ge(st("y"), 1)
            for g in range(NG):
                pool.dma_start(d["ks"][g].rearrange("t (h e) -> t h e", e=P), y[:, head(g, 1, 0):head(g, 1, H), :]).then_inc(st("ks_stored"), 16)
            pool.wait_ge(st("ks_stored"), 48)

        def copy_transposed(eng, i, j, u, copy):
            n = j * NU + u
            eng.wait_ge(t_done.sem, t_done.at(i, n + 1))
            copy(kT[:, n % 2], ps_t[:, n % 2, :].rearrange("p (h k) -> p h k", h=H)).then_inc(T_out[n % 2].sem, 1)

        @block.scalar
        def _(act):
            nc.scalar.preload_act_table_set(TABLES)
            act.wait_ge(st("x_in"), 64)
            act.wait_ge(st("eps"), 1)
            nc.scalar.activation(sq[:], x[:], ACT.Square).then_inc(st("sq"), 1)
            act.wait_ge(st("ss"), 1)
            nc.scalar.activation(stat[:, 1, :], stat[:, 0, :], ACT.Ln, bias=eps[0:NS, :], scale=1.0 / DK).then_inc(st("ln"), 1)
            act.wait_ge(st("ln"), 1)
            nc.scalar.activation(stat[:, 2, :], stat[:, 1, :], ACT.Exp, scale=-0.5).then_inc(st("rs"), 1)
            act.wait_ge(st("y_t"), 1)
            nc.scalar.copy(yT[:, 0:16, :], ps_t[:, 0, :].rearrange("p (h t) -> p h t", t=NS)).then_inc(st("yT"), 1)
            nc.scalar.copy(yT[:, 16:28, :], ps_t[:, 1, 0:384].rearrange("p (h t) -> p h t", t=NS)).then_inc(st("yT"), 1)
            with act.Fori(0, B // 2) as i:
                for j in range(2):
                    for u in range(NU):
                        if (j * NU + u) % 2 == 0:
                            copy_transposed(act, i, j, u, nc.scalar.copy)
            act.wait_ge(st("nm"), 1)
            for g in range(NG):
                last = nc.scalar.activation(p[:, g, :], s[:, g, :], ACT.Exp, bias=nm[:, g:g + 1], accum_out=den[:, g:g + 1])
            last = nc.scalar.activation(sm[:], sm[:], ACT.Exp, bias=nm[:, 3:4], accum_out=den[:, 3:4])
            last.then_inc(st("e"), 1)
            act.wait_ge(st("e"), 1)
            nc.scalar.activation(lse[:], den[:, 0:NG], ACT.Ln).then_inc(st("lnd"), 1)
            act.wait_ge(st("lse_m"), 1)
            nc.scalar.activation(wt[:], lse[:], ACT.Exp, accum_out=wsum[:, 1:2]).then_inc(st("wt"), 1)
            act.wait_ge(st("p_t"), 1)
            nc.scalar.copy(pT[:], ps_x[:]).then_inc(st("pT"), 1)
            nc.scalar.copy(pnT[:], ps_t[0:NS, 0, 0:NG * P].rearrange("p (g c) -> p g c", g=NG)).then_inc(st("pT"), 1)
            act.wait_ge(st("oT_done"), 1)
            nc.scalar.copy(oT[:, 0, :], ps_od).then_inc(st("oT"), 1)
            nc.scalar.copy(oT[:, 1, :], ps_om).then_inc(st("oT"), 1)
            act.wait_ge(st("o_t"), 1)
            nc.scalar.copy(o[:].rearrange("t n h e -> t (n h) e"), ps_t[0:NS].rearrange("t b (h e) -> t (b h) e", e=P)).then_inc(st("o_out"), 1)

        @block.vector
        def _(dve):
            nc.vector.memset(eps[:], EPS).then_inc(st("eps"), 1)
            nc.vector.memset(zero[:], 0.0).then_inc(st("zero"), 1)
            dve.wait_ge(st("sq"), 1)
            nc.vector.tensor_reduce(stat[:, 0, :], sq[:], axis=AX, op=ALU.add).then_inc(st("ss"), 1)
            dve.wait_ge(st("rs"), 1)
            nc.vector.tensor_tensor(xr[:], x[:], stat[:, 2, :].unsqueeze(2).to_broadcast([NS, NH, P]), ALU.mult).then_inc(st("xr"), 1)
            dve.wait_ge(st("xr"), 1)
            dve.wait_ge(st("tg"), 1)
            for g in range(NG):
                hs = slice(head(g, 0, 0), head(g, 1, H))
                last = nc.vector.tensor_tensor(t1[:, hs, :].rearrange("t (n h) e -> t n h e", n=2),
                                               xr[:, hs, :].rearrange("t (n h) e -> t n h e", n=2),
                                               tg[:, 0].unsqueeze(2).to_broadcast([NS, 2, H, P]), ALU.mult)
            last.then_inc(st("t1"), 1)
            nc.vector.tensor_tensor(y[:, NH - H:, :], xr[:, NH - H:, :], gain_m[:].unsqueeze(1).to_broadcast([NS, H, P]), ALU.mult).then_inc(st("ym"), 1)
            dve.wait_ge(st("t1"), 1)
            dve.wait_ge(st("t2"), 1)
            nc.vector.tensor_tensor(y[:, 0:NH - H, :], t1[:], t2[:], ALU.add).then_inc(st("y"), 1)
            with dve.Fori(0, B // 2) as i:
                for j in range(2):
                    for u in range(NU):
                        if (j * NU + u) % 2 == 1:
                            copy_transposed(dve, i, j, u, nc.vector.tensor_copy)
            dve.wait_ge(used.sem, used.at(B // 2 - 1))
            nc.vector.tensor_scalar(sT[:, 0:NG, :], ps_sd[:], SCALE, None, ALU.mult).then_inc(st("sT"), 1)
            nc.vector.tensor_scalar(sT[:, NG:, :], ps_sm[:], SCALE, None, ALU.mult).then_inc(st("sT"), 1)
            dve.wait_ge(st("s_t"), 1)
            nc.vector.tensor_tensor(s[:, :, 0:P], ps_x[:, 0:NG, :], mask[:, :, 0:P], ALU.add).then_inc(st("s"), 1)
            nc.vector.scalar_tensor_tensor(out=s[:, :, P:], in0=ps_n[:], scalar=SCALE, in1=mask[:, :, P:],
                                           op0=ALU.mult, op1=ALU.add).then_inc(st("s"), 1)
            nc.vector.tensor_copy(sm[:], ps_x[:, NG:, :]).then_inc(st("s"), 1)
            dve.wait_ge(st("s"), 3)
            nc.vector.tensor_reduce(mx[:, 0:NG], s[:], axis=AX, op=ALU.max)
            nc.vector.tensor_reduce(mx[:, 3:4], sm[:].rearrange("p k e -> p (k e)"), axis=AX, op=ALU.max).then_inc(st("mx"), 1)
            dve.wait_ge(st("mx"), 1)
            nc.vector.tensor_scalar(nm[:], mx[:], -1.0, None, ALU.mult).then_inc(st("nm"), 1)
            dve.wait_ge(st("e"), 1)
            nc.vector.reciprocal(rden[:], den[:]).then_inc(st("rd"), 1)
            dve.wait_ge(st("lnd"), 1)
            nc.vector.tensor_tensor(lse[:], lse[:], mx[:, 0:NG], ALU.add).then_inc(st("lse"), 1)
            dve.wait_ge(st("lse"), 1)
            nc.vector.tensor_reduce(wsum[:, 0:1], lse[:], axis=AX, op=ALU.max).then_inc(st("lse_x"), 1)
            dve.wait_ge(st("lse_x"), 1)
            nc.vector.tensor_scalar(lse[:], lse[:], wsum[:, 0:1], None, ALU.subtract).then_inc(st("lse_m"), 1)
            dve.wait_ge(st("wt"), 1)
            nc.vector.reciprocal(wsum[:, 2:3], wsum[:, 1:2]).then_inc(st("wr"), 1)
            dve.wait_ge(st("wr"), 1)
            dve.wait_ge(st("rd"), 1)
            nc.vector.scalar_tensor_tensor(out=rden[:, 0:NG], in0=wt[:], scalar=wsum[:, 2:3], in1=rden[:, 0:NG],
                                           op0=ALU.mult, op1=ALU.mult).then_inc(st("share"), 1)
            dve.wait_ge(st("share"), 1)
            for g in range(NG):
                nc.vector.tensor_scalar(p[:, g, :], p[:, g, :], rden[:, g:g + 1], None, ALU.mult).then_inc(st("p"), 1)
            nc.vector.tensor_scalar(sm[:], sm[:], rden[:, 3:4], None, ALU.mult).then_inc(st("p"), 1)

        @block.tensor
        def _(pe):
            pe.wait_ge(st("consts_in"), 16)
            pe.wait_ge(st("y"), 1)
            pe.wait_ge(st("ym"), 1)
            pe.wait_ge(st("consts_in"), 16 * 10)
            for n in range(NH):
                last = nc.tensor.transpose(ps_t[:, n // 16, NS * (n % 16):NS * (n % 16) + NS], y[:, n, :], ident[0:NS, 0:NS])
            last.then_inc(st("y_t"), 1)
            pe.wait_ge(st("yT"), 2)
            for g in range(NG):
                for h in range(H):
                    last = nc.tensor.matmul(ps_n[h * NS:(h + 1) * NS, g, :], yT[:, head(g, 0, h), :], yT[:, head(g, 1, h), :], start=True, stop=True)
            last.then_inc(st("n_done"), 1)

            def unit_scores(i, j, u):
                n = j * NU + u
                g, t, cols = UNITS[u]
                dst = ps_sd[:, g, :] if g < NG else ps_sm[:, g - NG, :]
                pe.wait_ge(T_out[n % 2].sem, T_out[n % 2].at(i, n // 2 + 1))
                for h in range(H):
                    last = nc.tensor.matmul(dst[:, bass.ds(i * 2 * T + j * T + h * NS + t, cols)], kT[:, n % 2, h, :],
                                            yT[:, query(g, h), bass.ds(i * 2 * T + j * T + t, cols)], start=True, stop=True)
                return last

            with pe.Fori(0, B // 2) as i:
                for j in range(2):
                    pe.wait_ge(kv_in[j], i * (16 * KV_LOADS) + 16 * KV_LOADS)
                    for u in range(NU):
                        n = j * NU + u
                        pe.wait_ge(T_out[n % 2].sem, T_out[n % 2].at(i, n // 2))
                        for h in range(H):
                            last = nc.tensor.transpose(ps_t[:, n % 2, h * P:(h + 1) * P], kv[:, j, u, h * P:(h + 1) * P], ident[:])
                        last.then_inc(t_done.sem, 1)
                        if u:
                            unit_scores(i, j, u - 1)
                    unit_scores(i, j, NU - 1).then_inc(used.sem, 1)
            pe.wait_ge(st("sT"), 2)
            for g in range(5):
                last = nc.tensor.transpose(ps_x[:, g, :], sT[:, g, :], ident[:])
            last.then_inc(st("s_t"), 1)
            pe.wait_ge(st("p"), 4)
            for side in T_out:
                pe.wait_ge(side.sem, side.at(B // 2 - 1))
            for g in range(5):
                nc.tensor.transpose(ps_x[:, g, :], p[:, g, 0:P] if g < NG else sm[:, g - NG, :], ident[:])
            for g in range(NG):
                last = nc.tensor.transpose(ps_t[0:NS, 0, g * P:(g + 1) * P], p[:, g, P:], ident[:])
            last.then_inc(st("p_t"), 1)
            pe.wait_ge(st("pT"), 2)
            pe.wait_ge(st("vn_in"), 48)
            for g in range(NG):
                for h in range(H):
                    last = nc.tensor.matmul(ps_od[:, h * NS:(h + 1) * NS], vn[:, g, h, :], pnT[:, g, h * NS:(h + 1) * NS],
                                            start=(g == 0 and h == 0), stop=False, skip_group_check=True)
            pe.wait_ge(st("zero"), 1)
            nc.tensor.matmul(ps_om[:], zero[:], zero[:], start=True, stop=False, skip_group_check=True)
            with pe.Fori(0, B // 2) as i:
                for j in range(2):
                    pe.wait_ge(kv_in[j], i * (16 * KV_LOADS) + 16 * KV_LOADS * (B // 2 + 1))
                    for u, (g, t, cols) in enumerate(UNITS):
                        dst = ps_od if g < NG else ps_om
                        for h in range(H):
                            c = bass.ds(i * 2 * T + j * T + h * NS + t, cols)
                            last = nc.tensor.matmul(dst[:, c], kv[:, j, u, h * P:(h + 1) * P], pT[:, g, c],
                                                    start=False, stop=False, skip_group_check=True)
                    last.then_inc(v_used.sem, 1)
            nc.tensor.matmul(ps_od[:], zero[:], zero[:], start=False, stop=True, skip_group_check=True)
            nc.tensor.matmul(ps_om[:], zero[:], zero[:], start=False, stop=True, skip_group_check=True).then_inc(st("oT_done"), 1)
            pe.wait_ge(st("oT"), 2)
            for n in range(2):
                for h in range(H):
                    last = nc.tensor.transpose(ps_t[0:NS, n, h * P:(h + 1) * P], oT[:, n, h * NS:(h + 1) * NS], ident[:])
            last.then_inc(st("o_t"), 1)


def merge(nc, d):
    import concourse.bass as bass
    from concourse import mybir
    from contextlib import ExitStack
    fp32, ACT, ALU = mybir.dt.float32, mybir.ActivationFunctionType, mybir.AluOpType
    AX = mybir.AxisListType.X
    KB = 16
    BRANCH = [(0, 8), (8, 12), (12, 16)]
    NGRP = 6

    with ExitStack() as ctx:
        sb = lambda n, s: ctx.enter_context(nc.sbuf_tensor("mg_" + n, s, fp32))
        pb = lambda n, s: ctx.enter_context(nc.psum_tensor("mg_" + n, s, fp32))
        sem = stage_semaphores(nc, ctx, "mg_")
        signals = []

        def signal(n, per=1):
            signals.append(Signal(sem(n), per))
            return signals[-1]

        ident, eps, g2 = sb("ident", [P, P]), sb("eps", [P, 1]), sb("g2", [P, D])
        wb, wo = sb("wb", [P, KB, D]), sb("wo", [P, KD, D])
        a, od3 = sb("a", [P, 2, 2 * D]), sb("od3", [P, NG, 512])
        gate, x = sb("gate", [P, 3 * D]), sb("x", [P, 2, D])
        lse, wts, lm = sb("lse", [P, 2, NG, H]), sb("wts", [P, NG, H]), sb("lm", [P, 2, H])
        aT, m, t, mT = sb("aT", [P, KB, P]), sb("m", [P, 2, D]), sb("t", [P, 512]), sb("mT", [P, KD, P])
        h, n2, stat = sb("h", [P, D]), sb("n2", [P, D]), sb("stat", [P, 3])
        ps_a, ps_b = pb("ps_a", [P, 8, P]), pb("ps_b", [P, 2, 512])
        ps_m, ps_h = pb("ps_m", [P, KD, P]), pb("ps_h", [P, D])

        w_in, set_up, moved = sem("w_in"), sem("set_up"), sem("moved")
        a_in, g_in, x_in = [sem(f"a_in{j}") for j in range(2)], sem("g_in"), [sem(f"x_in{j}") for j in range(2)]
        stored_h, stored_n = sem("stored_h"), sem("stored_n")
        lmax, lsub, lexp, lsum, lrec, wts_done = (signal(n) for n in ("lmax", "lsub", "lexp", "lsum", "lrec", "wts"))
        odw_done, od1_done, od_done = (signal(n) for n in ("odw", "od1", "od"))
        sig_done, a_t, aT_out = signal("sig"), signal("a_t", 2), signal("aT_out", 2)
        prod, gated, added = signal("prod", NGRP), signal("gated", NGRP), signal("added", NGRP)
        m_t, mT_out, h_prod, h_done = signal("m_t"), signal("mT_out", 2), signal("h_prod"), signal("h_done")
        sq_done, ln_done, rs_done, n2_done = (signal(n) for n in ("sq", "ln", "rs", "n2"))

        block = ctx.enter_context(nc.Block())
        N = NT + 1
        z = d["z"]

        def ahead(eng, front, back):
            front(0, 0, 0, P)
            with eng.Fori(0, NT // 2 - 1) as i:
                front(i * 2 + 1, i, 1, P)
                back(i * 2, i, 0, P)
                front(i * 2 + 2, i + 1, 0, P)
                back(i * 2 + 1, i, 1, P)
            i = NT // 2 - 1
            front(NT - 1, i, 1, P)
            back(NT - 2, i, 0, P)
            front(NT, i + 1, 0, NS)
            back(NT - 1, i, 1, P)
            back(NT, i + 1, 0, NS)

        def rows(i, j, n):
            return bass.ds(i * 2 * P + j * P, P) if n == P else slice(SEQ, ROWS)

        @block.sync
        def _(sp):
            for s in signals:
                s.prime(sp)
            sp.sem_inc(stored_h, 16)
            sp.sem_inc(stored_n, 16)

            def front(turn, i, j, n):
                r = rows(i, j, n)
                sp.wait_ge(a_t.sem, a_t.at(turn, back=2))
                if n == P:
                    sp.dma_start(a[:, j, 0:D], d["acts"][r, 0:D]).then_inc(a_in[j], 16)
                    sp.dma_start(a[:, j, 1536:2048], d["acts"][r, 1536:2048]).then_inc(a_in[j], 16)
                    sp.wait_ge(lsub.sem, lsub.at(turn, back=2))
                    sp.dma_start(lse[:, j], d["lse"][:, r, :].rearrange("g t h -> t g h")).then_inc(a_in[j], 16)
                    sp.wait_ge(od_done.sem, od_done.at(turn, back=1))
                    sp.dma_start(od3[:], d["od"][:, r, :].rearrange("g t n -> t g n")).then_inc(a_in[j], 16)
                else:
                    for q in range(4):
                        sp.dma_start(a[0:n, j, q * 512:(q + 1) * 512], d["acts"][r, q * 512:(q + 1) * 512]).then_inc(a_in[j], 16)
                sp.wait_ge(gated.sem, gated.at(turn, back=1))
                sp.dma_start(gate[0:n, :], z[r, C_GATE:C_GATE + 3 * D]).then_inc(g_in, 16)
                sp.wait_ge(h_done.sem, h_done.at(turn, back=2))
                src = d["x"][0][bass.ds(i * 2 * P + j * P, P), :] if n == P else d["x"][1]
                sp.dma_start(x[0:n, j, :], src).then_inc(x_in[j], 16)

            def back(turn, i, j, n):
                sp.wait_ge(h_done.sem, h_done.at(turn))
                sp.dma_start(d["h"][rows(i, j, n), :], h[0:n]).then_inc(stored_h, 16)
                sp.wait_ge(n2_done.sem, n2_done.at(turn))
                sp.dma_start(d["n2"][rows(i, j, n), :], n2[0:n]).then_inc(stored_n, 16)

            ahead(sp, front, back)
            sp.wait_ge(stored_h, 16 * (N + 1))
            sp.wait_ge(stored_n, 16 * (N + 1))

        @block.gpsimd
        def _(pool):
            for dst, src in ((ident[:], d["ident"]), (g2[:], d["ln2_g"].partition_broadcast(P)),
                             (wb[:, 0:8], d["w_br_gla"].rearrange("(k p) n -> p k n", p=P)),
                             (wb[:, 8:12], d["w_br_dil"].rearrange("(k p) n -> p k n", p=P)),
                             (wb[:, 12:16], d["w_br_mem"].rearrange("(k p) n -> p k n", p=P)),
                             (wo[:], d["w_out"].rearrange("(k p) n -> p k n", p=P))):
                pool.dma_start(dst, src).then_inc(w_in, 16)

            moves = [(d["mem_v_p"], d["zm"][:, 512:1024])]
            for name, wd, g in CACHES:
                keep = min(wd, SEQ)
                v_cols = slice(C_DIL + g * 1536 + 1024, C_DIL + g * 1536 + 1536)
                moves += [(d[f"{name}_p"], d["kr"][g][SEQ - keep:SEQ, :] if name[1] == "k" else z[SEQ - keep:SEQ, v_cols]),
                          (d[f"{name}_s"][:, wd - DEC_T:wd, :], (d["ks"][g] if name[1] == "k" else z[SEQ:ROWS, v_cols])
                           .rearrange("(b t) n -> b t n", b=DEC_B))]
            for dst, src in moves:
                pool.dma_start(dst, src).then_inc(moved, 16)

            def front(turn, i, j, n):
                if n == P:
                    pool.wait_ge(wts_done.sem, wts_done.at(turn))
                    pool.wait_ge(a_in[j], i * 64 + 64)
                    od_heads = od3[:].rearrange("p g (h e) -> p (g h) e", e=P)
                    nc.gpsimd.tensor_tensor(od_heads, od_heads,
                                            wts[:].rearrange("p g h -> p (g h)").unsqueeze(2).to_broadcast([P, NG * H, P]),
                                            ALU.mult).then_inc(odw_done.sem, 1)

            ahead(pool, front, lambda *_: None)
            pool.wait_ge(moved, 16 * len(moves))

        @block.scalar
        def _(act):
            act.wait_ge(set_up, 1)

            def front(turn, i, j, n):
                if n == P:
                    act.wait_ge(lsub.sem, lsub.at(turn))
                    act.wait_ge(wts_done.sem, wts_done.at(turn, back=1))
                    nc.scalar.activation(lse[:, j], lse[:, j], ACT.Exp).then_inc(lexp.sem, 1)
                act.wait_ge(g_in, turn * 16 + 16)
                nc.scalar.activation(gate[0:n], gate[0:n], ACT.Sigmoid).then_inc(sig_done.sem, 1)
                for half in range(2):
                    act.wait_ge(a_t.sem, a_t.at(turn, half + 1))
                    if half == 0:
                        act.wait_ge(prod.sem, prod.at(turn, back=1))
                    nc.scalar.copy(aT[:, 8 * half:8 * half + 8, 0:n], ps_a[:, :, 0:n]).then_inc(aT_out.sem, 1)

            def back(turn, i, j, n):
                act.wait_ge(m_t.sem, m_t.at(turn))
                act.wait_ge(h_prod.sem, h_prod.at(turn, back=1))
                for half in range(2):
                    k = slice(4 * half, 4 * half + 4)
                    nc.scalar.copy(mT[:, k, 0:n], ps_m[:, k, 0:n]).then_inc(mT_out.sem, 1)
                act.wait_ge(h_done.sem, h_done.at(turn))
                act.wait_ge(stored_n, turn * 16 + 16)
                nc.scalar.activation(n2[0:n], h[0:n], ACT.Square, accum_out=stat[0:n, 0:1]).then_inc(sq_done.sem, 1)
                act.wait_ge(sq_done.sem, sq_done.at(turn))
                nc.scalar.activation(stat[0:n, 1:2], stat[0:n, 0:1], ACT.Ln, bias=eps[0:n], scale=1.0 / D).then_inc(ln_done.sem, 1)
                act.wait_ge(ln_done.sem, ln_done.at(turn))
                nc.scalar.activation(stat[0:n, 2:3], stat[0:n, 1:2], ACT.Exp, scale=-0.5).then_inc(rs_done.sem, 1)

            ahead(act, front, back)

        @block.vector
        def _(dve):
            nc.vector.memset(eps[:], EPS).then_inc(set_up, 1)
            dve.wait_ge(w_in, 16 * 6)

            def front(turn, i, j, n):
                if n == P:
                    by_head = lse[:, j].rearrange("p g h -> p h g")
                    wide = lambda v: v.unsqueeze(1).to_broadcast([P, NG, H])
                    dve.wait_ge(a_in[j], i * 64 + 64)
                    nc.vector.tensor_reduce(lm[:, 0], by_head, axis=AX, op=ALU.max).then_inc(lmax.sem, 1)
                    dve.wait_ge(lmax.sem, lmax.at(turn))
                    nc.vector.tensor_tensor(lse[:, j], lse[:, j], wide(lm[:, 0]), ALU.subtract).then_inc(lsub.sem, 1)
                    dve.wait_ge(lexp.sem, lexp.at(turn))
                    nc.vector.tensor_reduce(lm[:, 1], by_head, axis=AX, op=ALU.add).then_inc(lsum.sem, 1)
                    dve.wait_ge(lsum.sem, lsum.at(turn))
                    nc.vector.reciprocal(lm[:, 0], lm[:, 1]).then_inc(lrec.sem, 1)
                    dve.wait_ge(lrec.sem, lrec.at(turn))
                    dve.wait_ge(odw_done.sem, odw_done.at(turn, back=1))
                    nc.vector.tensor_tensor(wts[:], lse[:, j], wide(lm[:, 0]), ALU.mult).then_inc(wts_done.sem, 1)
                    dve.wait_ge(odw_done.sem, odw_done.at(turn))
                    nc.vector.tensor_tensor(od3[:, 0], od3[:, 0], od3[:, 1], ALU.add).then_inc(od1_done.sem, 1)
                    dve.wait_ge(od1_done.sem, od1_done.at(turn))
                    nc.vector.tensor_tensor(a[:, j, D:D + 512], od3[:, 0], od3[:, 2], ALU.add).then_inc(od_done.sem, 1)
                else:
                    dve.wait_ge(a_in[j], i * 64 + 64)
                    dve.sem_inc(od_done.sem, 1)
                dve.wait_ge(sig_done.sem, sig_done.at(turn))
                dve.wait_ge(m_t.sem, m_t.at(turn, back=2))
                for q in range(NGRP):
                    b, c = divmod(q, 2)
                    cols = slice(512 * c, 512 * c + 512)
                    dve.wait_ge(prod.sem, prod.at(turn, q + 1))
                    g = gate[0:n, b * D + 512 * c:b * D + 512 * c + 512]
                    if b == 0:
                        nc.vector.tensor_tensor(m[0:n, j, cols], ps_b[0:n, q % 2], g, ALU.mult).then_inc(gated.sem, 1)
                        dve.sem_inc(added.sem, 1)
                    else:
                        dve.wait_ge(added.sem, added.at(turn, q))
                        dve.wait_ge(gated.sem, gated.at(turn, q))
                        nc.vector.tensor_tensor(t[0:n], ps_b[0:n, q % 2], g, ALU.mult).then_inc(gated.sem, 1)
                        dve.wait_ge(gated.sem, gated.at(turn, q + 1))
                        nc.vector.tensor_tensor(m[0:n, j, cols], m[0:n, j, cols], t[0:n], ALU.add).then_inc(added.sem, 1)

            def back(turn, i, j, n):
                dve.wait_ge(h_prod.sem, h_prod.at(turn))
                dve.wait_ge(x_in[j], i * 16 + 16)
                dve.wait_ge(stored_h, turn * 16 + 16)
                dve.wait_ge(n2_done.sem, n2_done.at(turn, back=1))
                nc.vector.tensor_tensor(h[0:n], ps_h[0:n], x[0:n, j], ALU.add).then_inc(h_done.sem, 1)
                dve.wait_ge(rs_done.sem, rs_done.at(turn))
                nc.vector.scalar_tensor_tensor(out=n2[0:n], in0=h[0:n], scalar=stat[0:n, 2:3], in1=g2[0:n],
                                               op0=ALU.mult, op1=ALU.mult).then_inc(n2_done.sem, 1)

            ahead(dve, front, back)

        @block.tensor
        def _(pe):
            pe.wait_ge(w_in, 16 * 6)

            def front(turn, i, j, n):
                pe.wait_ge(od_done.sem, od_done.at(turn))
                pe.wait_ge(a_in[j], i * 64 + 64)
                for half in range(2):
                    pe.wait_ge(aT_out.sem, aT_out.at(turn, half, back=0))
                    for k in range(8):
                        b = 8 * half + k
                        last = nc.tensor.transpose(ps_a[:, k, 0:n], a[0:n, j, b * P:(b + 1) * P], ident[0:n, 0:n])
                    last.then_inc(a_t.sem, 1)
                pe.wait_ge(aT_out.sem, aT_out.at(turn))
                for q in range(NGRP):
                    b, c = divmod(q, 2)
                    k0, k1 = BRANCH[b]
                    if q >= 2:
                        pe.wait_ge(gated.sem, gated.at(turn, q - 1))
                    else:
                        pe.wait_ge(gated.sem, gated.at(turn, NGRP + q - 1, back=1))
                    for k in range(k0, k1):
                        last = nc.tensor.matmul(ps_b[0:n, q % 2], aT[:, k, 0:n], wb[:, k, 512 * c:512 * c + 512],
                                                start=(k == k0), stop=(k == k1 - 1))
                    last.then_inc(prod.sem, 1)

            def back(turn, i, j, n):
                pe.wait_ge(added.sem, added.at(turn))
                pe.wait_ge(gated.sem, gated.at(turn))
                pe.wait_ge(mT_out.sem, mT_out.at(turn, back=1))
                for k in range(KD):
                    last = nc.tensor.transpose(ps_m[:, k, 0:n], m[0:n, j, k * P:(k + 1) * P], ident[0:n, 0:n])
                last.then_inc(m_t.sem, 1)
                pe.wait_ge(mT_out.sem, mT_out.at(turn))
                pe.wait_ge(h_done.sem, h_done.at(turn, back=1))
                for c in range(2):
                    for k in range(KD):
                        last = nc.tensor.matmul(ps_h[0:n, 512 * c:512 * c + 512], mT[:, k, 0:n], wo[:, k, 512 * c:512 * c + 512],
                                                start=(k == 0), stop=(k == KD - 1))
                last.then_inc(h_prod.sem, 1)

            ahead(pe, front, back)


def experts(nc, d):
    import concourse.bass as bass
    from concourse import mybir
    from contextlib import ExitStack
    fp32, u32, ACT, ALU = mybir.dt.float32, mybir.dt.uint32, mybir.ActivationFunctionType, mybir.AluOpType
    AX = mybir.AxisListType.X
    TILES = NT + 1
    K = TOPK
    SLOTS = 8
    USES = K // SLOTS
    LOW = -3e38

    with ExitStack() as ctx:
        sb = lambda n, s, t=fp32: ctx.enter_context(nc.sbuf_tensor("ex_" + n, s, t))
        pb = lambda n, s: ctx.enter_context(nc.psum_tensor("ex_" + n, s, fp32))
        sem = stage_semaphores(nc, ctx, "ex_")
        signals = []

        def signal(n, per=1):
            signals.append(Signal(sem(n), per))
            return signals[-1]

        ident, iota = sb("ident", [P, P]), sb("iota", [P, K])
        wq, keysT = sb("wq", [P, KD, PH * 256]), sb("keysT", [P, 2 * PH, NKEY])
        u_rows, v_rows = sb("u_rows", [P, SLOTS, D]), sb("v_rows", [P, SLOTS, D])
        n2r, n2u, n2T = sb("n2r", [P, D]), sb("n2u", [P, D]), sb("n2T", [P, KD, P])
        hy = sb("hy", [P, D])
        qh, qhT, sc, sc2 = sb("qh", [P, 256]), sb("qhT", [P, 2, P]), sb("sc", [P, 2, NKEY]), sb("sc2", [P, 2, NKEY])
        top, top_at = sb("top", [P, 2, K]), sb("top_at", [P, 2, K], u32)
        cand, cand2 = sb("cand", [P, K, K]), sb("cand2", [P, K * K])
        best, best_at = sb("best", [P, K]), sb("best_at", [P, K], u32)
        pair, pair_f, at_f = sb("pair", [P, 2, K], u32), sb("pair_f", [P, 2, K]), sb("at_f", [P, 2, K])
        hot, picked = sb("hot", [P, 2 * K, K]), sb("picked", [P, 2, K])
        ex, esum, erec = sb("ex", [P, K]), sb("esum", [P, 1]), sb("erec", [P, 1])
        E, gates = sb("E", [P, TILES * NEXP], u32), sb("gates", [P, TILES * NEXP])
        idx = sb("idx", [P, 2, 2, K], u32)
        dots, hp, gel, w = sb("dots", [P, K]), sb("hp", [P, NEXP]), sb("gel", [P, NEXP]), sb("w", [P, NEXP])
        zero = sb("zero", [P, 512])
        w16, diag = sb("w16", [P, K]), sb("diag", [P, K, P])
        ps_y, ps_t = pb("ps_y", [P, D]), pb("ps_t", [P, KD, P])
        ps_q, ps_qt, ps_s = pb("ps_q", [P, 256]), pb("ps_qt", [P, 2, P]), pb("ps_s", [P, 2, P])

        consts_in, keys_in, keys_t, keys_out = sem("consts_in"), sem("keys_in"), sem("keys_t"), sem("keys_out")
        zero_set = sem("zero_set")
        passed = {e.engine: sem(f"passed{n}") for n, e in enumerate((nc.sync, nc.gpsimd, nc.vector, nc.tensor))}
        n2r_in, n2u_in, h_in, y_stored = sem("n2r_in"), sem("n2u_in"), sem("h_in"), sem("y_stored")
        n2_t, n2T_out = signal("n2_t"), signal("n2T_out")
        hp_done, gel_done, w_done, y_sum, y_done = (signal(n) for n in ("hp_done", "gel", "w", "y_sum", "y_done"))
        q_done, q_out, q_t, qT_out, s_done, s_out = (signal(n) for n in ("q", "q_out", "q_t", "qT_out", "s", "s_out"))
        top1, at1, cut, top2, at2 = (signal(n, 2) for n in ("top1", "at1", "cut", "top2", "at2"))
        cand_done, best1, bat1, ccut, best2, bat2 = (signal(n) for n in ("cand", "best1", "bat1", "ccut", "best2", "bat2"))
        atf_done, pair_done, pairf_done, hot_done, sel_done, pick_done = (signal(n) for n in ("atf", "pair", "pairf", "hot", "sel", "pick"))
        E_done, ex_in, ex_out, er_done, gate_done = (signal(n) for n in ("E", "ex_in", "ex_out", "er", "gate"))
        u_in, v_in = [sem(f"u_in{i}") for i in range(SLOTS)], [sem(f"v_in{i}") for i in range(SLOTS)]
        idx_sets = [signal("idx_u"), signal("idx_v")]
        dot_done, dots_kept = signal("dot", K), signal("dots_kept")
        w16_done, diag_done, v_done = signal("w16"), signal("diag", K), signal("v", K)

        block = ctx.enter_context(nc.Block())

        def steps(eng, step):
            step((0, P), None, None)
            step((1, P), (0, P), None)
            with eng.Fori(0, TILES - 3) as i:
                step((i + 2, P), (i + 1, P), (i, P))
            step((TILES - 1, NS), (TILES - 2, P), (TILES - 3, P))
            step(None, (TILES - 1, NS), (TILES - 2, P))
            step(None, None, (TILES - 1, NS))

        def settle(eng):
            eng.sem_inc(passed[eng.engine], 1)

        def rows(tile, n):
            return bass.ds(tile * P, P) if n == P else slice(SEQ, ROWS)

        @block.sync
        def _(sp):
            for s in signals:
                s.prime(sp)
            sp.dma_start(ident[:], d["ident"]).then_inc(consts_in, 16)
            sp.dma_start(iota[:], d["iota"]).then_inc(consts_in, 16)
            for g in range(2 * PH):
                sp.dma_start(u_rows[:, g // 8, (g % 8) * P:(g % 8 + 1) * P], d["peer_keys"][g // 2, g % 2]).then_inc(keys_in, 16)
            sp.dma_start(wq[:], d["peer_wq"].rearrange("(k p) n -> p k n", p=P)).then_inc(consts_in, 16)

            def step(R, U, V):
                if R:
                    tile, n = R
                    sp.wait_ge(n2_t.sem, n2_t.at(tile, back=1))
                    sp.dma_start(n2r[0:n], d["n2"][rows(tile, n), :]).then_inc(n2r_in, 16)
                if U:
                    tile, n = U
                    sp.wait_ge(hp_done.sem, hp_done.at(tile, back=1))
                    sp.dma_start(n2u[0:n], d["n2"][rows(tile, n), :]).then_inc(n2u_in, 16)
                if V:
                    tile, n = V
                    sp.dma_start(hy[0:n], d["h"][rows(tile, n), :]).then_inc(h_in, 16)
                    sp.wait_ge(y_done.sem, y_done.at(tile))
                    y = d["y_prompt"][bass.ds(tile * P, P), :] if n == P else d["y_sample"]
                    sp.dma_start(y, hy[0:n]).then_inc(y_stored, 16)
                    sp.wait_ge(y_stored, tile * 16 + 16)
                settle(sp)

            steps(sp, step)

        @block.gpsimd
        def _(pool):
            def step(R, U, V):
                if not U and not V:
                    return
                with pool.Fori(0, PH // 2) as two:
                    for odd in range(2):
                        head = two * 2 + odd
                        for part, which, done in ((U, 0, dot_done), (V, 1, v_done)):
                            if part:
                                tile, n = part
                                turn = tile * PH + head
                                pool.wait_ge(E_done.sem, E_done.at(turn))
                                if which:
                                    pool.wait_ge(w_done.sem, w_done.at(tile))
                                pool.wait_ge(done.sem, done.at(turn, back=2))
                                nc.gpsimd.tensor_copy(idx[0:n, which, odd], E[0:n, bass.ds(tile * NEXP + head * K, K)]).then_inc(idx_sets[which].sem, 1)
                                pool.wait_ge(idx_sets[which].sem, idx_sets[which].at(turn))
                        for k in range(K):
                            for part, which, slots, done, arrived, table in ((U, 0, u_rows, dot_done, u_in, "peer_u"),
                                                                             (V, 1, v_rows, v_done, v_in, "peer_v")):
                                if part:
                                    tile, n = part
                                    turn = tile * PH + head
                                    pool.wait_ge(done.sem, done.at(turn, k - SLOTS + 1) if k >= SLOTS else done.at(turn, K - SLOTS + k + 1, back=1))
                                    settle(pool)
                                    pool.indirect_dma_start(out=slots[0:n, k % SLOTS, :], out_offset=None, in_=d[table],
                                                            in_offset=bass.IndirectOffsetOnAxis(ap=idx[0:n, which, odd, k:k + 1], axis=0))\
                                        .then_inc(arrived[k % SLOTS], 16)

            pool.wait_ge(keys_t, 2)
            steps(pool, step)

        @block.scalar
        def _(act):
            for g in range(2):
                act.wait_ge(keys_t, g + 1)
                nc.scalar.copy(keysT[:, 8 * g:8 * g + 8], ps_t[:]).then_inc(keys_out, 1)

            def step(R, U, V):
                if R:
                    tile, n = R
                    act.wait_ge(n2_t.sem, n2_t.at(tile))
                    act.wait_ge(q_done.sem, q_done.at(tile * PH, back=1))
                    nc.scalar.copy(n2T[:, :, 0:n], ps_t[:, :, 0:n]).then_inc(n2T_out.sem, 1)
                with act.Fori(0, PH) as head:
                    if R:
                        tile, n = R
                        turn = tile * PH + head
                        act.wait_ge(q_done.sem, q_done.at(turn))
                        nc.scalar.copy(qh[0:n], ps_q[0:n]).then_inc(q_out.sem, 1)
                        act.wait_ge(q_t.sem, q_t.at(turn))
                        nc.scalar.copy(qhT[:, :, 0:n], ps_qt[:, :, 0:n]).then_inc(qT_out.sem, 1)
                        act.wait_ge(s_done.sem, s_done.at(turn))
                        act.wait_ge(cut.sem, cut.at(turn, back=1))
                        act.wait_ge(at1.sem, at1.at(turn, back=1))
                        nc.scalar.copy(sc[0:n], ps_s[0:n]).then_inc(s_out.sem, 1)
                    if V:
                        tile, m = V
                        turn = tile * PH + head
                        act.wait_ge(w_done.sem, w_done.at(tile))
                        act.wait_ge(diag_done.sem, diag_done.at(turn, back=1))
                        nc.scalar.copy(w16[0:m], w[0:m, bass.ds(head * K, K)]).then_inc(w16_done.sem, 1)
                        act.wait_ge(w16_done.sem, w16_done.at(turn))
                        for k in range(K):
                            act.wait_ge(v_done.sem, v_done.at(turn, k + 1, back=1))
                            nc.scalar.mul(diag[0:m, k, 0:m], ident[0:m, 0:m], w16[0:m, k:k + 1]).then_inc(diag_done.sem, 1)
                    if R:
                        tile, n = R
                        turn = tile * PH + head
                        act.wait_ge(ex_in.sem, ex_in.at(turn))
                        nc.scalar.activation(ex[0:n], ex[0:n], ACT.Exp, accum_out=esum[0:n]).then_inc(ex_out.sem, 1)
                if U:
                    tile, n = U
                    act.wait_ge(hp_done.sem, hp_done.at(tile))
                    act.wait_ge(w_done.sem, w_done.at(tile, back=1))
                    nc.scalar.activation(gel[0:n], hp[0:n], ACT.Gelu).then_inc(gel_done.sem, 1)

            steps(act, step)

        @block.vector
        def _(dve):
            nc.vector.memset(zero[:], 0.0).then_inc(zero_set, 1)
            dve.wait_ge(consts_in, 48)

            def route(turn, n, col):
                wait = lambda s, done=None: dve.wait_ge(s.sem, s.at(turn, done))
                wait(s_out)
                settle(dve)
                for c in range(2):
                    nc.vector.max(top[0:n, c, 0:8], sc[0:n, c]).then_inc(top1.sem, 1)
                for c in range(2):
                    wait(top1, c + 1)
                    settle(dve)
                    nc.vector.max_index(top_at[0:n, c, 0:8], top[0:n, c, 0:8], sc[0:n, c]).then_inc(at1.sem, 1)
                    nc.vector.match_replace(sc2[0:n, c], top[0:n, c, 0:8], sc[0:n, c], LOW).then_inc(cut.sem, 1)
                for c in range(2):
                    wait(cut, c + 1)
                    settle(dve)
                    nc.vector.max(top[0:n, c, 8:16], sc2[0:n, c]).then_inc(top2.sem, 1)
                for c in range(2):
                    wait(top2, c + 1)
                    settle(dve)
                    nc.vector.max_index(top_at[0:n, c, 8:16], top[0:n, c, 8:16], sc2[0:n, c]).then_inc(at2.sem, 1)
                nc.vector.tensor_tensor(cand[0:n], top[0:n, 0].unsqueeze(2).to_broadcast([n, K, K]),
                                        top[0:n, 1].unsqueeze(1).to_broadcast([n, K, K]), ALU.add).then_inc(cand_done.sem, 1)
                wait(at2)
                wait(at1)
                nc.vector.tensor_copy(at_f[0:n], top_at[0:n]).then_inc(atf_done.sem, 1)
                wait(cand_done)
                flat = cand[0:n].rearrange("p a b -> p (a b)")
                settle(dve)
                nc.vector.max(best[0:n, 0:8], flat).then_inc(best1.sem, 1)
                wait(best1)
                settle(dve)
                nc.vector.max_index(best_at[0:n, 0:8], best[0:n, 0:8], flat).then_inc(bat1.sem, 1)
                nc.vector.match_replace(cand2[0:n], best[0:n, 0:8], flat, LOW).then_inc(ccut.sem, 1)
                wait(ccut)
                settle(dve)
                nc.vector.max(best[0:n, 8:16], cand2[0:n]).then_inc(best2.sem, 1)
                wait(best2)
                settle(dve)
                nc.vector.max_index(best_at[0:n, 8:16], best[0:n, 8:16], cand2[0:n]).then_inc(bat2.sem, 1)
                dve.wait_ge(gate_done.sem, gate_done.at(turn, back=1))
                nc.vector.tensor_scalar(ex[0:n], best[0:n], best[0:n, 0:1], None, ALU.subtract).then_inc(ex_in.sem, 1)
                wait(bat1)
                wait(bat2)
                nc.vector.tensor_scalar(pair[0:n, 0], best_at[0:n], 4, None, ALU.logical_shift_right)
                nc.vector.tensor_scalar(pair[0:n, 1], best_at[0:n], K - 1, None, ALU.bitwise_and).then_inc(pair_done.sem, 1)
                wait(pair_done)
                nc.vector.tensor_copy(pair_f[0:n], pair[0:n]).then_inc(pairf_done.sem, 1)
                wait(pairf_done)
                nc.vector.tensor_tensor(hot[0:n], pair_f[0:n].rearrange("p c k -> p (c k)").unsqueeze(2).to_broadcast([n, 2 * K, K]),
                                        iota[0:n].unsqueeze(1).to_broadcast([n, 2 * K, K]), ALU.is_equal).then_inc(hot_done.sem, 1)
                wait(hot_done)
                wait(atf_done)
                by_half = hot[0:n].rearrange("p (c k) m -> p c k m", c=2)
                nc.vector.tensor_tensor(by_half, by_half, at_f[0:n].unsqueeze(2).to_broadcast([n, 2, K, K]), ALU.mult).then_inc(sel_done.sem, 1)
                wait(sel_done)
                nc.vector.tensor_reduce(picked[0:n].rearrange("p c k -> p (c k)"), hot[0:n], axis=AX, op=ALU.add).then_inc(pick_done.sem, 1)
                wait(pick_done)
                nc.vector.scalar_tensor_tensor(out=E[0:n, col], in0=picked[0:n, 0], scalar=float(NKEY), in1=picked[0:n, 1],
                                               op0=ALU.mult, op1=ALU.add).then_inc(E_done.sem, 1)
                wait(ex_out)
                nc.vector.reciprocal(erec[0:n], esum[0:n]).then_inc(er_done.sem, 1)
                wait(er_done)
                nc.vector.tensor_scalar(gates[0:n, col], ex[0:n], erec[0:n, 0:1], None, ALU.mult).then_inc(gate_done.sem, 1)

            def step(R, U, V):
                if U:
                    tile, n = U
                    dve.wait_ge(n2u_in, tile * 16 + 16)
                    settle(dve)
                with dve.Fori(0, PH) as head:
                    if U:
                        tile, n = U
                        turn = tile * PH + head
                        dve.wait_ge(dots_kept.sem, dots_kept.at(turn, back=1))
                        for k in range(K):
                            dve.wait_ge(u_in[k % SLOTS], turn * (16 * USES) + 16 * (k // SLOTS + 1))
                            row = u_rows[0:n, k % SLOTS, :]
                            nc.vector.tensor_tensor_reduce(out=row, in0=row, in1=n2u[0:n], scale=1.0, scalar=0.0, op0=ALU.mult,
                                                           op1=ALU.add, accum_out=dots[0:n, k:k + 1]).then_inc(dot_done.sem, 1)
                        dve.wait_ge(dot_done.sem, dot_done.at(turn))
                        dve.wait_ge(gel_done.sem, gel_done.at(tile, back=1))
                        nc.vector.tensor_copy(hp[0:n, bass.ds(head * K, K)], dots[0:n]).then_inc(dots_kept.sem, 1)
                    if R:
                        tile, n = R
                        route(tile * PH + head, n, bass.ds(tile * NEXP + head * K, K))
                if U:
                    tile, n = U
                    dve.wait_ge(dots_kept.sem, dots_kept.at(tile * PH + PH - 1))
                    dve.sem_inc(hp_done.sem, 1)
                if V:
                    tile, n = V
                    dve.wait_ge(y_sum.sem, y_sum.at(tile))
                    dve.wait_ge(h_in, tile * 16 + 16)
                    nc.vector.tensor_tensor(hy[0:n], ps_y[0:n], hy[0:n], ALU.add).then_inc(y_done.sem, 1)
                if U:
                    tile, n = U
                    dve.wait_ge(gel_done.sem, gel_done.at(tile))
                    dve.wait_ge(gate_done.sem, gate_done.at(tile * PH + PH - 1))
                    dve.wait_ge(diag_done.sem, diag_done.at(tile * PH, back=1))
                    nc.vector.tensor_tensor(w[0:n], gel[0:n], gates[0:n, bass.ds(tile * NEXP, NEXP)], ALU.mult).then_inc(w_done.sem, 1)

            steps(dve, step)

        @block.tensor
        def _(pe):
            pe.wait_ge(consts_in, 48)
            pe.wait_ge(zero_set, 1)
            pe.wait_ge(keys_in, 16 * 2 * PH)
            for g in range(2):
                if g:
                    pe.wait_ge(keys_out, 1)
                for k in range(8):
                    last = nc.tensor.transpose(ps_t[:, k, :], u_rows[:, g, k * P:(k + 1) * P], ident[:])
                last.then_inc(keys_t, 1)
            pe.wait_ge(keys_out, 2)

            def step(R, U, V):
                if R:
                    tile, n = R
                    pe.wait_ge(n2r_in, tile * 16 + 16)
                    settle(pe)
                    for k in range(KD):
                        last = nc.tensor.transpose(ps_t[:, k, 0:n], n2r[0:n, k * P:(k + 1) * P], ident[0:n, 0:n])
                    last.then_inc(n2_t.sem, 1)
                    pe.wait_ge(n2T_out.sem, n2T_out.at(tile))
                if V:
                    tile, m = V
                    pe.wait_ge(y_done.sem, y_done.at(tile, back=1))
                    for c in range(2):
                        nc.tensor.matmul(ps_y[:, 512 * c:512 * c + 512], zero[:, 0:P], zero[:], start=True, stop=False, skip_group_check=True)
                with pe.Fori(0, PH) as head:
                    if R:
                        tile, n = R
                        turn = tile * PH + head
                        pe.wait_ge(q_out.sem, q_out.at(turn, back=1))
                        for k in range(KD):
                            last = nc.tensor.matmul(ps_q[0:n], n2T[:, k, 0:n], wq[:, k, bass.ds(head * 256, 256)],
                                                    start=(k == 0), stop=(k == KD - 1))
                        last.then_inc(q_done.sem, 1)
                        pe.wait_ge(q_out.sem, q_out.at(turn))
                        pe.wait_ge(qT_out.sem, qT_out.at(turn, back=1))
                        settle(pe)
                        for c in range(2):
                            last = nc.tensor.transpose(ps_qt[:, c, 0:n], qh[0:n, c * P:(c + 1) * P], ident[0:n, 0:n])
                        last.then_inc(q_t.sem, 1)
                        pe.wait_ge(qT_out.sem, qT_out.at(turn))
                        pe.wait_ge(s_out.sem, s_out.at(turn, back=1))
                        for c in range(2):
                            last = nc.tensor.matmul(ps_s[0:n, c, :], qhT[:, c, 0:n], keysT[:, bass.ds(head * 2 + c, 1), :].rearrange("p a k -> p (a k)"),
                                                    start=True, stop=True)
                        last.then_inc(s_done.sem, 1)
                    if V:
                        tile, m = V
                        turn = tile * PH + head
                        for k in range(K):
                            pe.wait_ge(diag_done.sem, diag_done.at(turn, k + 1))
                            pe.wait_ge(v_in[k % SLOTS], turn * (16 * USES) + 16 * (k // SLOTS + 1))
                            if m < P:
                                settle(pe)
                            for c in range(2):
                                last = nc.tensor.matmul(ps_y[0:m, 512 * c:512 * c + 512], diag[0:m, k, 0:m],
                                                        v_rows[0:m, k % SLOTS, 512 * c:512 * c + 512],
                                                        start=False, stop=False, skip_group_check=True)
                            last.then_inc(v_done.sem, 1)
                if V:
                    for c in range(2):
                        last = nc.tensor.matmul(ps_y[:, 512 * c:512 * c + 512], zero[:, 0:P], zero[:], start=False, stop=True, skip_group_check=True)
                    last.then_inc(y_sum.sem, 1)

            steps(pe, step)


_INS = ["x_prompt", "x_sample", "mem_prompt", "state_gla",
        "cache_dil_k0", "cache_dil_v0", "cache_dil_k1", "cache_dil_v1", "cache_dil_k2", "cache_dil_v2",
        "cache_mem_k", "cache_mem_v", "ln1_g", "w_in", "gla_wg2", "gla_bg", "gla_onorm_g", "dil_qn_g", "dil_kn_g",
        "mem_norm_g", "w_mem_kv", "mem_qn_g", "mem_kn_g", "w_br_gla", "w_br_dil", "w_br_mem", "w_out", "ln2_g",
        "peer_wq", "peer_keys", "peer_u", "peer_v"]
_OUTS = [("y_prompt", (1, SEQ, D)), ("y_sample", (DEC_B, DEC_T, D)), ("gla_state_p", (1, H, DK, DV))]
_OUTS += [(f"{name}_p", (1, min(wd, SEQ), H, DK)) for name, wd, _ in CACHES]
_OUTS += [("mem_k_p", (1, MEM, H, DK)), ("mem_v_p", (1, MEM, H, DK)), ("gla_state_s", (DEC_B, H, DK, DV))]
_OUTS += [(f"{name}_s", (DEC_B, wd, H, DK)) for name, wd, _ in CACHES]
_SCRATCH = [("z", (ROWS, COLS)), ("zm", (MEM, D)), ("acts", (ROWS, 2 * D)), ("od", (NG, SEQ, 512)), ("lse", (NG, SEQ, H)),
            ("kr", (NG, SEQ, 512)), ("ks", (NG, NS, 512)), ("h", (ROWS, D)), ("n2", (ROWS, D))]


def constants():
    import numpy as np
    f = np.float32
    allow = lambda c: np.where(c, f(0), f(NEG)).astype(f)
    q, k = np.arange(P)[:, None], np.arange(P)[None, :]
    s, t = np.arange(NS)[:, None], np.arange(NS)[None, :]
    pos = np.concatenate([np.arange(SEQ), WINDOWS[-1][0] + np.tile(np.arange(DEC_T), DEC_B)]).astype(f)
    half = DK // 2
    inv = f(10000.0) ** (-np.arange(half, dtype=f) / f(half))
    ang = pos[:, None] * inv.astype(f)[None, :]
    cos, sin = np.cos(ang), np.sin(ang)
    row = np.tile(np.arange(NS), H)[:, None]
    dec = np.zeros((P, NG, P + NS), f)
    dec[:, 0, :P] = allow(k >= row % DEC_T)
    dec[:, 0, P:] = allow((t // DEC_T == row // DEC_T) & (t <= row))
    dec[:, 1:, P:] = allow(t == row)[:, None, :]
    return {
        "ident": np.eye(P, dtype=f),
        "causal": (q <= k).astype(f),
        "mask_own": allow(k <= q), "mask_prev": allow(k >= q), "mask_pair": allow((k <= q) & (k // 64 == q // 64)),
        "rope": np.concatenate([cos, cos, -sin, sin], 1).astype(f),
        "restart": np.tile((np.arange(NS) % DEC_T != 0).astype(f), (P, 1)),
        "own": (s // DEC_T == np.arange(DEC_B)[None, :]).astype(f),
        "own_causal": ((s // DEC_T == t // DEC_T) & (s <= t)).astype(f),
        "dec_mask": dec,
        "iota": np.tile(np.arange(TOPK, dtype=f), (P, 1)),
    }


def build(nc, d):
    d["x"] = (d["x_prompt"].rearrange("b s n -> (b s) n"), d["x_sample"].rearrange("b t n -> (b t) n"))
    d["mem_prompt"] = d["mem_prompt"].rearrange("b m n -> (b m) n")
    d["y_prompt"] = d["y_prompt"].rearrange("b s n -> (b s) n")
    d["y_sample"] = d["y_sample"].rearrange("b t n -> (b t) n")
    d["gla_state_p"] = d["gla_state_p"].rearrange("b h p e -> (b h) p e")
    for name in ("mem_k_p", "mem_v_p", *(f"{c}_p" for c, _, _ in CACHES)):
        d[name] = d[name].rearrange("b m h e -> (b m) (h e)")
    for name in ("cache_mem_k", "cache_mem_v", *(f"{c}_s" for c, _, _ in CACHES), *(f"cache_dil_{kv}{g}" for kv in "kv" for g in range(NG))):
        d[name] = d[name].rearrange("b m h e -> b m (h e)")
    project(nc, d)
    gla(nc, d)
    gla_sample(nc, d)
    for group in range(NG + 1):
        attend(nc, d, group)
    decode(nc, d)
    merge(nc, d)
    experts(nc, d)


def kernel(**inputs):
    import numpy as _np
    import concourse.bacc as _bacc
    from concourse import mybir as _mybir
    from concourse.bass_utils import run_bass_kernel_spmd as _run

    nc = _bacc.Bacc("TRN2", target_bir_lowering=False, num_devices=1)
    arrays, d = {}, {}
    given = {name: _np.ascontiguousarray(inputs[name]) for name in _INS} | constants()
    for name, a in given.items():
        arrays[f"in_{name}"] = a
        d[name] = nc.dram_tensor(f"in_{name}", a.shape, _mybir.dt.from_np(a.dtype), kind="ExternalInput").ap()
    for name, shape in _OUTS:
        d[name] = nc.dram_tensor(f"out_{name}", shape, _mybir.dt.float32, kind="ExternalOutput").ap()
    for name, shape in _SCRATCH:
        d[name] = nc.dram_tensor(f"scratch_{name}", shape, _mybir.dt.float32, kind="Internal").ap()
    build(nc, d)
    r = _run(nc, [arrays], core_ids=[0])
    return tuple(r.results[0][f"out_{name}"] for name, _ in _OUTS)
```

```python
P = 128
D = 1024
KD = D // P
SEQ, DEC_B, DEC_T = 1024, 8, 4
NS = DEC_B * DEC_T
NT = SEQ // P
ROWS = SEQ + NS
H = 4
DK, DV, RANK = 128, 256, 16
NG = 3
MEM = 256
C_Q, C_K, C_V, C_R, C_A = 0, 512, 1024, 2048, 3072
C_DIL = C_A + RANK
C_QM = C_DIL + NG * 3 * 512
C_GATE = C_QM + 512
COLS = C_GATE + 3 * D
WINDOWS = ((128, 1), (512, 4), (2048, 16))
CACHES = [(f"d{kv}{g}", WINDOWS[g][0], g) for g in range(NG) for kv in "kv"]
PH, NKEY, TOPK, NEXP = 8, 128, 16, 128
EPS = 1e-6
NEG = -1e30
TABLES = "natural_log_exp_and_others"


def stage_semaphores(nc, ctx, tag):
    taken = []

    def sem(name):
        taken.append(nc.alloc_semaphore(tag + name))
        return taken[-1]

    def give_back():
        nc.clear_and_free_semaphores(taken)
        nc.all_engine_barrier()

    ctx.callback(give_back)
    return sem


def project(nc, d):
    import concourse.bass as bass
    from concourse import mybir
    from contextlib import ExitStack
    fp32, ACT, ALU = mybir.dt.float32, mybir.ActivationFunctionType, mybir.AluOpType

    CW = 470
    CHUNKS = COLS // CW
    tiles = [(P * t, P, False) for t in range(NT)] + [(SEQ, NS, False)] + [(P * t, P, True) for t in range(2)]
    XT = NT + 1
    BANKS = 6
    STEPS = 2 * XT
    USES = STEPS // BANKS
    MW = 512

    with ExitStack() as ctx:
        sb = lambda n, s: ctx.enter_context(nc.sbuf_tensor("pj_" + n, s, fp32))
        sem = stage_semaphores(nc, ctx, "pj_")
        xin = sb("xin", [P, 2, D])
        sq = sb("sq", [P, D])
        xn = sb("xn", [P, 2, D])
        g1, gm = sb("g1", [P, D]), sb("gm", [P, D])
        ident = sb("ident", [P, P])
        stat = sb("stat", [P, 3, len(tiles)])
        eps = sb("eps", [P, 1])
        nT = sb("nT", [P, KD, ROWS])
        nmT = sb("nmT", [P, KD, MEM])
        w = sb("w", [P, 2, KD, CW])
        wm = sb("wm", [P, KD, MW])
        zo = sb("zo", [P, BANKS, MW])
        ps = ctx.enter_context(nc.psum_tensor("pj_ps", [P, 8, 512], fp32))
        consts_in, eps_set = sem("consts_in"), sem("eps_set")
        x_in = [sem(f"x_in{i}") for i in range(2)]
        square_done, log_done, rms_done, xn_done = sem("square"), sem("log"), sem("rms"), sem("xn_done")
        halves_done, halves_out = sem("halves_done"), sem("halves_out")
        w_in = [sem(f"w_in{i}") for i in range(2)]
        w_used = sem("w_used")
        product_done = sem("product_done")
        bank_out = [sem(f"bank_out{i}") for i in range(BANKS)]
        stored = [sem(f"stored{i}") for i in range(BANKS)]
        cache_moved = sem("cache_moved")
        wm_in, wm_used = sem("wm_in"), sem("wm_used")

        block = ctx.enter_context(nc.Block())
        w_dram = d["w_in"].rearrange("(k p) n -> p k n", p=P)
        wm_dram = d["w_mem_kv"].rearrange("(k p) n -> p k n", p=P)

        @block.sync
        def _(sp):
            sp.dma_start(g1[:], d["ln1_g"].partition_broadcast(P)).then_inc(consts_in, 16)
            sp.dma_start(gm[:], d["mem_norm_g"].partition_broadcast(P)).then_inc(consts_in, 16)
            sp.dma_start(ident[:], d["ident"]).then_inc(consts_in, 16)
            for s in stored:
                sp.sem_inc(s, 16)
            for t, (row, n, mem) in enumerate(tiles):
                if t >= 2:
                    sp.wait_ge(xn_done, t - 1)
                src = d["mem_prompt"][row:row + n, :] if mem else d["x"][0][row:row + n, :] if row < SEQ else d["x"][1]
                sp.dma_start(xin[0:n, t % 2, :], src).then_inc(x_in[t % 2], 16)
            with sp.Fori(0, CHUNKS // 2) as i:
                for s in range(STEPS):
                    c, t = divmod(s, XT)
                    row, n, _ = tiles[t]
                    sp.wait_ge(bank_out[s % BANKS], i * USES + s // BANKS + 2)
                    sp.dma_start(d["z"][row:row + n, bass.ds(i * 2 * CW + c * CW, CW)],
                                 zo[0:n, s % BANKS, 0:CW]).then_inc(stored[s % BANKS], 16)
            for s in range(4):
                c, t = divmod(s, 2)
                sp.wait_ge(bank_out[s], USES * CHUNKS // 2 + 2)
                sp.dma_start(d["zm"][P * t:P * t + P, c * MW:(c + 1) * MW], zo[:, s, :]).then_inc(stored[s], 16)
            for s in range(BANKS):
                sp.wait_ge(stored[s], 16 * (1 + USES * CHUNKS // 2 + (s < 4)))

        @block.gpsimd
        def _(pool):
            pool.sem_inc(w_used, 2)
            with pool.Fori(0, CHUNKS // 2) as i:
                for c in range(2):
                    pool.wait_ge(w_used, i * 2 + c + 1)
                    pool.dma_start(w[:, c], w_dram[:, :, bass.ds(i * 2 * CW + c * CW, CW)]).then_inc(w_in[c], 16)
            for c in range(2):
                if c:
                    pool.wait_ge(wm_used, 1)
                pool.dma_start(wm[:], wm_dram[:, :, c * MW:(c + 1) * MW]).then_inc(wm_in, 16)

        def evacuate(act, t):
            row, n, mem = tiles[t]
            dst = nmT[:, :, row:row + n] if mem else nT[:, :, row:row + n]
            for h in range(2):
                act.wait_ge(halves_done, 2 * t + h + 1)
                src = ps[:, 6 + h, :].rearrange("p (k t) -> p k t", k=4)[:, :, 0:n]
                nc.scalar.copy(dst[:, 4 * h:4 * h + 4, :], src).then_inc(halves_out, 1)

        @block.scalar
        def _(act):
            nc.scalar.preload_act_table_set(TABLES)
            act.wait_ge(eps_set, 1)
            for t, (row, n, mem) in enumerate(tiles):
                act.wait_ge(x_in[t % 2], 16 * (t // 2 + 1))
                if t:
                    act.wait_ge(square_done, t)
                nc.scalar.activation(sq[0:n, :], xin[0:n, t % 2, :], ACT.Square,
                                     accum_out=stat[0:n, 0, t:t + 1]).then_inc(square_done, 1)
                act.wait_ge(square_done, t + 1)
                nc.scalar.activation(stat[0:n, 1, t:t + 1], stat[0:n, 0, t:t + 1], ACT.Ln,
                                     bias=eps[0:n, :], scale=1.0 / D).then_inc(log_done, 1)
                act.wait_ge(log_done, t + 1)
                nc.scalar.activation(stat[0:n, 2, t:t + 1], stat[0:n, 1, t:t + 1], ACT.Exp,
                                     scale=-0.5).then_inc(rms_done, 1)
                if t:
                    evacuate(act, t - 1)
            evacuate(act, len(tiles) - 1)
            for b in range(0, BANKS, 2):
                act.sem_inc(bank_out[b], 1)

            def copy_out(i):
                for s in range(0, STEPS, 2):
                    n = tiles[s % XT][1]
                    act.wait_ge(product_done, i * STEPS + s + 1)
                    act.wait_ge(stored[s % BANKS], i * (16 * USES) + 16 * (s // BANKS + 1))
                    nc.scalar.copy(zo[0:n, s % BANKS, 0:CW], ps[0:n, s % BANKS, 0:CW]).then_inc(bank_out[s % BANKS], 1)

            with act.Fori(0, DEC_B) as i:
                for name, wd, _ in CACHES:
                    old = d[f"cache_{name[:-1].replace('d', 'dil_')}{name[-1]}"][bass.ds(i, 1)]
                    kept = old[:, DEC_T:wd, :].rearrange("b w n -> (b w n)").rearrange("(s x) -> s x", s=P)
                    new = d[f"{name}_s"][bass.ds(i, 1)][:, 0:wd - DEC_T, :].rearrange("b w n -> (b w n)").rearrange("(s x) -> s x", s=P)
                    act.dma_start(new, kept).then_inc(cache_moved, 16)
                copy_out(i)
            with act.Fori(DEC_B, CHUNKS // 2) as i:
                copy_out(i)
            for s in (0, 2):
                act.wait_ge(product_done, STEPS * CHUNKS // 2 + s + 1)
                act.wait_ge(stored[s], 16 * (1 + USES * CHUNKS // 2))
                nc.scalar.copy(zo[:, s, :], ps[:, s, :]).then_inc(bank_out[s], 1)
            act.wait_ge(cache_moved, 16 * DEC_B * len(CACHES))

        @block.vector
        def _(dve):
            nc.vector.memset(eps[:], EPS).then_inc(eps_set, 1)
            dve.wait_ge(consts_in, 48)
            for t, (row, n, mem) in enumerate(tiles):
                dve.wait_ge(rms_done, t + 1)
                if t >= 2:
                    dve.wait_ge(halves_done, 2 * (t - 1))
                gain = gm if mem else g1
                nc.vector.scalar_tensor_tensor(out=xn[0:n, t % 2, :], in0=xin[0:n, t % 2, :],
                                               scalar=stat[0:n, 2, t:t + 1], in1=gain[0:n, :],
                                               op0=ALU.mult, op1=ALU.mult).then_inc(xn_done, 1)
            for b in range(1, BANKS, 2):
                dve.sem_inc(bank_out[b], 1)
            with dve.Fori(0, CHUNKS // 2) as i:
                for s in range(1, STEPS, 2):
                    n = tiles[s % XT][1]
                    dve.wait_ge(product_done, i * STEPS + s + 1)
                    dve.wait_ge(stored[s % BANKS], i * (16 * USES) + 16 * (s // BANKS + 1))
                    nc.vector.tensor_copy(zo[0:n, s % BANKS, 0:CW], ps[0:n, s % BANKS, 0:CW]).then_inc(bank_out[s % BANKS], 1)
            for s in (1, 3):
                dve.wait_ge(product_done, STEPS * CHUNKS // 2 + s + 1)
                dve.wait_ge(stored[s], 16 * (1 + USES * CHUNKS // 2))
                nc.vector.tensor_copy(zo[:, s, :], ps[:, s, :]).then_inc(bank_out[s], 1)

        @block.tensor
        def _(pe):
            pe.wait_ge(consts_in, 48)
            for t, (row, n, mem) in enumerate(tiles):
                pe.wait_ge(xn_done, t + 1)
                for h in range(2):
                    if t:
                        pe.wait_ge(halves_out, 2 * t - 1 + h)
                    for k in range(4):
                        last = nc.tensor.transpose(ps[:, 6 + h, P * k:P * k + n],
                                                   xn[0:n, t % 2, P * (4 * h + k):P * (4 * h + k + 1)],
                                                   ident[0:n, 0:n])
                    last.then_inc(halves_done, 1)
            pe.wait_ge(halves_out, 2 * len(tiles))
            with pe.Fori(0, CHUNKS // 2) as i:
                for s in range(STEPS):
                    c, t = divmod(s, XT)
                    row, n, _ = tiles[t]
                    if t == 0:
                        pe.wait_ge(w_in[c], i * 16 + 16)
                    pe.wait_ge(bank_out[s % BANKS], i * USES + s // BANKS + 1)
                    for k in range(KD):
                        last = nc.tensor.matmul(ps[0:n, s % BANKS, 0:CW], nT[:, k, row:row + n], w[:, c, k, :],
                                                start=(k == 0), stop=(k == KD - 1))
                    last.then_inc(product_done, 1)
                    if t == XT - 1:
                        pe.wait_ge(product_done, i * STEPS + s + 1)
                        pe.sem_inc(w_used, 1)
            for s in range(4):
                c, t = divmod(s, 2)
                if t == 0:
                    pe.wait_ge(wm_in, 16 * (c + 1))
                pe.wait_ge(bank_out[s], USES * CHUNKS // 2 + 1)
                for k in range(KD):
                    last = nc.tensor.matmul(ps[:, s, :], nmT[:, k, P * t:P * t + P], wm[:, k, :],
                                            start=(k == 0), stop=(k == KD - 1))
                last.then_inc(product_done, 1)
                if s == 1:
                    pe.wait_ge(product_done, STEPS * CHUNKS // 2 + 2)
                    pe.sem_inc(wm_used, 1)


class Signal:

    def __init__(self, sem, per=1):
        self.sem, self.per = sem, per

    def prime(self, eng):
        eng.sem_inc(self.sem, 2 * self.per)

    def at(self, turn, done=None, back=0):
        return turn * self.per + (2 - back) * self.per + (self.per if done is None else done)


def gla(nc, d):
    import concourse.bass as bass
    from concourse import mybir
    from contextlib import ExitStack
    fp32, ACT, ALU = mybir.dt.float32, mybir.ActivationFunctionType, mybir.AluOpType
    SUB = 16
    NSUB = P // SUB
    TAU = 16.0
    CAP = 70.0 * TAU

    with ExitStack() as ctx:
        sb = lambda n, s: ctx.enter_context(nc.sbuf_tensor("gl_" + n, s, fp32))
        pb = lambda n, s: ctx.enter_context(nc.psum_tensor("gl_" + n, s, fp32))
        sem = stage_semaphores(nc, ctx, "gl_")
        signals = []

        def signal(n, per=1):
            signals.append(Signal(sem(n), per))
            return signals[-1]

        ident, causal = sb("ident", [P, P]), sb("causal", [P, P])
        wg2, bg = sb("wg2", [RANK, 512]), sb("bg", [P, H])
        gn = sb("gn", [P, DV])
        eps, ones = sb("eps", [P, 1]), sb("ones", [P, P])
        qk, v = sb("qk", [P, 2, 2 * H, DK]), sb("v", [P, 2, H, DV])
        r, a = sb("r", [P, 2, H * DV]), sb("a", [P, 2, RANK])
        aT = sb("aT", [RANK, P])
        qkT = sb("qkT", [P, 2 * H, P])
        x0, x1, x2 = sb("x0", [P, H, P]), sb("x1", [P, H, P]), sb("x2", [P, H, P])
        b = sb("b", [P, H, P])
        ref = sb("ref", [P, H, NSUB])
        eb, eq, ek = sb("eb", [P, H, P]), sb("eq", [P, H, P]), sb("ek", [P, H, P])
        qs, qin, kin = sb("qs", [P, H, P]), sb("qin", [P, H, P]), sb("kin", [P, H, P])
        kinT = sb("kinT", [P, H, DK])
        kx = sb("kx", [P, 2, NSUB, P])
        A = sb("A", [P, H, P])
        S = sb("S", [P, H, DV])
        sq, stat = sb("sq", [P, H, DV]), sb("stat", [P, 3, H])
        er, u = sb("er", [P, H * DV]), sb("u", [P, H * DV])
        og = sb("og", [P, 2, H * DV])
        ps_t, ps_g, ps_a = pb("ps_t", [P, 2 * H, P]), pb("ps_g", [P, H, P]), pb("ps_a", [P, H, P])
        ps_k, ps_o = pb("ps_k", [P, H, P]), pb("ps_o", [P, H, DV])
        ps_kv = ps_t[:, :, :].rearrange("p (h two) t -> p h (two t)", two=2)

        consts_in, set_up = sem("consts_in"), sem("set_up")
        z_in = [sem(f"z_in{i}") for i in range(2)]
        stored = [sem(f"stored{i}") for i in range(2)]
        a_t, a_out, gate = signal("a_t"), signal("a_out"), signal("gate")
        qk_t, qk_out = signal("qk_t"), signal("qk_out", 2)
        x0_done, neg_done, abs_done = signal("x0_done"), signal("neg_done"), signal("abs_done")
        exp_done, ln_done, lg_done = signal("exp_done"), signal("ln_done"), signal("lg_done")
        b_done, ref_done, dq_done, dk_done = signal("b_done"), signal("ref_done"), signal("dq_done"), signal("dk_done")
        eb_done, eq_done, ek_done = signal("eb_done"), signal("eq_done"), signal("ek_done")
        qs_done, qin_done, kin_done = signal("qs_done"), signal("qin_done"), signal("kin_done")
        kx_sub, kx_min, kx_exp = signal("kx_sub", H), signal("kx_min", H), signal("kx_exp", H)
        kx_done, scores, A_done = signal("kx_done", H), signal("scores", H), signal("A_done")
        kin_t, kinT_out = signal("kin_t"), signal("kinT_out")
        o_done, kv_done, S_done = signal("o_done"), signal("kv_done"), signal("S_done")
        sq_done, lnv_done, rms_done, u_done = signal("sq_done"), signal("lnv_done"), signal("rms_done"), signal("u_done")
        er_done, er1_done, sig_done = signal("er_done"), signal("er1_done"), signal("sig_done")
        swish_done, og_done = signal("swish_done"), signal("og_done")

        block = ctx.enter_context(nc.Block())
        z = d["z"]

        def turns(eng):
            with eng.Fori(0, NT // 2) as i:
                for j in range(2):
                    yield i * 2 + j, i, j

        @block.sync
        def _(sp):
            for dst, src in ((ident[:], d["ident"]), (causal[:], d["causal"]), (wg2[:], d["gla_wg2"]),
                             (gn[:], d["gla_onorm_g"].partition_broadcast(P))):
                sp.dma_start(dst, src).then_inc(consts_in, 16)
            with nc.allow_non_contiguous_dma(reason="a bias of 512 numbers, once"):
                sp.dma_start(bg[:], d["gla_bg"].rearrange("(h p) -> p h", p=P)).then_inc(consts_in, 16)
            for s in stored:
                sp.sem_inc(s, 16)
            for s in signals:
                s.prime(sp)

            def load(i, j):
                rows, turn = bass.ds(i * 2 * P + j * P, P), i * 2 + j
                sp.wait_ge(kv_done.sem, kv_done.at(turn, back=2))
                sp.wait_ge(swish_done.sem, swish_done.at(turn, back=2))
                sp.wait_ge(er_done.sem, er_done.at(turn, back=2))
                sp.dma_start(a[:, j, :], z[rows, C_A:C_A + RANK]).then_inc(z_in[j], 16)
                sp.dma_start(qk[:, j, :, :], z[rows, C_Q:C_Q + 2 * H * DK].rearrange("t (h e) -> t h e", e=DK)).then_inc(z_in[j], 16)
                sp.dma_start(v[:, j, :, :], z[rows, C_V:C_V + H * DV].rearrange("t (h e) -> t h e", e=DV)).then_inc(z_in[j], 16)
                sp.dma_start(r[:, j, :], z[rows, C_R:C_R + H * DV]).then_inc(z_in[j], 16)

            def store(i, j):
                sp.wait_ge(og_done.sem, og_done.at(i * 2 + j))
                sp.dma_start(d["acts"][bass.ds(i * 2 * P + j * P, P), 0:H * DV], og[:, j, :]).then_inc(stored[j], 16)

            load(0, 0)
            load(0, 1)
            with sp.Fori(0, NT // 2 - 1) as i:
                for j in range(2):
                    store(i, j)
                    load(i + 1, j)
            for j in range(2):
                store(NT // 2 - 1, j)
                sp.wait_ge(stored[j], 16 * (NT // 2 + 1))
            sp.wait_ge(S_done.sem, NT + 2)
            sp.dma_start(d["gla_state_p"].rearrange("h p e -> p h e"), S[:]).then_inc(consts_in, 16)
            sp.wait_ge(consts_in, 6 * 16)

        @block.gpsimd
        def _(pool):
            for turn, i, j in turns(pool):
                pool.wait_ge(qk_out.sem, qk_out.at(turn))
                pool.wait_ge(eq_done.sem, eq_done.at(turn))
                pool.wait_ge(scores.sem, scores.at(turn, back=1))
                nc.gpsimd.tensor_tensor(qs[:], qkT[:, 0:H, :], eq[:], ALU.mult).then_inc(qs_done.sem, 1)
                for h in range(H):
                    pool.wait_ge(kx_exp.sem, kx_exp.at(turn, h + 1))
                    nc.gpsimd.tensor_tensor(kx[:, h % 2], kx[:, h % 2],
                                            qkT[:, H + h, :].unsqueeze(1).to_broadcast([P, NSUB, P]),
                                            ALU.mult).then_inc(kx_done.sem, 1)
                pool.wait_ge(eb_done.sem, eb_done.at(turn))
                pool.wait_ge(o_done.sem, o_done.at(turn, back=1))
                nc.gpsimd.tensor_tensor(qin[:], qkT[:, 0:H, :], eb[:], ALU.mult).then_inc(qin_done.sem, 1)
                pool.wait_ge(ek_done.sem, ek_done.at(turn))
                pool.wait_ge(kin_t.sem, kin_t.at(turn, back=1))
                nc.gpsimd.tensor_tensor(kin[:], qkT[:, H:, :], ek[:], ALU.mult).then_inc(kin_done.sem, 1)
                pool.wait_ge(sig_done.sem, sig_done.at(turn))
                nc.gpsimd.tensor_tensor(er[:], r[:, j, :], er[:], ALU.mult).then_inc(swish_done.sem, 1)
                pool.wait_ge(swish_done.sem, swish_done.at(turn))
                pool.wait_ge(u_done.sem, u_done.at(turn))
                pool.wait_ge(stored[j], i * 16 + 16)
                nc.gpsimd.tensor_tensor(og[:, j, :], u[:], er[:], ALU.mult).then_inc(og_done.sem, 1)

        @block.scalar
        def _(act):
            nc.scalar.preload_act_table_set(TABLES)
            act.wait_ge(set_up, 3)
            for turn, i, j in turns(act):
                act.wait_ge(a_t.sem, a_t.at(turn))
                nc.scalar.copy(aT[:], ps_g[0:RANK, 0, :]).then_inc(a_out.sem, 1)
                act.wait_ge(qk_t.sem, qk_t.at(turn))
                act.wait_ge(kin_done.sem, kin_done.at(turn, back=1))
                nc.scalar.mul(qkT[:, 0:H, :], ps_t[:, 0:H, :], DK ** -0.5).then_inc(qk_out.sem, 1)
                nc.scalar.copy(qkT[:, H:, :], ps_t[:, H:, :]).then_inc(qk_out.sem, 1)
                act.wait_ge(x0_done.sem, x0_done.at(turn))
                nc.scalar.activation(x1[:], x0[:], ACT.Abs).then_inc(abs_done.sem, 1)
                act.wait_ge(abs_done.sem, abs_done.at(turn))
                nc.scalar.activation(x1[:], x1[:], ACT.Exp, scale=-1.0).then_inc(exp_done.sem, 1)
                act.wait_ge(exp_done.sem, exp_done.at(turn))
                nc.scalar.activation(x1[:], x1[:], ACT.Ln, bias=1.0).then_inc(ln_done.sem, 1)
                act.wait_ge(dq_done.sem, dq_done.at(turn))
                nc.scalar.activation(eq[:], eq[:], ACT.Exp, scale=1.0 / TAU).then_inc(eq_done.sem, 1)
                for h in range(H):
                    act.wait_ge(kx_min.sem, kx_min.at(turn, h + 1))
                    nc.scalar.activation(kx[:, h % 2], kx[:, h % 2], ACT.Exp, scale=1.0 / TAU).then_inc(kx_exp.sem, 1)
                act.wait_ge(b_done.sem, b_done.at(turn))
                act.wait_ge(qin_done.sem, qin_done.at(turn, back=1))
                act.wait_ge(S_done.sem, S_done.at(turn, back=1))
                nc.scalar.activation(eb[:], b[:], ACT.Exp, scale=1.0 / TAU).then_inc(eb_done.sem, 1)
                act.wait_ge(dk_done.sem, dk_done.at(turn))
                nc.scalar.activation(ek[:], ek[:], ACT.Exp, scale=1.0 / TAU).then_inc(ek_done.sem, 1)
                act.wait_ge(z_in[j], i * 64 + 64)
                act.wait_ge(og_done.sem, og_done.at(turn, back=1))
                nc.scalar.activation(er[:], r[:, j, :], ACT.Exp, scale=-1.0).then_inc(er_done.sem, 1)
                act.wait_ge(kin_t.sem, kin_t.at(turn))
                nc.scalar.copy(kinT[:], ps_k[:]).then_inc(kinT_out.sem, 1)
                act.wait_ge(o_done.sem, o_done.at(turn))
                for h in range(H):
                    last = nc.scalar.activation(sq[:, h, :], ps_o[:, h, :], ACT.Square, accum_out=stat[:, 0, h:h + 1])
                last.then_inc(sq_done.sem, 1)
                act.wait_ge(sq_done.sem, sq_done.at(turn))
                nc.scalar.activation(stat[:, 1, :], stat[:, 0, :], ACT.Ln, bias=eps[:], scale=1.0 / DV).then_inc(lnv_done.sem, 1)
                act.wait_ge(lnv_done.sem, lnv_done.at(turn))
                act.wait_ge(u_done.sem, u_done.at(turn, back=1))
                nc.scalar.activation(stat[:, 2, :], stat[:, 1, :], ACT.Exp, scale=-0.5).then_inc(rms_done.sem, 1)

        @block.vector
        def _(dve):
            nc.vector.memset(ref[:], 0.0).then_inc(set_up, 1)
            nc.vector.memset(ones[:], 1.0).then_inc(set_up, 1)
            nc.vector.memset(eps[:], EPS).then_inc(set_up, 1)
            nc.vector.memset(S[:], 0.0).then_inc(set_up, 1)
            dve.wait_ge(set_up, 4)
            dve.wait_ge(consts_in, 5 * 16)
            for turn, i, j in turns(dve):
                dve.wait_ge(gate.sem, gate.at(turn))
                nc.vector.tensor_tensor(x0[:], ps_g[:], bg[:].unsqueeze(2).to_broadcast([P, H, P]), ALU.add).then_inc(x0_done.sem, 1)
                dve.wait_ge(x0_done.sem, x0_done.at(turn))
                nc.vector.tensor_scalar(x2[:], x0[:], 0.0, None, ALU.min).then_inc(neg_done.sem, 1)
                dve.wait_ge(neg_done.sem, neg_done.at(turn))
                dve.wait_ge(ln_done.sem, ln_done.at(turn))
                nc.vector.tensor_tensor(x2[:], x2[:], x1[:], ALU.subtract).then_inc(lg_done.sem, 1)
                dve.wait_ge(lg_done.sem, lg_done.at(turn))
                dve.wait_ge(eb_done.sem, eb_done.at(turn, back=1))
                for h in range(H):
                    last = nc.vector.tensor_tensor_scan(b[:, h, :], ones[:], x2[:, h, :], 0.0, ALU.mult, ALU.add)
                last.then_inc(b_done.sem, 1)
                dve.wait_ge(b_done.sem, b_done.at(turn))
                nc.vector.tensor_copy(ref[:, :, 1:NSUB], b[:, :, SUB - 1:P - 1:SUB]).then_inc(ref_done.sem, 1)
                dve.wait_ge(ref_done.sem, ref_done.at(turn))
                dve.wait_ge(qs_done.sem, qs_done.at(turn, back=1))
                nc.vector.tensor_tensor(eq[:].rearrange("p h (s t) -> p (h s) t", t=SUB),
                                        b[:].rearrange("p h (s t) -> p (h s) t", t=SUB),
                                        ref[:].rearrange("p h s -> p (h s)").unsqueeze(2).to_broadcast([P, H * NSUB, SUB]),
                                        ALU.subtract).then_inc(dq_done.sem, 1)
                for h in range(H):
                    if h < 2:
                        dve.wait_ge(scores.sem, scores.at(turn, h + 3, back=1))
                    else:
                        dve.wait_ge(scores.sem, scores.at(turn, h - 1))
                    nc.vector.tensor_tensor(kx[:, h % 2], ref[:, h, :].unsqueeze(2).to_broadcast([P, NSUB, P]),
                                            b[:, h, :].unsqueeze(1).to_broadcast([P, NSUB, P]),
                                            ALU.subtract).then_inc(kx_sub.sem, 1)
                    dve.wait_ge(kx_sub.sem, kx_sub.at(turn, h + 1))
                    nc.vector.tensor_scalar(kx[:, h % 2], kx[:, h % 2], CAP, None, ALU.min).then_inc(kx_min.sem, 1)
                    if h == 0:
                        dve.wait_ge(kin_done.sem, kin_done.at(turn, back=1))
                        nc.vector.tensor_tensor(ek[:], b[:, :, P - 1:P].to_broadcast([P, H, P]), b[:],
                                                ALU.subtract).then_inc(dk_done.sem, 1)
                dve.wait_ge(scores.sem, scores.at(turn))
                dve.wait_ge(o_done.sem, o_done.at(turn, back=1))
                nc.vector.tensor_tensor(A[:], ps_a[:], causal[:].unsqueeze(1).to_broadcast([P, H, P]), ALU.mult).then_inc(A_done.sem, 1)
                dve.wait_ge(er_done.sem, er_done.at(turn))
                nc.vector.tensor_scalar(er[:], er[:], 1.0, None, ALU.add).then_inc(er1_done.sem, 1)
                dve.wait_ge(er1_done.sem, er1_done.at(turn))
                nc.vector.reciprocal(er[:], er[:]).then_inc(sig_done.sem, 1)
                dve.wait_ge(kv_done.sem, kv_done.at(turn))
                dve.wait_ge(o_done.sem, o_done.at(turn))
                for h in range(H):
                    last = nc.vector.scalar_tensor_tensor(out=S[:, h, :], in0=S[:, h, :], scalar=eb[:, h, P - 1:P],
                                                          in1=ps_kv[:, h, :], op0=ALU.mult, op1=ALU.add)
                last.then_inc(S_done.sem, 1)
                dve.wait_ge(rms_done.sem, rms_done.at(turn))
                dve.wait_ge(og_done.sem, og_done.at(turn, back=1))
                for h in range(H):
                    last = nc.vector.scalar_tensor_tensor(out=u[:, h * DV:(h + 1) * DV], in0=ps_o[:, h, :],
                                                          scalar=stat[:, 2, h:h + 1], in1=gn[:], op0=ALU.mult, op1=ALU.mult)
                last.then_inc(u_done.sem, 1)

        @block.tensor
        def _(pe):
            pe.wait_ge(consts_in, 5 * 16)
            pe.wait_ge(set_up, 4)
            for turn, i, j in turns(pe):
                pe.wait_ge(z_in[j], i * 64 + 64)
                pe.wait_ge(x0_done.sem, x0_done.at(turn, back=1))
                nc.tensor.transpose(ps_g[0:RANK, 0, :], a[:, j, :], ident[:]).then_inc(a_t.sem, 1)
                pe.wait_ge(S_done.sem, S_done.at(turn, back=1))
                for h in range(2 * H):
                    last = nc.tensor.transpose(ps_t[:, h, :], qk[:, j, h, :], ident[:])
                last.then_inc(qk_t.sem, 1)
                pe.wait_ge(a_out.sem, a_out.at(turn))
                for h in range(H):
                    last = nc.tensor.matmul(ps_g[:, h, :], wg2[:, h * DK:(h + 1) * DK], aT[:], start=True, stop=True)
                last.then_inc(gate.sem, 1)
                pe.wait_ge(qs_done.sem, qs_done.at(turn))
                pe.wait_ge(A_done.sem, A_done.at(turn, back=1))
                for h in range(H):
                    pe.wait_ge(kx_done.sem, kx_done.at(turn, h + 1))
                    for s in range(NSUB):
                        last = nc.tensor.matmul(ps_a[:, h, s * SUB:(s + 1) * SUB], kx[:, h % 2, s, :],
                                                qs[:, h, s * SUB:(s + 1) * SUB], start=True, stop=True)
                    last.then_inc(scores.sem, 1)
                pe.wait_ge(kin_done.sem, kin_done.at(turn))
                pe.wait_ge(kinT_out.sem, kinT_out.at(turn, back=1))
                for h in range(H):
                    last = nc.tensor.transpose(ps_k[:, h, :], kin[:, h, :], ident[:])
                last.then_inc(kin_t.sem, 1)
                pe.wait_ge(A_done.sem, A_done.at(turn))
                pe.wait_ge(qin_done.sem, qin_done.at(turn))
                pe.wait_ge(u_done.sem, u_done.at(turn, back=1))
                for h in range(H):
                    nc.tensor.matmul(ps_o[:, h, :], A[:, h, :], v[:, j, h, :], start=True, stop=False)
                    last = nc.tensor.matmul(ps_o[:, h, :], qin[:, h, :], S[:, h, :], start=False, stop=True)
                last.then_inc(o_done.sem, 1)
                pe.wait_ge(kinT_out.sem, kinT_out.at(turn))
                pe.wait_ge(qk_out.sem, qk_out.at(turn))
                for h in range(H):
                    last = nc.tensor.matmul(ps_kv[:, h, :], kinT[:, h, :], v[:, j, h, :], start=True, stop=True)
                last.then_inc(kv_done.sem, 1)


def gla_sample(nc, d):
    from concourse import mybir
    from contextlib import ExitStack
    fp32, ACT, ALU = mybir.dt.float32, mybir.ActivationFunctionType, mybir.AluOpType
    TAU = 16.0
    CAP = 70.0 * TAU
    B, T = DEC_B, DEC_T
    HC = 2 * H

    with ExitStack() as ctx:
        sb = lambda n, s: ctx.enter_context(nc.sbuf_tensor("gs_" + n, s, fp32))
        pb = lambda n, s: ctx.enter_context(nc.psum_tensor("gs_" + n, s, fp32))
        sem = stage_semaphores(nc, ctx, "gs_")
        ident, restart = sb("ident", [P, P]), sb("restart", [P, NS])
        own, own_causal = sb("own", [NS, B]), sb("own_causal", [NS, NS])
        wg2, bg, gn = sb("wg2", [RANK, 512]), sb("bg", [P, H]), sb("gn", [NS, DV])
        eps = sb("eps", [P, 1])
        qk, v = sb("qk", [NS, 2 * H, DK]), sb("v", [NS, H, DV])
        r, a = sb("r", [NS, H * DV]), sb("a", [NS, RANK])
        S = sb("S", [P, B, H, DV])
        aT, qkT = sb("aT", [RANK, NS]), sb("qkT", [P, HC, NS])
        x0, x1, x2 = sb("x0", [P, H, NS]), sb("x1", [P, H, NS]), sb("x2", [P, H, NS])
        b, eb, ei, ek = sb("b", [P, H, NS]), sb("eb", [P, H, NS]), sb("ei", [P, H, NS]), sb("ek", [P, H, NS])
        qin, kx, kin = sb("qin", [P, H, NS]), sb("kx", [P, H, NS]), sb("kin", [P, H, NS])
        A, kinT, own_k = sb("A", [NS, H, NS]), sb("kinT", [NS, H, DK]), sb("own_k", [NS, B, H, DK])
        oT, sq, stat = sb("oT", [P, HC, NS]), sb("sq", [NS, H, DV]), sb("stat", [NS, 3, H])
        er, u, og = sb("er", [NS, H * DV]), sb("u", [NS, H * DV]), sb("og", [NS, H * DV])
        ps_a, ps_t = pb("ps_a", [P, 512]), pb("ps_t", [P, HC, NS])
        ps_o, ps_kv = pb("ps_o", [NS, H, DV]), pb("ps_kv", [P, 2, H, DV])
        a_v = ps_a[0:RANK, 0:NS]
        gate_v = ps_a[:, 128:256].rearrange("p (h t) -> p h t", h=H)
        A_v = ps_a[0:NS, 256:384].rearrange("p (h t) -> p h t", h=H)
        kinT_v = ps_kv[0:NS, 0, 0:2, :].rearrange("p x (h e) -> p (x h) e", e=DK)

        consts_in, z_in, S_in, set_up = sem("consts_in"), sem("z_in"), sem("S_in"), sem("set_up")
        a_t, a_out, qk_t, qk_out, gate = sem("a_t"), sem("a_out"), sem("qk_t"), sem("qk_out"), sem("gate")
        x0_done, neg_done, abs_done, exp_done, ln_done = sem("x0"), sem("neg"), sem("abs"), sem("exp"), sem("ln")
        lg_done, b_done, eb_done, ni_done, ei_done = sem("lg"), sem("b"), sem("eb"), sem("ni"), sem("ei")
        dk_done, ek_done, prod_done, scores, A_done = sem("dk"), sem("ek"), sem("prod"), sem("scores"), sem("A")
        kin_t, kinT_out, ownk_done = sem("kin_t"), sem("kinT_out"), sem("ownk")
        oT_done, oT_out, o_t = sem("oT"), sem("oT_out"), sem("o_t")
        kv_done, S_done, stored = sem("kv"), sem("S"), sem("stored")
        sq_done, lnv_done, rms_done, u_done = sem("sq"), sem("lnv"), sem("rms"), sem("u")
        er_done, er1_done, sig_done, swish_done, og_done = sem("er"), sem("er1"), sem("sig"), sem("swish"), sem("og")

        block = ctx.enter_context(nc.Block())
        z = d["z"]
        rows = slice(SEQ, ROWS)

        @block.sync
        def _(sp):
            sp.dma_start(a[:], z[rows, C_A:C_A + RANK]).then_inc(z_in, 16)
            sp.dma_start(qk[:], z[rows, C_Q:C_Q + 2 * H * DK].rearrange("t (h e) -> t h e", e=DK)).then_inc(z_in, 16)
            sp.dma_start(v[:], z[rows, C_V:C_V + H * DV].rearrange("t (h e) -> t h e", e=DV)).then_inc(z_in, 16)
            sp.dma_start(r[:], z[rows, C_R:C_R + H * DV]).then_inc(z_in, 16)
            for q in range(B):
                sp.dma_start(S[:, q], d["state_gla"][q].rearrange("h p e -> p h e")).then_inc(S_in, 16)
            sp.wait_ge(og_done, 1)
            sp.dma_start(d["acts"][rows, 0:H * DV], og[:]).then_inc(stored, 16)
            for q in range(B):
                sp.wait_ge(S_done, q + 1)
                sp.dma_start(d["gla_state_s"][q].rearrange("h p e -> p h e"), S[:, q]).then_inc(stored, 16)
            sp.wait_ge(stored, 16 * (B + 1))

        @block.gpsimd
        def _(pool):
            for dst, src in ((ident[:], d["ident"]), (restart[:], d["restart"]), (own[:], d["own"]),
                             (own_causal[:], d["own_causal"]), (wg2[:], d["gla_wg2"]),
                             (gn[:], d["gla_onorm_g"].partition_broadcast(NS))):
                pool.dma_start(dst, src).then_inc(consts_in, 16)
            with nc.allow_non_contiguous_dma(reason="a bias of 512 numbers, once"):
                pool.dma_start(bg[:], d["gla_bg"].rearrange("(h p) -> p h", p=P)).then_inc(consts_in, 16)
            pool.wait_ge(qk_out, 2)
            pool.wait_ge(eb_done, 1)
            nc.gpsimd.tensor_tensor(qin[:], qkT[:, 0:H, :], eb[:], ALU.mult).then_inc(prod_done, 1)
            pool.wait_ge(ei_done, 1)
            nc.gpsimd.tensor_tensor(kx[:], qkT[:, H:, :], ei[:], ALU.mult).then_inc(prod_done, 1)
            pool.wait_ge(ek_done, 1)
            nc.gpsimd.tensor_tensor(kin[:], qkT[:, H:, :], ek[:], ALU.mult).then_inc(prod_done, 1)
            pool.wait_ge(sig_done, 1)
            nc.gpsimd.tensor_tensor(er[:], r[:], er[:], ALU.mult).then_inc(swish_done, 1)
            pool.wait_ge(swish_done, 1)
            pool.wait_ge(u_done, 1)
            nc.gpsimd.tensor_tensor(og[:], u[:], er[:], ALU.mult).then_inc(og_done, 1)

        @block.scalar
        def _(act):
            nc.scalar.preload_act_table_set(TABLES)
            act.wait_ge(a_t, 1)
            nc.scalar.copy(aT[:], a_v).then_inc(a_out, 1)
            act.wait_ge(qk_t, 1)
            nc.scalar.mul(qkT[:, 0:H, :], ps_t[:, 0:H, :], DK ** -0.5).then_inc(qk_out, 1)
            nc.scalar.copy(qkT[:, H:, :], ps_t[:, H:, :]).then_inc(qk_out, 1)
            act.wait_ge(x0_done, 1)
            nc.scalar.activation(x1[:], x0[:], ACT.Abs).then_inc(abs_done, 1)
            act.wait_ge(abs_done, 1)
            nc.scalar.activation(x1[:], x1[:], ACT.Exp, scale=-1.0).then_inc(exp_done, 1)
            act.wait_ge(exp_done, 1)
            nc.scalar.activation(x1[:], x1[:], ACT.Ln, bias=1.0).then_inc(ln_done, 1)
            act.wait_ge(b_done, 1)
            nc.scalar.activation(eb[:], b[:], ACT.Exp, scale=1.0 / TAU).then_inc(eb_done, 1)
            act.wait_ge(ni_done, 1)
            nc.scalar.activation(ei[:], ei[:], ACT.Exp, scale=1.0 / TAU).then_inc(ei_done, 1)
            act.wait_ge(dk_done, 1)
            nc.scalar.activation(ek[:], ek[:], ACT.Exp, scale=1.0 / TAU).then_inc(ek_done, 1)
            act.wait_ge(z_in, 64)
            nc.scalar.activation(er[:], r[:], ACT.Exp, scale=-1.0).then_inc(er_done, 1)
            act.wait_ge(kin_t, 1)
            nc.scalar.copy(kinT[:], kinT_v).then_inc(kinT_out, 1)
            act.wait_ge(oT_done, 1)
            nc.scalar.copy(oT[:], ps_t[:]).then_inc(oT_out, 1)
            act.wait_ge(o_t, 1)
            act.wait_ge(set_up, 1)
            for h in range(H):
                last = nc.scalar.activation(sq[:, h, :], ps_o[:, h, :], ACT.Square, accum_out=stat[:, 0, h:h + 1])
            last.then_inc(sq_done, 1)
            act.wait_ge(sq_done, 1)
            nc.scalar.activation(stat[:, 1, :], stat[:, 0, :], ACT.Ln, bias=eps[0:NS, :], scale=1.0 / DV).then_inc(lnv_done, 1)
            act.wait_ge(lnv_done, 1)
            nc.scalar.activation(stat[:, 2, :], stat[:, 1, :], ACT.Exp, scale=-0.5).then_inc(rms_done, 1)

        @block.vector
        def _(dve):
            nc.vector.memset(eps[:], EPS).then_inc(set_up, 1)
            dve.wait_ge(consts_in, 7 * 16)
            dve.wait_ge(gate, 1)
            nc.vector.tensor_tensor(x0[:], gate_v, bg[:].unsqueeze(2).to_broadcast([P, H, NS]), ALU.add).then_inc(x0_done, 1)
            dve.wait_ge(x0_done, 1)
            nc.vector.tensor_scalar(x2[:], x0[:], 0.0, None, ALU.min).then_inc(neg_done, 1)
            dve.wait_ge(neg_done, 1)
            dve.wait_ge(ln_done, 1)
            nc.vector.tensor_tensor(x2[:], x2[:], x1[:], ALU.subtract).then_inc(lg_done, 1)
            dve.wait_ge(lg_done, 1)
            for h in range(H):
                last = nc.vector.tensor_tensor_scan(b[:, h, :], restart[:], x2[:, h, :], 0.0, ALU.mult, ALU.add)
            last.then_inc(b_done, 1)
            dve.wait_ge(b_done, 1)
            nc.vector.tensor_scalar(ei[:], b[:], -1.0, CAP, ALU.mult, ALU.min).then_inc(ni_done, 1)
            last_b = b[:].rearrange("p h (q t) -> p (h q) t", t=T)
            nc.vector.tensor_tensor(ek[:].rearrange("p h (q t) -> p (h q) t", t=T),
                                    last_b[:, :, T - 1:T].to_broadcast([P, H * B, T]), last_b, ALU.subtract).then_inc(dk_done, 1)
            dve.wait_ge(er_done, 1)
            nc.vector.tensor_scalar(er[:], er[:], 1.0, None, ALU.add).then_inc(er1_done, 1)
            dve.wait_ge(er1_done, 1)
            nc.vector.reciprocal(er[:], er[:]).then_inc(sig_done, 1)
            dve.wait_ge(scores, 1)
            nc.vector.tensor_tensor(A[:], A_v, own_causal[:].unsqueeze(1).to_broadcast([NS, H, NS]), ALU.mult).then_inc(A_done, 1)
            dve.wait_ge(kinT_out, 1)
            for q in range(B):
                nc.vector.tensor_scalar(own_k[:, q], kinT[:], own[:, q:q + 1], None, ALU.mult).then_inc(ownk_done, 1)
            dve.wait_ge(oT_done, 1)
            for q in range(B):
                dve.wait_ge(kv_done, q + 1)
                for h in range(H):
                    last = nc.vector.scalar_tensor_tensor(out=S[:, q, h, :], in0=S[:, q, h, :],
                                                          scalar=eb[:, h, T * q + T - 1:T * q + T],
                                                          in1=ps_kv[:, q % 2, h, :], op0=ALU.mult, op1=ALU.add)
                last.then_inc(S_done, 1)
            dve.wait_ge(rms_done, 1)
            for h in range(H):
                last = nc.vector.scalar_tensor_tensor(out=u[:, h * DV:(h + 1) * DV], in0=ps_o[:, h, :],
                                                      scalar=stat[:, 2, h:h + 1], in1=gn[:], op0=ALU.mult, op1=ALU.mult)
            last.then_inc(u_done, 1)

        @block.tensor
        def _(pe):
            pe.wait_ge(consts_in, 7 * 16)
            pe.wait_ge(z_in, 64)
            nc.tensor.transpose(a_v, a[:], ident[0:NS, 0:NS]).then_inc(a_t, 1)
            for h in range(2 * H):
                last = nc.tensor.transpose(ps_t[:, h, :], qk[:, h, :], ident[0:NS, 0:NS])
            last.then_inc(qk_t, 1)
            pe.wait_ge(a_out, 1)
            for h in range(H):
                last = nc.tensor.matmul(gate_v[:, h, :], wg2[:, h * DK:(h + 1) * DK], aT[:], start=True, stop=True)
            last.then_inc(gate, 1)
            pe.wait_ge(prod_done, 2)
            pe.wait_ge(x0_done, 1)
            for h in range(H):
                last = nc.tensor.matmul(A_v[:, h, :], kx[:, h, :], qin[:, h, :], start=True, stop=True)
            last.then_inc(scores, 1)
            pe.wait_ge(prod_done, 3)
            for h in range(H):
                last = nc.tensor.transpose(kinT_v[:, h, :], kin[:, h, :], ident[:])
            last.then_inc(kin_t, 1)
            pe.wait_ge(A_done, 1)
            pe.wait_ge(S_in, 16 * B)
            pe.wait_ge(qk_out, 2)
            for h in range(H):
                for c in range(2):
                    hc, e = 2 * h + c, slice(c * P, (c + 1) * P)
                    nc.tensor.matmul(ps_t[:, hc, :], v[:, h, e], A[:, h, :], start=True, stop=False)
                    for q in range(B):
                        last = nc.tensor.matmul(ps_t[:, hc, T * q:T * q + T], S[:, q, h, e], qin[:, h, T * q:T * q + T],
                                                start=False, stop=(q == B - 1))
            last.then_inc(oT_done, 1)
            pe.wait_ge(oT_out, 1)
            o_v = ps_o[:].rearrange("t h (c e) -> t (h c) e", c=2)
            for hc in range(HC):
                last = nc.tensor.transpose(o_v[:, hc, :], oT[:, hc, :], ident[:])
            last.then_inc(o_t, 1)
            pe.wait_ge(kinT_out, 1)
            for q in range(B):
                pe.wait_ge(ownk_done, q + 1)
                if q >= 2:
                    pe.wait_ge(S_done, q - 1)
                for h in range(H):
                    last = nc.tensor.matmul(ps_kv[:, q % 2, h, :], own_k[:, q, h, :], v[:, h, :], start=True, stop=True)
                last.then_inc(kv_done, 1)


def attend(nc, d, group):
    import concourse.bass as bass
    from concourse import mybir
    from contextlib import ExitStack
    fp32, ACT, ALU = mybir.dt.float32, mybir.ActivationFunctionType, mybir.AluOpType
    AX = mybir.AxisListType.X
    memory = group == NG
    R = 1 if memory else WINDOWS[group][1]
    NH = H if memory else 2 * H
    SCALE = DK ** -0.5
    CLASS = min(P, SEQ // R)
    col = C_QM if memory else C_DIL + group * 3 * 512

    def tiles(j):
        return (0, 1) if memory or R == 1 or (R == 4 and j == 1) else (1,)

    def rows(t2, i, j):
        if R == 1:
            return [(0, t2[bass.ds(i * 2 * P + j * P, P), :])]
        v = t2.rearrange("(m r) n -> r m n", r=R)
        if R == 4:
            return [(0, v[bass.ds(i, 1), j * P:(j + 1) * P, :].rearrange("a m n -> (a m) n"))]
        return [(c * CLASS, v[bass.ds(i * 4 + j * 2 + c, 1), :, :].rearrange("a m n -> (a m) n")) for c in range(P // CLASS)]

    PARTS = P // CLASS
    tag = f"at{group}_"
    with ExitStack() as ctx:
        sb = lambda n, s: ctx.enter_context(nc.sbuf_tensor(tag + n, s, fp32))
        pb = lambda n, s: ctx.enter_context(nc.psum_tensor(tag + n, s, fp32))
        sem = stage_semaphores(nc, ctx, tag)
        signals = []

        def signal(n, per=1):
            signals.append(Signal(sem(n), per))
            return signals[-1]

        ident, mask, mask_prev = sb("ident", [P, P]), sb("mask", [P, 2, P]), sb("mask_prev", [P, P])
        eps = sb("eps", [P, 1])
        gain = sb("gain", [P, 2, 2, P])
        x, tab = sb("x", [P, 2, NH, P]), sb("tab", [P, 2, 2, P])
        tg = sb("tg", [P, 2, 2, P])
        sq, stat = sb("sq", [P, 2 * H, P]), sb("stat", [P, 3, 2 * H])
        xr, t1, t2 = sb("xr", [P, NH, P]), sb("t1", [P, NH, P]), sb("t2", [P, NH, P])
        y = sb("y", [P, 2, NH, P])
        qT, kT = sb("qT", [P, H, P]), sb("kT", [P, 2, H, P])
        v = sb("v", [P, 2, H, P])
        e, pT = sb("e", [P, H, 2, P]), sb("pT", [P, H, 2, P])
        mx, nm, den, rden, lnd = (sb(n, [P, H]) for n in ("mx", "nm", "den", "rden", "lnd"))
        o, lse = sb("o", [P, 2, H, P]), sb("lse", [P, 2, H])
        zk = sb("zk", [P, H, P]) if memory else None
        ps_t, ps_s = pb("ps_t", [P, 2 * H, P]), pb("ps_s", [P, H, 2, P])
        ps_p, ps_o = pb("ps_p", [P, H, 2, P]), pb("ps_o", [P, H, P])

        zk_in, key_sq, key_ss, key_ln, key_rs = (sem(n) for n in ("zk_in", "key_sq", "key_ss", "key_ln", "key_rs"))
        key_normed, key_gained, key_t, key_out, key_stored = (sem(n) for n in ("key_normed", "key_gained", "key_t", "key_out", "key_stored"))
        consts_in, set_up, masked = sem("consts_in"), sem("set_up"), sem("masked")
        x_in, v_in = [sem(f"x_in{i}") for i in range(2)], [sem(f"v_in{i}") for i in range(2)]
        X_LOADS = PARTS * (1 if memory else 2)
        k_stored, o_stored = [sem(f"k_stored{i}") for i in range(2)], [sem(f"o_stored{i}") for i in range(2)]
        O_STORES = PARTS * (1 if memory else 2)
        tg_done, sq_done, ss_done, ln_done, rs_done = (signal(n) for n in ("tg", "sq", "ss", "ln", "rs"))
        xr_done, t1_done, t2_done, y_done = (signal(n) for n in ("xr", "t1", "t2", "y"))
        t_done, T_out, scores = signal("t"), signal("T_out", 2), signal("scores")
        sm_done, mx_done, nm_done, e_done = (signal(n) for n in ("sm", "mx", "nm", "e"))
        p_t, pT_act, pT_dve, o_done = (signal(n) for n in ("p_t", "pT_act", "pT_dve", "o"))
        rd_done, lnd_done, lse_done, out_done = (signal(n) for n in ("rd", "lnd", "lse", "out"))
        keeps = lambda j: not memory and (R == 16 or (R == 4 and j == 1))

        block = ctx.enter_context(nc.Block())
        z, zm = d["z"][0:SEQ, :], d["zm"]

        def ahead(eng, front, back):
            front(0, 0, 0)
            with eng.Fori(0, NT // 2 - 1) as i:
                front(i * 2 + 1, i, 1)
                back(i * 2, i, 0)
                front(i * 2 + 2, i + 1, 0)
                back(i * 2 + 1, i, 1)
            i = NT // 2 - 1
            front(2 * i + 1, i, 1)
            back(2 * i, i, 0)
            back(2 * i + 1, i, 1)

        @block.sync
        def _(sp):
            for s in signals:
                s.prime(sp)
            for s in k_stored + o_stored:
                sp.sem_inc(s, 16)
            sp.dma_start(ident[:], d["ident"]).then_inc(consts_in, 16)
            gains = [d["mem_qn_g"], d["mem_kn_g"]] if memory else [d["dil_qn_g"], d["dil_kn_g"]]
            for n, g in enumerate(gains):
                sp.dma_start(gain[:, 0, n, :], g.partition_broadcast(P)).then_inc(consts_in, 16)
                for half in range(2):
                    sp.dma_start(gain[:, 1, n, half * 64:half * 64 + 64],
                                 g[64 - half * 64:128 - half * 64].partition_broadcast(P)).then_inc(consts_in, 16)
            if memory:
                for m in range(2):
                    sp.dma_start(v[:, m], zm[m * P:(m + 1) * P, 512:1024].rearrange("t (h e) -> t h e", h=H)).then_inc(v_in[m], 16)
                    if m:
                        sp.wait_ge(key_normed, 1)
                    sp.dma_start(zk[:], zm[m * P:(m + 1) * P, 0:512].rearrange("t (h e) -> t h e", h=H)).then_inc(zk_in, 16)
                    sp.wait_ge(key_gained, m + 1)
                    sp.dma_start(d["mem_k_p"][m * P:(m + 1) * P, :].rearrange("t (h e) -> t h e", h=H), y[:, m]).then_inc(key_stored, 16)
                    sp.wait_ge(key_stored, 16 * (m + 1))
            else:
                own = d["mask_pair"] if R == 16 else d["mask_own"]
                sp.dma_start(mask[:, 1, :], own).then_inc(consts_in, 16)
                sp.dma_start(mask_prev[:], d["mask_prev"]).then_inc(consts_in, 16)

            def load_x(turn, i, j):
                sp.wait_ge(xr_done.sem, xr_done.at(turn, back=2))
                sp.wait_ge(sq_done.sem, sq_done.at(turn, back=2))
                for p0, src in rows(z[:, col:col + NH * P], i, j):
                    sp.dma_start(x[p0:p0 + CLASS, j, :, :], src.rearrange("t (h e) -> t h e", e=P)).then_inc(x_in[j], 16)
                if not memory:
                    sp.wait_ge(tg_done.sem, tg_done.at(turn, back=2))
                    for p0, src in rows(d["rope"][0:SEQ, :], i, j):
                        sp.dma_start(tab[p0:p0 + CLASS, j], src.rearrange("t (c e) -> t c e", c=2)).then_inc(x_in[j], 16)

            def load_v(turn, i, j):
                for p0, src in rows(z[:, col + 1024:col + 1536], i, j):
                    sp.dma_start(v[p0:p0 + CLASS, j], src.rearrange("t (h e) -> t h e", h=H)).then_inc(v_in[j], 16)

            def back(turn, i, j, more_x=True, more_v=True):
                if not memory:
                    sp.wait_ge(y_done.sem, y_done.at(turn))
                    for p0, dst in rows(d["kr"][group], i, j):
                        sp.dma_start(dst.rearrange("t (h e) -> t h e", h=H), y[p0:p0 + CLASS, j, H:, :]).then_inc(k_stored[j], 16)
                if more_x:
                    load_x(turn + 2, i + 1, j)
                sp.wait_ge(o_done.sem, o_done.at(turn))
                if more_v and not memory:
                    load_v(turn + 1, i + j, 1 - j)
                sp.wait_ge(out_done.sem, out_done.at(turn))
                out = d["acts"][0:SEQ, 1536:2048] if memory else d["od"][group]
                for p0, dst in rows(out, i, j):
                    sp.dma_start(dst.rearrange("t (h e) -> t h e", h=H), o[p0:p0 + CLASS, j]).then_inc(o_stored[j], 16)
                if not memory:
                    sp.wait_ge(lse_done.sem, lse_done.at(turn))
                    for p0, dst in rows(d["lse"][group], i, j):
                        sp.dma_start(dst, lse[p0:p0 + CLASS, j, :]).then_inc(o_stored[j], 16)

            load_x(0, 0, 0)
            load_x(1, 0, 1)
            if not memory:
                load_v(0, 0, 0)
            with sp.Fori(0, NT // 2 - 1) as i:
                for j in range(2):
                    back(i * 2 + j, i, j)
            for j in range(2):
                back(NT - 2 + j, NT // 2 - 1, j, more_x=False, more_v=(j == 0))
            for j in range(2):
                if not memory:
                    sp.wait_ge(k_stored[j], 16 + 16 * PARTS * (NT // 2))
                sp.wait_ge(o_stored[j], 16 + 16 * O_STORES * (NT // 2))

        N_CONSTS = 1 + 6 + (0 if memory else 2)

        @block.gpsimd
        def _(pool):
            pool.wait_ge(consts_in, 16 * N_CONSTS)

            def front(turn, i, j):
                pool.wait_ge(x_in[j], i * (16 * X_LOADS) + 16 * X_LOADS)
                if not memory:
                    pool.wait_ge(t1_done.sem, t1_done.at(turn, back=1))
                    pool.wait_ge(t2_done.sem, t2_done.at(turn, back=1))
                    nc.gpsimd.tensor_tensor(tg[:], tab[:, j].unsqueeze(2).to_broadcast([P, 2, 2, P]), gain[:],
                                            ALU.mult).then_inc(tg_done.sem, 1)
                pool.wait_ge(rs_done.sem, rs_done.at(turn))
                pool.wait_ge(t1_done.sem, t1_done.at(turn, back=1))
                nc.gpsimd.tensor_tensor(xr[:], x[:, j], stat[:, 2, 0:NH].unsqueeze(2).to_broadcast([P, NH, P]),
                                        ALU.mult).then_inc(xr_done.sem, 1)
                if not memory:
                    pool.wait_ge(xr_done.sem, xr_done.at(turn))
                    pool.wait_ge(tg_done.sem, tg_done.at(turn))
                    pool.wait_ge(y_done.sem, y_done.at(turn, back=1))
                    for n in range(2):
                        for half in range(2):
                            dst, src = slice(half * 64, half * 64 + 64), slice(64 - half * 64, 128 - half * 64)
                            last = nc.gpsimd.tensor_tensor(t2[:, n * H:(n + 1) * H, dst], xr[:, n * H:(n + 1) * H, src],
                                                           tg[:, 1, n, dst].unsqueeze(1).to_broadcast([P, H, 64]), ALU.mult)
                    last.then_inc(t2_done.sem, 1)

            ahead(pool, front, lambda turn, i, j: None)

        @block.scalar
        def _(act):
            nc.scalar.preload_act_table_set(TABLES)
            act.wait_ge(set_up, 1)
            if memory:
                for m in range(2):
                    act.wait_ge(zk_in, 16 * (m + 1))
                    act.wait_ge(key_ss, m) if m else None
                    nc.scalar.activation(sq[:, 0:H], zk[:], ACT.Square).then_inc(key_sq, 1)
                    act.wait_ge(key_ss, m + 1)
                    nc.scalar.activation(stat[:, 1, 0:H], stat[:, 0, 0:H], ACT.Ln, bias=eps[:], scale=1.0 / DK).then_inc(key_ln, 1)
                    act.wait_ge(key_ln, m + 1)
                    nc.scalar.activation(stat[:, 2, 0:H], stat[:, 1, 0:H], ACT.Exp, scale=-0.5).then_inc(key_rs, 1)
                    act.wait_ge(key_t, m + 1)
                    nc.scalar.copy(kT[:, m], ps_t[:, 0:H]).then_inc(key_out, 1)

            def front(turn, i, j):
                act.wait_ge(x_in[j], i * (16 * X_LOADS) + 16 * X_LOADS)
                act.wait_ge(ss_done.sem, ss_done.at(turn, back=1))
                nc.scalar.activation(sq[:, 0:NH], x[:, j], ACT.Square).then_inc(sq_done.sem, 1)
                act.wait_ge(ss_done.sem, ss_done.at(turn))
                nc.scalar.activation(stat[:, 1, 0:NH], stat[:, 0, 0:NH], ACT.Ln, bias=eps[:], scale=1.0 / DK).then_inc(ln_done.sem, 1)
                act.wait_ge(ln_done.sem, ln_done.at(turn))
                act.wait_ge(xr_done.sem, xr_done.at(turn, back=1))
                nc.scalar.activation(stat[:, 2, 0:NH], stat[:, 1, 0:NH], ACT.Exp, scale=-0.5).then_inc(rs_done.sem, 1)
                act.wait_ge(t_done.sem, t_done.at(turn))
                act.wait_ge(scores.sem, scores.at(turn, back=1))
                nc.scalar.copy(qT[:], ps_t[:, 0:H]).then_inc(T_out.sem, 1)
                if memory:
                    act.sem_inc(T_out.sem, 1)
                else:
                    nc.scalar.copy(kT[:, j], ps_t[:, H:]).then_inc(T_out.sem, 1)

            def back(turn, i, j):
                act.wait_ge(nm_done.sem, nm_done.at(turn))
                act.wait_ge(rd_done.sem, rd_done.at(turn, back=1))
                w = slice(tiles(j)[0], 2)
                for h in range(H):
                    last = nc.scalar.activation(e[:, h, w], e[:, h, w], ACT.Exp, bias=nm[:, h:h + 1], accum_out=den[:, h:h + 1])
                last.then_inc(e_done.sem, 1)
                if not memory:
                    act.wait_ge(e_done.sem, e_done.at(turn))
                    act.wait_ge(lse_done.sem, lse_done.at(turn, back=1))
                    nc.scalar.activation(lnd[:], den[:], ACT.Ln).then_inc(lnd_done.sem, 1)
                act.wait_ge(p_t.sem, p_t.at(turn))
                act.wait_ge(o_done.sem, o_done.at(turn, back=1))
                nc.scalar.copy(pT[:, 0:2, w], ps_p[:, 0:2, w]).then_inc(pT_act.sem, 1)

            ahead(act, front, back)

        @block.vector
        def _(dve):
            nc.vector.memset(eps[:], EPS).then_inc(set_up, 1)
            if memory:
                dve.wait_ge(consts_in, 16 * N_CONSTS)
                for m in range(2):
                    dve.wait_ge(key_sq, m + 1)
                    nc.vector.tensor_reduce(stat[:, 0, 0:H], sq[:, 0:H], axis=AX, op=ALU.add).then_inc(key_ss, 1)
                    dve.wait_ge(key_rs, m + 1)
                    nc.vector.tensor_tensor(xr[:], zk[:], stat[:, 2, 0:H].unsqueeze(2).to_broadcast([P, H, P]), ALU.mult).then_inc(key_normed, 1)
                    dve.wait_ge(key_normed, m + 1)
                    nc.vector.tensor_tensor(y[:, m], xr[:], gain[:, 0, 1, :].unsqueeze(1).to_broadcast([P, H, P]), ALU.mult).then_inc(key_gained, 1)
                dve.wait_ge(key_stored, 32)
            else:
                nc.vector.memset(mask[:, 0, :], NEG).then_inc(masked, 1)
                nc.vector.memset(kT[:], 0.0).then_inc(masked, 1)
                nc.vector.memset(v[:, 1], 0.0).then_inc(masked, 1)
                dve.wait_ge(masked, 3)
            dve.wait_ge(consts_in, 16 * N_CONSTS)
            if R == 4:
                nc.vector.tensor_copy(mask[:, 0, :], mask_prev[:]).then_inc(masked, 1)
                dve.wait_ge(masked, 4)

            def front(turn, i, j):
                dve.wait_ge(sq_done.sem, sq_done.at(turn))
                dve.wait_ge(ln_done.sem, ln_done.at(turn, back=1))
                nc.vector.tensor_reduce(stat[:, 0, 0:NH], sq[:, 0:NH], axis=AX, op=ALU.add).then_inc(ss_done.sem, 1)
                dve.wait_ge(xr_done.sem, xr_done.at(turn))
                dve.wait_ge(t_done.sem, t_done.at(turn, back=2))
                if memory:
                    nc.vector.tensor_tensor(y[:, j], xr[:], gain[:, 0, 0, :].unsqueeze(1).to_broadcast([P, H, P]), ALU.mult).then_inc(y_done.sem, 1)
                    dve.sem_inc(t1_done.sem, 1)
                    return
                dve.wait_ge(k_stored[j], i * (16 * PARTS) + 16)
                dve.wait_ge(tg_done.sem, tg_done.at(turn))
                dve.wait_ge(y_done.sem, y_done.at(turn, back=1))
                nc.vector.tensor_tensor(t1[:].rearrange("p (n h) e -> p n h e", n=2), xr[:].rearrange("p (n h) e -> p n h e", n=2),
                                        tg[:, 0].unsqueeze(2).to_broadcast([P, 2, H, P]), ALU.mult).then_inc(t1_done.sem, 1)
                dve.wait_ge(t1_done.sem, t1_done.at(turn))
                dve.wait_ge(t2_done.sem, t2_done.at(turn))
                nc.vector.tensor_tensor(y[:, j], t1[:], t2[:], ALU.add).then_inc(y_done.sem, 1)

            def back(turn, i, j):
                first = tiles(j)[0]
                n, w = 2 - first, slice(first, 2)
                dve.wait_ge(scores.sem, scores.at(turn))
                dve.wait_ge(p_t.sem, p_t.at(turn, back=1))
                if memory:
                    nc.vector.tensor_scalar(e[:], ps_s[:], SCALE, None, ALU.mult).then_inc(sm_done.sem, 1)
                else:
                    nc.vector.scalar_tensor_tensor(out=e[:, :, w], in0=ps_s[:, :, w], scalar=SCALE,
                                                   in1=mask[:, w].unsqueeze(1).to_broadcast([P, H, n, P]),
                                                   op0=ALU.mult, op1=ALU.add).then_inc(sm_done.sem, 1)
                dve.wait_ge(sm_done.sem, sm_done.at(turn))
                if R == 1 and not memory:
                    nc.vector.tensor_copy(mask[:, 0, :], mask_prev[:]).then_inc(masked, 1)
                dve.wait_ge(lse_done.sem, lse_done.at(turn, back=1)) if not memory else None
                nc.vector.tensor_reduce(mx[:], e[:, :, w].rearrange("p h n k -> p h (n k)"), axis=AX, op=ALU.max).then_inc(mx_done.sem, 1)
                dve.wait_ge(mx_done.sem, mx_done.at(turn))
                dve.wait_ge(e_done.sem, e_done.at(turn, back=1))
                nc.vector.tensor_scalar(nm[:], mx[:], -1.0, None, ALU.mult).then_inc(nm_done.sem, 1)
                dve.wait_ge(e_done.sem, e_done.at(turn))
                nc.vector.reciprocal(rden[:], den[:]).then_inc(rd_done.sem, 1)
                dve.wait_ge(p_t.sem, p_t.at(turn))
                dve.wait_ge(o_done.sem, o_done.at(turn, back=1))
                nc.vector.tensor_copy(pT[:, 2:4, w], ps_p[:, 2:4, w]).then_inc(pT_dve.sem, 1)
                dve.wait_ge(o_stored[j], i * (16 * O_STORES) + 16)
                if not memory:
                    dve.wait_ge(lnd_done.sem, lnd_done.at(turn))
                    nc.vector.tensor_tensor(lse[:, j], lnd[:], mx[:], ALU.add).then_inc(lse_done.sem, 1)
                dve.wait_ge(rd_done.sem, rd_done.at(turn))
                dve.wait_ge(o_done.sem, o_done.at(turn))
                nc.vector.tensor_tensor(o[:, j], ps_o[:], rden[:].unsqueeze(2).to_broadcast([P, H, P]), ALU.mult).then_inc(out_done.sem, 1)

            ahead(dve, front, back)

        @block.tensor
        def _(pe):
            pe.wait_ge(consts_in, 16)
            if memory:
                for m in range(2):
                    pe.wait_ge(key_gained, m + 1)
                    if m:
                        pe.wait_ge(key_out, m)
                    for h in range(H):
                        last = nc.tensor.transpose(ps_t[:, h, :], y[:, m, h, :], ident[:])
                    last.then_inc(key_t, 1)
                pe.wait_ge(key_out, 2)
            else:
                pe.wait_ge(masked, 3)
                pe.wait_ge(consts_in, 16 * N_CONSTS)

            def front(turn, i, j):
                pe.wait_ge(y_done.sem, y_done.at(turn))
                pe.wait_ge(T_out.sem, T_out.at(turn, back=1))
                for h in range(NH):
                    last = nc.tensor.transpose(ps_t[:, h, :], y[:, j, h, :], ident[:])
                last.then_inc(t_done.sem, 1)
                pe.wait_ge(T_out.sem, T_out.at(turn))
                pe.wait_ge(sm_done.sem, sm_done.at(turn, back=1))
                for h in range(H):
                    for n in tiles(j):
                        key = n if memory else (j if n else 1 - j)
                        last = nc.tensor.matmul(ps_s[:, h, n, :], qT[:, h, :], kT[:, key, h, :], start=True, stop=True)
                last.then_inc(scores.sem, 1)

            def back(turn, i, j):
                pe.wait_ge(e_done.sem, e_done.at(turn))
                pe.wait_ge(pT_act.sem, pT_act.at(turn, back=1))
                pe.wait_ge(pT_dve.sem, pT_dve.at(turn, back=1))
                for h in range(H):
                    for n in tiles(j):
                        last = nc.tensor.transpose(ps_p[:, h, n, :], e[:, h, n, :], ident[:])
                last.then_inc(p_t.sem, 1)
                pe.wait_ge(pT_act.sem, pT_act.at(turn))
                pe.wait_ge(pT_dve.sem, pT_dve.at(turn))
                if memory:
                    pe.wait_ge(v_in[0], 16)
                    pe.wait_ge(v_in[1], 16)
                else:
                    pe.wait_ge(v_in[j], i * (16 * PARTS) + 16 * PARTS)
                pe.wait_ge(out_done.sem, out_done.at(turn, back=1))
                for h in range(H):
                    for n in tiles(j):
                        key = n if memory else (j if n else 1 - j)
                        last = nc.tensor.matmul(ps_o[:, h, :], pT[:, h, n, :], v[:, key, h, :],
                                                start=(n == tiles(j)[0]), stop=(n == 1))
                last.then_inc(o_done.sem, 1)

            ahead(pe, front, back)


def decode(nc, d):
    import concourse.bass as bass
    from concourse import mybir
    from contextlib import ExitStack
    fp32, ACT, ALU = mybir.dt.float32, mybir.ActivationFunctionType, mybir.AluOpType
    AX = mybir.AxisListType.X
    B, T = DEC_B, DEC_T
    NH = NG * 2 * H + H
    SCALE = DK ** -0.5
    UNITS = [(0, 0, T)] + [(1, t, 1) for t in range(T)] + [(2, t, 1) for t in range(T)] + [(3, 0, T), (4, 0, T)]
    NU = len(UNITS)
    KEYS = P + NS

    with ExitStack() as ctx:
        sb = lambda n, s: ctx.enter_context(nc.sbuf_tensor("de_" + n, s, fp32))
        pb = lambda n, s: ctx.enter_context(nc.psum_tensor("de_" + n, s, fp32))
        sem = stage_semaphores(nc, ctx, "de_")
        signals = []

        def signal(n, per=1):
            signals.append(Signal(sem(n), per))
            return signals[-1]

        ident, mask, eps = sb("ident", [P, P]), sb("mask", [P, NG, KEYS]), sb("eps", [P, 1])
        gain, tab, tg = sb("gain", [NS, 2, 2, P]), sb("tab", [NS, 2, P]), sb("tg", [NS, 2, 2, P])
        gain_m = sb("gain_m", [NS, P])
        x, sq, xr = sb("x", [NS, NH, P]), sb("sq", [NS, NH, P]), sb("xr", [NS, NH, P])
        stat = sb("stat", [NS, 3, NH])
        t1, t2, y = sb("t1", [NS, NH - H, P]), sb("t2", [NS, NH - H, P]), sb("y", [NS, NH, P])
        vn = sb("vn", [NS, NG, H, P])
        yT = sb("yT", [P, NH, NS])
        kv = sb("kv", [P, 2, NU, 512])
        kT = sb("kT", [P, 2, H, P])
        sT, s, sm, p = sb("sT", [P, 5, P]), sb("s", [P, NG, KEYS]), sb("sm", [P, 2, P]), sb("p", [P, NG, KEYS])
        nm, den, rden = sb("nm", [P, 4]), sb("den", [P, 4]), sb("rden", [P, 4])
        mx, lse, wt, wsum = sb("mx", [P, 4]), sb("lse", [P, NG]), sb("wt", [P, NG]), sb("wsum", [P, 3])
        pT, pnT = sb("pT", [P, 5, P]), sb("pnT", [NS, NG, P])
        oT, o = sb("oT", [P, 2, P]), sb("o", [NS, 2, H, P])
        zero = sb("zero", [P, P])
        ps_t = pb("ps_t", [P, 2, 512])
        ps_sd, ps_sm = pb("ps_sd", [P, NG, P]), pb("ps_sm", [P, 2, P])
        ps_n, ps_x = pb("ps_n", [P, NG, NS]), pb("ps_x", [P, 5, P])
        ps_od, ps_om = ps_sd[:, 0, :], ps_sm[:, 0, :]
        head = lambda g, n, h: (g * 2 + n) * H + h
        query = lambda g, h: head(g, 0, h) if g < NG else NG * 2 * H + h

        steps = {}

        def st(n):
            if n not in steps:
                steps[n] = sem(n)
            return steps[n]

        kv_in = [sem(f"kv_in{i}") for i in range(2)]
        KV_LOADS = 4
        t_done, T_out, used = signal("t", 2 * NU), (signal("T_act", NU), signal("T_dve", NU)), signal("used", 2)
        v_used = signal("v_used", 2)

        block = ctx.enter_context(nc.Block())
        z = d["z"][SEQ:ROWS, :]

        def load(eng, caches, mem, b, j):
            row = lambda a: a[bass.ds(b, 1), :, :].rearrange("a m n -> (a m) n")
            eng.dma_start(kv[:, j, 0, :], row(caches[0])).then_inc(kv_in[j], 16)
            for g in (1, 2):
                src = row(caches[g]).rearrange("(m r) n -> m r n", m=P)[:, 0:T, :]
                eng.dma_start(kv[:, j, 1 + T * (g - 1):1 + T * g, :], src).then_inc(kv_in[j], 16)
            eng.dma_start(kv[:, j, NU - 2:NU, :], row(mem).rearrange("(k m) n -> m k n", k=2)).then_inc(kv_in[j], 16)

        @block.sync
        def _(sp):
            for s_ in signals:
                s_.prime(sp)
            for g in range(NG):
                c = C_DIL + g * 1536
                sp.dma_start(x[:, g * 8:g * 8 + 8, :], z[:, c:c + 1024].rearrange("t (h e) -> t h e", e=P)).then_inc(st("x_in"), 16)
                sp.dma_start(vn[:, g], z[:, c + 1024:c + 1536].rearrange("t (h e) -> t h e", e=P)).then_inc(st("vn_in"), 16)
            sp.dma_start(x[:, 24:28, :], z[:, C_QM:C_QM + 512].rearrange("t (h e) -> t h e", e=P)).then_inc(st("x_in"), 16)
            with sp.Fori(0, B // 2) as i:
                for j in range(2):
                    sp.wait_ge(used.sem, used.at(i, j + 1, back=1))
                    load(sp, [d[f"cache_dil_k{g}"] for g in range(NG)], d["cache_mem_k"], i * 2 + j, j)
            values = [d[f"cache_dil_v{g}"] for g in range(NG)], d["cache_mem_v"]
            for j in range(2):
                sp.wait_ge(used.sem, used.at(B // 2 - 1, j + 1))
                load(sp, *values, j, j)
            with sp.Fori(1, B // 2) as i:
                for j in range(2):
                    sp.wait_ge(v_used.sem, v_used.at(i, j + 1, back=1))
                    load(sp, *values, i * 2 + j, j)
            sp.wait_ge(st("o_out"), 1)
            for n in range(2):
                sp.dma_start(d["acts"][SEQ:ROWS, 1024 + 512 * n:1536 + 512 * n].rearrange("t (h e) -> t h e", e=P), o[:, n]).then_inc(st("stored"), 16)
            sp.wait_ge(st("stored"), 32)

        @block.gpsimd
        def _(pool):
            consts = [(ident[:], d["ident"]), (mask[:], d["dec_mask"]),
                      (tab[:], d["rope"][SEQ:ROWS, :].rearrange("t (c e) -> t c e", c=2)),
                      (gain_m[:], d["mem_qn_g"].partition_broadcast(NS))]
            for n, g in enumerate((d["dil_qn_g"], d["dil_kn_g"])):
                consts += [(gain[:, 0, n, :], g.partition_broadcast(NS))]
                consts += [(gain[:, 1, n, f:f + 64], g[64 - f:128 - f].partition_broadcast(NS)) for f in (0, 64)]
            for dst, src in consts:
                pool.dma_start(dst, src).then_inc(st("consts_in"), 16)
            pool.wait_ge(st("consts_in"), 16 * len(consts))
            nc.gpsimd.tensor_tensor(tg[:], tab[:].unsqueeze(2).to_broadcast([NS, 2, 2, P]), gain[:], ALU.mult).then_inc(st("tg"), 1)
            pool.wait_ge(st("xr"), 1)
            pool.wait_ge(st("tg"), 1)
            for g in range(NG):
                for n in range(2):
                    hs = slice(head(g, n, 0), head(g, n, H))
                    for f in (0, 64):
                        last = nc.gpsimd.tensor_tensor(t2[:, hs, f:f + 64], xr[:, hs, 64 - f:128 - f],
                                                       tg[:, 1, n, f:f + 64].unsqueeze(1).to_broadcast([NS, H, 64]), ALU.mult)
            last.then_inc(st("t2"), 1)
            pool.wait_ge(st("y"), 1)
            for g in range(NG):
                pool.dma_start(d["ks"][g].rearrange("t (h e) -> t h e", e=P), y[:, head(g, 1, 0):head(g, 1, H), :]).then_inc(st("ks_stored"), 16)
            pool.wait_ge(st("ks_stored"), 48)

        def copy_transposed(eng, i, j, u, copy):
            n = j * NU + u
            eng.wait_ge(t_done.sem, t_done.at(i, n + 1))
            copy(kT[:, n % 2], ps_t[:, n % 2, :].rearrange("p (h k) -> p h k", h=H)).then_inc(T_out[n % 2].sem, 1)

        @block.scalar
        def _(act):
            nc.scalar.preload_act_table_set(TABLES)
            act.wait_ge(st("x_in"), 64)
            act.wait_ge(st("eps"), 1)
            nc.scalar.activation(sq[:], x[:], ACT.Square).then_inc(st("sq"), 1)
            act.wait_ge(st("ss"), 1)
            nc.scalar.activation(stat[:, 1, :], stat[:, 0, :], ACT.Ln, bias=eps[0:NS, :], scale=1.0 / DK).then_inc(st("ln"), 1)
            act.wait_ge(st("ln"), 1)
            nc.scalar.activation(stat[:, 2, :], stat[:, 1, :], ACT.Exp, scale=-0.5).then_inc(st("rs"), 1)
            act.wait_ge(st("y_t"), 1)
            nc.scalar.copy(yT[:, 0:16, :], ps_t[:, 0, :].rearrange("p (h t) -> p h t", t=NS)).then_inc(st("yT"), 1)
            nc.scalar.copy(yT[:, 16:28, :], ps_t[:, 1, 0:384].rearrange("p (h t) -> p h t", t=NS)).then_inc(st("yT"), 1)
            with act.Fori(0, B // 2) as i:
                for j in range(2):
                    for u in range(NU):
                        if (j * NU + u) % 2 == 0:
                            copy_transposed(act, i, j, u, nc.scalar.copy)
            act.wait_ge(st("nm"), 1)
            for g in range(NG):
                last = nc.scalar.activation(p[:, g, :], s[:, g, :], ACT.Exp, bias=nm[:, g:g + 1], accum_out=den[:, g:g + 1])
            last = nc.scalar.activation(sm[:], sm[:], ACT.Exp, bias=nm[:, 3:4], accum_out=den[:, 3:4])
            last.then_inc(st("e"), 1)
            act.wait_ge(st("e"), 1)
            nc.scalar.activation(lse[:], den[:, 0:NG], ACT.Ln).then_inc(st("lnd"), 1)
            act.wait_ge(st("lse_m"), 1)
            nc.scalar.activation(wt[:], lse[:], ACT.Exp, accum_out=wsum[:, 1:2]).then_inc(st("wt"), 1)
            act.wait_ge(st("p_t"), 1)
            nc.scalar.copy(pT[:], ps_x[:]).then_inc(st("pT"), 1)
            nc.scalar.copy(pnT[:], ps_t[0:NS, 0, 0:NG * P].rearrange("p (g c) -> p g c", g=NG)).then_inc(st("pT"), 1)
            act.wait_ge(st("oT_done"), 1)
            nc.scalar.copy(oT[:, 0, :], ps_od).then_inc(st("oT"), 1)
            nc.scalar.copy(oT[:, 1, :], ps_om).then_inc(st("oT"), 1)
            act.wait_ge(st("o_t"), 1)
            nc.scalar.copy(o[:].rearrange("t n h e -> t (n h) e"), ps_t[0:NS].rearrange("t b (h e) -> t (b h) e", e=P)).then_inc(st("o_out"), 1)

        @block.vector
        def _(dve):
            nc.vector.memset(eps[:], EPS).then_inc(st("eps"), 1)
            nc.vector.memset(zero[:], 0.0).then_inc(st("zero"), 1)
            dve.wait_ge(st("sq"), 1)
            nc.vector.tensor_reduce(stat[:, 0, :], sq[:], axis=AX, op=ALU.add).then_inc(st("ss"), 1)
            dve.wait_ge(st("rs"), 1)
            nc.vector.tensor_tensor(xr[:], x[:], stat[:, 2, :].unsqueeze(2).to_broadcast([NS, NH, P]), ALU.mult).then_inc(st("xr"), 1)
            dve.wait_ge(st("xr"), 1)
            dve.wait_ge(st("tg"), 1)
            for g in range(NG):
                hs = slice(head(g, 0, 0), head(g, 1, H))
                last = nc.vector.tensor_tensor(t1[:, hs, :].rearrange("t (n h) e -> t n h e", n=2),
                                               xr[:, hs, :].rearrange("t (n h) e -> t n h e", n=2),
                                               tg[:, 0].unsqueeze(2).to_broadcast([NS, 2, H, P]), ALU.mult)
            last.then_inc(st("t1"), 1)
            nc.vector.tensor_tensor(y[:, NH - H:, :], xr[:, NH - H:, :], gain_m[:].unsqueeze(1).to_broadcast([NS, H, P]), ALU.mult).then_inc(st("ym"), 1)
            dve.wait_ge(st("t1"), 1)
            dve.wait_ge(st("t2"), 1)
            nc.vector.tensor_tensor(y[:, 0:NH - H, :], t1[:], t2[:], ALU.add).then_inc(st("y"), 1)
            with dve.Fori(0, B // 2) as i:
                for j in range(2):
                    for u in range(NU):
                        if (j * NU + u) % 2 == 1:
                            copy_transposed(dve, i, j, u, nc.vector.tensor_copy)
            dve.wait_ge(used.sem, used.at(B // 2 - 1))
            nc.vector.tensor_scalar(sT[:, 0:NG, :], ps_sd[:], SCALE, None, ALU.mult).then_inc(st("sT"), 1)
            nc.vector.tensor_scalar(sT[:, NG:, :], ps_sm[:], SCALE, None, ALU.mult).then_inc(st("sT"), 1)
            dve.wait_ge(st("s_t"), 1)
            nc.vector.tensor_tensor(s[:, :, 0:P], ps_x[:, 0:NG, :], mask[:, :, 0:P], ALU.add).then_inc(st("s"), 1)
            nc.vector.scalar_tensor_tensor(out=s[:, :, P:], in0=ps_n[:], scalar=SCALE, in1=mask[:, :, P:],
                                           op0=ALU.mult, op1=ALU.add).then_inc(st("s"), 1)
            nc.vector.tensor_copy(sm[:], ps_x[:, NG:, :]).then_inc(st("s"), 1)
            dve.wait_ge(st("s"), 3)
            nc.vector.tensor_reduce(mx[:, 0:NG], s[:], axis=AX, op=ALU.max)
            nc.vector.tensor_reduce(mx[:, 3:4], sm[:].rearrange("p k e -> p (k e)"), axis=AX, op=ALU.max).then_inc(st("mx"), 1)
            dve.wait_ge(st("mx"), 1)
            nc.vector.tensor_scalar(nm[:], mx[:], -1.0, None, ALU.mult).then_inc(st("nm"), 1)
            dve.wait_ge(st("e"), 1)
            nc.vector.reciprocal(rden[:], den[:]).then_inc(st("rd"), 1)
            dve.wait_ge(st("lnd"), 1)
            nc.vector.tensor_tensor(lse[:], lse[:], mx[:, 0:NG], ALU.add).then_inc(st("lse"), 1)
            dve.wait_ge(st("lse"), 1)
            nc.vector.tensor_reduce(wsum[:, 0:1], lse[:], axis=AX, op=ALU.max).then_inc(st("lse_x"), 1)
            dve.wait_ge(st("lse_x"), 1)
            nc.vector.tensor_scalar(lse[:], lse[:], wsum[:, 0:1], None, ALU.subtract).then_inc(st("lse_m"), 1)
            dve.wait_ge(st("wt"), 1)
            nc.vector.reciprocal(wsum[:, 2:3], wsum[:, 1:2]).then_inc(st("wr"), 1)
            dve.wait_ge(st("wr"), 1)
            dve.wait_ge(st("rd"), 1)
            nc.vector.scalar_tensor_tensor(out=rden[:, 0:NG], in0=wt[:], scalar=wsum[:, 2:3], in1=rden[:, 0:NG],
                                           op0=ALU.mult, op1=ALU.mult).then_inc(st("share"), 1)
            dve.wait_ge(st("share"), 1)
            for g in range(NG):
                nc.vector.tensor_scalar(p[:, g, :], p[:, g, :], rden[:, g:g + 1], None, ALU.mult).then_inc(st("p"), 1)
            nc.vector.tensor_scalar(sm[:], sm[:], rden[:, 3:4], None, ALU.mult).then_inc(st("p"), 1)

        @block.tensor
        def _(pe):
            pe.wait_ge(st("consts_in"), 16)
            pe.wait_ge(st("y"), 1)
            pe.wait_ge(st("ym"), 1)
            pe.wait_ge(st("consts_in"), 16 * 10)
            for n in range(NH):
                last = nc.tensor.transpose(ps_t[:, n // 16, NS * (n % 16):NS * (n % 16) + NS], y[:, n, :], ident[0:NS, 0:NS])
            last.then_inc(st("y_t"), 1)
            pe.wait_ge(st("yT"), 2)
            for g in range(NG):
                for h in range(H):
                    last = nc.tensor.matmul(ps_n[h * NS:(h + 1) * NS, g, :], yT[:, head(g, 0, h), :], yT[:, head(g, 1, h), :], start=True, stop=True)
            last.then_inc(st("n_done"), 1)

            def unit_scores(i, j, u):
                n = j * NU + u
                g, t, cols = UNITS[u]
                dst = ps_sd[:, g, :] if g < NG else ps_sm[:, g - NG, :]
                pe.wait_ge(T_out[n % 2].sem, T_out[n % 2].at(i, n // 2 + 1))
                for h in range(H):
                    last = nc.tensor.matmul(dst[:, bass.ds(i * 2 * T + j * T + h * NS + t, cols)], kT[:, n % 2, h, :],
                                            yT[:, query(g, h), bass.ds(i * 2 * T + j * T + t, cols)], start=True, stop=True)
                return last

            with pe.Fori(0, B // 2) as i:
                for j in range(2):
                    pe.wait_ge(kv_in[j], i * (16 * KV_LOADS) + 16 * KV_LOADS)
                    for u in range(NU):
                        n = j * NU + u
                        pe.wait_ge(T_out[n % 2].sem, T_out[n % 2].at(i, n // 2))
                        for h in range(H):
                            last = nc.tensor.transpose(ps_t[:, n % 2, h * P:(h + 1) * P], kv[:, j, u, h * P:(h + 1) * P], ident[:])
                        last.then_inc(t_done.sem, 1)
                        if u:
                            unit_scores(i, j, u - 1)
                    unit_scores(i, j, NU - 1).then_inc(used.sem, 1)
            pe.wait_ge(st("sT"), 2)
            for g in range(5):
                last = nc.tensor.transpose(ps_x[:, g, :], sT[:, g, :], ident[:])
            last.then_inc(st("s_t"), 1)
            pe.wait_ge(st("p"), 4)
            for side in T_out:
                pe.wait_ge(side.sem, side.at(B // 2 - 1))
            for g in range(5):
                nc.tensor.transpose(ps_x[:, g, :], p[:, g, 0:P] if g < NG else sm[:, g - NG, :], ident[:])
            for g in range(NG):
                last = nc.tensor.transpose(ps_t[0:NS, 0, g * P:(g + 1) * P], p[:, g, P:], ident[:])
            last.then_inc(st("p_t"), 1)
            pe.wait_ge(st("pT"), 2)
            pe.wait_ge(st("vn_in"), 48)
            for g in range(NG):
                for h in range(H):
                    last = nc.tensor.matmul(ps_od[:, h * NS:(h + 1) * NS], vn[:, g, h, :], pnT[:, g, h * NS:(h + 1) * NS],
                                            start=(g == 0 and h == 0), stop=False, skip_group_check=True)
            pe.wait_ge(st("zero"), 1)
            nc.tensor.matmul(ps_om[:], zero[:], zero[:], start=True, stop=False, skip_group_check=True)
            with pe.Fori(0, B // 2) as i:
                for j in range(2):
                    pe.wait_ge(kv_in[j], i * (16 * KV_LOADS) + 16 * KV_LOADS * (B // 2 + 1))
                    for u, (g, t, cols) in enumerate(UNITS):
                        dst = ps_od if g < NG else ps_om
                        for h in range(H):
                            c = bass.ds(i * 2 * T + j * T + h * NS + t, cols)
                            last = nc.tensor.matmul(dst[:, c], kv[:, j, u, h * P:(h + 1) * P], pT[:, g, c],
                                                    start=False, stop=False, skip_group_check=True)
                    last.then_inc(v_used.sem, 1)
            nc.tensor.matmul(ps_od[:], zero[:], zero[:], start=False, stop=True, skip_group_check=True)
            nc.tensor.matmul(ps_om[:], zero[:], zero[:], start=False, stop=True, skip_group_check=True).then_inc(st("oT_done"), 1)
            pe.wait_ge(st("oT"), 2)
            for n in range(2):
                for h in range(H):
                    last = nc.tensor.transpose(ps_t[0:NS, n, h * P:(h + 1) * P], oT[:, n, h * NS:(h + 1) * NS], ident[:])
            last.then_inc(st("o_t"), 1)


def merge(nc, d):
    import concourse.bass as bass
    from concourse import mybir
    from contextlib import ExitStack
    fp32, ACT, ALU = mybir.dt.float32, mybir.ActivationFunctionType, mybir.AluOpType
    AX = mybir.AxisListType.X
    KB = 16
    BRANCH = [(0, 8), (8, 12), (12, 16)]
    NGRP = 6

    with ExitStack() as ctx:
        sb = lambda n, s: ctx.enter_context(nc.sbuf_tensor("mg_" + n, s, fp32))
        pb = lambda n, s: ctx.enter_context(nc.psum_tensor("mg_" + n, s, fp32))
        sem = stage_semaphores(nc, ctx, "mg_")
        signals = []

        def signal(n, per=1):
            signals.append(Signal(sem(n), per))
            return signals[-1]

        ident, eps, g2 = sb("ident", [P, P]), sb("eps", [P, 1]), sb("g2", [P, D])
        wb, wo = sb("wb", [P, KB, D]), sb("wo", [P, KD, D])
        a, od3 = sb("a", [P, 2, 2 * D]), sb("od3", [P, 2, NG, 512])
        gate, x = sb("gate", [P, 2, 3 * D]), sb("x", [P, 2, D])
        lse, wts, lm = sb("lse", [P, 2, NG, H]), sb("wts", [P, NG, H]), sb("lm", [P, 2, H])
        aT, m, t, mT = sb("aT", [P, KB, P]), sb("m", [P, 2, D]), sb("t", [P, 512]), sb("mT", [P, KD, P])
        h, n2, stat = sb("h", [P, D]), sb("n2", [P, D]), sb("stat", [P, 3])
        ps_a, ps_b = pb("ps_a", [P, 8, P]), pb("ps_b", [P, 2, 512])
        ps_m, ps_h = pb("ps_m", [P, KD, P]), pb("ps_h", [P, D])

        consts_in, set_up, moved = sem("consts_in"), sem("set_up"), sem("moved")
        wb_in, wo_in = [sem(f"wb_in{b}") for b in range(3)], sem("wo_in")
        a_in, g_in, x_in = ([sem(f"{n}_in{j}") for j in range(2)] for n in "agx")
        stored_h, stored_n = sem("stored_h"), sem("stored_n")
        lmax, lsub, lexp, lsum, lrec, wts_done = (signal(n) for n in ("lmax", "lsub", "lexp", "lsum", "lrec", "wts"))
        odw_done, od1_done, od_done = (signal(n) for n in ("odw", "od1", "od"))
        sig_done, a_t, aT_out = signal("sig"), signal("a_t", 2), signal("aT_out", 2)
        prod, gated, added = signal("prod", NGRP), signal("gated", NGRP), signal("added", NGRP)
        m_t, mT_out, h_prod, h_done = signal("m_t"), signal("mT_out", 2), signal("h_prod"), signal("h_done")
        sq_done, ln_done, rs_done, n2_done = (signal(n) for n in ("sq", "ln", "rs", "n2"))

        block = ctx.enter_context(nc.Block())
        N = NT + 1
        z = d["z"]

        class Turn:

            def __init__(self, i, j, n=P):
                self.turn, self.i, self.j, self.n = i * 2 + j, i, j, n

        def steps(eng, step):
            step(Turn(0, 0), None, None)
            step(Turn(0, 1), Turn(0, 0), None)
            with eng.Fori(0, NT // 2 - 1) as i:
                step(Turn(i + 1, 0), Turn(i, 1), Turn(i, 0))
                step(Turn(i + 1, 1), Turn(i + 1, 0), Turn(i, 1))
            last = NT // 2
            step(Turn(last, 0, NS), Turn(last - 1, 1), Turn(last - 1, 0))
            step(None, Turn(last, 0, NS), Turn(last - 1, 1))
            step(None, None, Turn(last, 0, NS))

        def rows(t):
            return bass.ds(t.turn * P, P) if t.n == P else slice(SEQ, ROWS)

        @block.sync
        def _(sp):
            for s in signals:
                s.prime(sp)
            sp.sem_inc(stored_h, 16)
            sp.sem_inc(stored_n, 16)

            def load_x(t):
                src = d["x"][0][rows(t), :] if t.n == P else d["x"][1]
                sp.dma_start(x[0:t.n, t.j, :], src).then_inc(x_in[t.j], 16)

            def pre(t):
                turn, j, n, r = t.turn, t.j, t.n, rows(t)
                sp.wait_ge(a_t.sem, a_t.at(turn, back=2))
                if n == P:
                    sp.dma_start(a[:, j, 0:D], d["acts"][r, 0:D]).then_inc(a_in[j], 16)
                    sp.dma_start(a[:, j, 1536:2048], d["acts"][r, 1536:2048]).then_inc(a_in[j], 16)
                    sp.dma_start(lse[:, j], d["lse"][:, r, :].rearrange("g t h -> t g h")).then_inc(a_in[j], 16)
                    sp.dma_start(od3[:, j], d["od"][:, r, :].rearrange("g t n -> t g n")).then_inc(a_in[j], 16)
                else:
                    for q in range(4):
                        sp.dma_start(a[0:n, j, q * 512:(q + 1) * 512], d["acts"][r, q * 512:(q + 1) * 512]).then_inc(a_in[j], 16)
                sp.wait_ge(gated.sem, gated.at(turn, back=2))
                sp.dma_start(gate[0:n, j, :], z[r, C_GATE:C_GATE + 3 * D]).then_inc(g_in[j], 16)

            def step(p, f, b):
                if p:
                    pre(p)
                    if b is None:
                        load_x(p)
                if b:
                    sp.wait_ge(h_done.sem, h_done.at(b.turn))
                    sp.dma_start(d["h"][rows(b), :], h[0:b.n]).then_inc(stored_h, 16)
                    if p:
                        load_x(p)
                    sp.wait_ge(n2_done.sem, n2_done.at(b.turn))
                    sp.dma_start(d["n2"][rows(b), :], n2[0:b.n]).then_inc(stored_n, 16)

            steps(sp, step)
            sp.wait_ge(stored_h, 16 * (N + 1))
            sp.wait_ge(stored_n, 16 * (N + 1))

        @block.gpsimd
        def _(pool):
            weights = lambda n: d[n].rearrange("(k p) n -> p k n", p=P)
            for dst, src, arrived in ((ident[:], d["ident"], consts_in), (g2[:], d["ln2_g"].partition_broadcast(P), consts_in),
                                      (wb[:, 0:8], weights("w_br_gla"), wb_in[0]), (wb[:, 8:12], weights("w_br_dil"), wb_in[1]),
                                      (wb[:, 12:16], weights("w_br_mem"), wb_in[2]), (wo[:], weights("w_out"), wo_in)):
                pool.dma_start(dst, src).then_inc(arrived, 16)

            moves = [(d["mem_v_p"], d["zm"][:, 512:1024])]
            for name, wd, g in CACHES:
                keep = min(wd, SEQ)
                v_cols = slice(C_DIL + g * 1536 + 1024, C_DIL + g * 1536 + 1536)
                moves += [(d[f"{name}_p"], d["kr"][g][SEQ - keep:SEQ, :] if name[1] == "k" else z[SEQ - keep:SEQ, v_cols]),
                          (d[f"{name}_s"][:, wd - DEC_T:wd, :], (d["ks"][g] if name[1] == "k" else z[SEQ:ROWS, v_cols])
                           .rearrange("(b t) n -> b t n", b=DEC_B))]
            for dst, src in moves:
                pool.dma_start(dst, src).then_inc(moved, 16)

            def step(p, f, b):
                if p and p.n == P:
                    pool.wait_ge(wts_done.sem, wts_done.at(p.turn))
                    pool.wait_ge(a_in[p.j], p.i * 64 + 64)
                    od_heads = od3[:, p.j].rearrange("p g (h e) -> p (g h) e", e=P)
                    nc.gpsimd.tensor_tensor(od_heads, od_heads,
                                            wts[:].rearrange("p g h -> p (g h)").unsqueeze(2).to_broadcast([P, NG * H, P]),
                                            ALU.mult).then_inc(odw_done.sem, 1)

            steps(pool, step)
            pool.wait_ge(moved, 16 * len(moves))

        @block.scalar
        def _(act):
            act.wait_ge(set_up, 1)

            def step(p, f, b):
                if f:
                    for half in range(2):
                        act.wait_ge(a_t.sem, a_t.at(f.turn, half + 1))
                        if half == 0:
                            act.wait_ge(prod.sem, prod.at(f.turn, back=1))
                        nc.scalar.copy(aT[:, 8 * half:8 * half + 8, 0:f.n], ps_a[:, :, 0:f.n]).then_inc(aT_out.sem, 1)
                if b:
                    act.wait_ge(m_t.sem, m_t.at(b.turn))
                    act.wait_ge(h_prod.sem, h_prod.at(b.turn, back=1))
                    for half in range(2):
                        k = slice(4 * half, 4 * half + 4)
                        nc.scalar.copy(mT[:, k, 0:b.n], ps_m[:, k, 0:b.n]).then_inc(mT_out.sem, 1)
                if p:
                    act.wait_ge(g_in[p.j], p.i * 16 + 16)
                    nc.scalar.activation(gate[0:p.n, p.j], gate[0:p.n, p.j], ACT.Sigmoid).then_inc(sig_done.sem, 1)
                    if p.n == P:
                        act.wait_ge(lsub.sem, lsub.at(p.turn))
                        nc.scalar.activation(lse[:, p.j], lse[:, p.j], ACT.Exp).then_inc(lexp.sem, 1)
                if b:
                    turn, n = b.turn, b.n
                    act.wait_ge(h_done.sem, h_done.at(turn))
                    act.wait_ge(stored_n, turn * 16 + 16)
                    nc.scalar.activation(n2[0:n], h[0:n], ACT.Square, accum_out=stat[0:n, 0:1]).then_inc(sq_done.sem, 1)
                    act.wait_ge(sq_done.sem, sq_done.at(turn))
                    nc.scalar.activation(stat[0:n, 1:2], stat[0:n, 0:1], ACT.Ln, bias=eps[0:n], scale=1.0 / D).then_inc(ln_done.sem, 1)
                    act.wait_ge(ln_done.sem, ln_done.at(turn))
                    nc.scalar.activation(stat[0:n, 2:3], stat[0:n, 1:2], ACT.Exp, scale=-0.5).then_inc(rs_done.sem, 1)

            steps(act, step)

        @block.vector
        def _(dve):
            nc.vector.memset(eps[:], EPS).then_inc(set_up, 1)
            dve.wait_ge(consts_in, 16 * 2)

            def pre(t):
                turn, i, j, n = t.turn, t.i, t.j, t.n
                if n == P:
                    by_head = lse[:, j].rearrange("p g h -> p h g")
                    wide = lambda v: v.unsqueeze(1).to_broadcast([P, NG, H])
                    dve.wait_ge(a_in[j], i * 64 + 64)
                    nc.vector.tensor_reduce(lm[:, 0], by_head, axis=AX, op=ALU.max).then_inc(lmax.sem, 1)
                    dve.wait_ge(lmax.sem, lmax.at(turn))
                    nc.vector.tensor_tensor(lse[:, j], lse[:, j], wide(lm[:, 0]), ALU.subtract).then_inc(lsub.sem, 1)
                    dve.wait_ge(lexp.sem, lexp.at(turn))
                    nc.vector.tensor_reduce(lm[:, 1], by_head, axis=AX, op=ALU.add).then_inc(lsum.sem, 1)
                    dve.wait_ge(lsum.sem, lsum.at(turn))
                    nc.vector.reciprocal(lm[:, 0], lm[:, 1]).then_inc(lrec.sem, 1)
                    dve.wait_ge(lrec.sem, lrec.at(turn))
                    dve.wait_ge(odw_done.sem, odw_done.at(turn, back=1))
                    nc.vector.tensor_tensor(wts[:], lse[:, j], wide(lm[:, 0]), ALU.mult).then_inc(wts_done.sem, 1)
                    dve.wait_ge(odw_done.sem, odw_done.at(turn))
                    nc.vector.tensor_tensor(od3[:, j, 0], od3[:, j, 0], od3[:, j, 1], ALU.add).then_inc(od1_done.sem, 1)
                    dve.wait_ge(od1_done.sem, od1_done.at(turn))
                    dve.wait_ge(a_t.sem, a_t.at(turn, back=2))
                    nc.vector.tensor_tensor(a[:, j, D:D + 512], od3[:, j, 0], od3[:, j, 2], ALU.add).then_inc(od_done.sem, 1)
                else:
                    dve.wait_ge(a_in[j], i * 64 + 64)
                    dve.sem_inc(od_done.sem, 1)

            def front(f):
                turn, j, n = f.turn, f.j, f.n
                dve.wait_ge(sig_done.sem, sig_done.at(turn))
                dve.wait_ge(m_t.sem, m_t.at(turn, back=2))
                for q in range(NGRP):
                    b, c = divmod(q, 2)
                    cols = slice(512 * c, 512 * c + 512)
                    dve.wait_ge(prod.sem, prod.at(turn, q + 1))
                    g = gate[0:n, j, b * D + 512 * c:b * D + 512 * c + 512]
                    if b == 0:
                        nc.vector.tensor_tensor(m[0:n, j, cols], ps_b[0:n, q % 2], g, ALU.mult).then_inc(gated.sem, 1)
                        dve.sem_inc(added.sem, 1)
                    else:
                        dve.wait_ge(added.sem, added.at(turn, q))
                        dve.wait_ge(gated.sem, gated.at(turn, q))
                        nc.vector.tensor_tensor(t[0:n], ps_b[0:n, q % 2], g, ALU.mult).then_inc(gated.sem, 1)
                        dve.wait_ge(gated.sem, gated.at(turn, q + 1))
                        nc.vector.tensor_tensor(m[0:n, j, cols], m[0:n, j, cols], t[0:n], ALU.add).then_inc(added.sem, 1)

            def back(t):
                turn, i, j, n = t.turn, t.i, t.j, t.n
                dve.wait_ge(h_prod.sem, h_prod.at(turn))
                dve.wait_ge(x_in[j], i * 16 + 16)
                dve.wait_ge(stored_h, turn * 16 + 16)
                dve.wait_ge(n2_done.sem, n2_done.at(turn, back=1))
                nc.vector.tensor_tensor(h[0:n], ps_h[0:n], x[0:n, j], ALU.add).then_inc(h_done.sem, 1)
                dve.wait_ge(rs_done.sem, rs_done.at(turn))
                nc.vector.scalar_tensor_tensor(out=n2[0:n], in0=h[0:n], scalar=stat[0:n, 2:3], in1=g2[0:n],
                                               op0=ALU.mult, op1=ALU.mult).then_inc(n2_done.sem, 1)

            def step(p, f, b):
                if f:
                    front(f)
                if p:
                    pre(p)
                if b:
                    back(b)

            steps(dve, step)

        @block.tensor
        def _(pe):
            pe.wait_ge(consts_in, 16 * 2)

            def front(t):
                turn, i, j, n = t.turn, t.i, t.j, t.n
                first = isinstance(turn, int) and turn == 0
                pe.wait_ge(od_done.sem, od_done.at(turn))
                pe.wait_ge(a_in[j], i * 64 + 64)
                for half in range(2):
                    pe.wait_ge(aT_out.sem, aT_out.at(turn, half, back=0))
                    for k in range(8):
                        b = 8 * half + k
                        last = nc.tensor.transpose(ps_a[:, k, 0:n], a[0:n, j, b * P:(b + 1) * P], ident[0:n, 0:n])
                    last.then_inc(a_t.sem, 1)
                pe.wait_ge(aT_out.sem, aT_out.at(turn))
                for q in range(NGRP):
                    b, c = divmod(q, 2)
                    k0, k1 = BRANCH[b]
                    if first and c == 0:
                        pe.wait_ge(wb_in[b], 16)
                    if q >= 2:
                        pe.wait_ge(gated.sem, gated.at(turn, q - 1))
                    else:
                        pe.wait_ge(gated.sem, gated.at(turn, NGRP + q - 1, back=1))
                    for k in range(k0, k1):
                        last = nc.tensor.matmul(ps_b[0:n, q % 2], aT[:, k, 0:n], wb[:, k, 512 * c:512 * c + 512],
                                                start=(k == k0), stop=(k == k1 - 1))
                    last.then_inc(prod.sem, 1)
                if first:
                    pe.wait_ge(wo_in, 16)

            def back(t):
                turn, j, n = t.turn, t.j, t.n
                pe.wait_ge(added.sem, added.at(turn))
                pe.wait_ge(gated.sem, gated.at(turn))
                pe.wait_ge(mT_out.sem, mT_out.at(turn, back=1))
                for k in range(KD):
                    last = nc.tensor.transpose(ps_m[:, k, 0:n], m[0:n, j, k * P:(k + 1) * P], ident[0:n, 0:n])
                last.then_inc(m_t.sem, 1)
                pe.wait_ge(mT_out.sem, mT_out.at(turn))
                pe.wait_ge(h_done.sem, h_done.at(turn, back=1))
                for c in range(2):
                    for k in range(KD):
                        last = nc.tensor.matmul(ps_h[0:n, 512 * c:512 * c + 512], mT[:, k, 0:n], wo[:, k, 512 * c:512 * c + 512],
                                                start=(k == 0), stop=(k == KD - 1))
                last.then_inc(h_prod.sem, 1)

            def step(p, f, b):
                if f:
                    front(f)
                if b:
                    back(b)

            steps(pe, step)


def experts(nc, d):
    import concourse.bass as bass
    from concourse import mybir
    from contextlib import ExitStack
    fp32, u32, ACT, ALU = mybir.dt.float32, mybir.dt.uint32, mybir.ActivationFunctionType, mybir.AluOpType
    AX = mybir.AxisListType.X
    TILES = NT + 1
    K = TOPK
    SLOTS = 8
    USES = K // SLOTS
    LOW = -3e38

    with ExitStack() as ctx:
        sb = lambda n, s, t=fp32: ctx.enter_context(nc.sbuf_tensor("ex_" + n, s, t))
        pb = lambda n, s: ctx.enter_context(nc.psum_tensor("ex_" + n, s, fp32))
        sem = stage_semaphores(nc, ctx, "ex_")
        signals = []

        def signal(n, per=1):
            signals.append(Signal(sem(n), per))
            return signals[-1]

        ident, iota = sb("ident", [P, P]), sb("iota", [P, K])
        wq, keysT = sb("wq", [P, KD, PH * 256]), sb("keysT", [P, 2 * PH, NKEY])
        u_rows, v_rows = sb("u_rows", [P, SLOTS, D]), sb("v_rows", [P, SLOTS, D])
        n2r, n2u, n2T = sb("n2r", [P, D]), sb("n2u", [P, D]), sb("n2T", [P, KD, P])
        h, yo = sb("h", [P, D]), sb("yo", [P, D])
        qh, qhT, sc, sc2 = sb("qh", [P, 256]), sb("qhT", [P, 2, P]), sb("sc", [P, 2, NKEY]), sb("sc2", [P, 2, NKEY])
        top, top_at = sb("top", [P, 2, K]), sb("top_at", [P, 2, K], u32)
        cand, cand2 = sb("cand", [P, K, K]), sb("cand2", [P, K * K])
        best, best_at = sb("best", [P, K]), sb("best_at", [P, K], u32)
        pair, pair_f, at_f = sb("pair", [P, 2, K], u32), sb("pair_f", [P, 2, K]), sb("at_f", [P, 2, K])
        hot, picked = sb("hot", [P, 2 * K, K]), sb("picked", [P, 2, K])
        ex, esum, erec = sb("ex", [P, K]), sb("esum", [P, 1]), sb("erec", [P, 1])
        E, gates = sb("E", [P, TILES * NEXP], u32), sb("gates", [P, TILES * NEXP])
        idx = sb("idx", [P, 2, 2, K], u32)
        dots, gel, w = sb("dots", [P, K]), sb("gel", [P, K]), sb("w", [P, K])
        diag = sb("diag", [P, K, P])
        ps_y, ps_t = pb("ps_y", [P, D]), pb("ps_t", [P, KD, P])
        ps_q, ps_qt, ps_s = pb("ps_q", [P, 256]), pb("ps_qt", [P, 2, P]), pb("ps_s", [P, 2, P])

        consts_in, keys_in, keys_t, keys_out = sem("consts_in"), sem("keys_in"), sem("keys_t"), sem("keys_out")
        passed = {e.engine: sem(f"passed{n}") for n, e in enumerate((nc.sync, nc.gpsimd, nc.vector, nc.tensor))}
        n2r_in, n2u_in, h_in, y_stored = sem("n2r_in"), sem("n2u_in"), sem("h_in"), sem("y_stored")
        n2_t, n2T_out, h_used, y_sum, y_done = (signal(n) for n in ("n2_t", "n2T_out", "h_used", "y_sum", "y_done"))
        q_done, q_out, q_t, qT_out, s_done, s_out = (signal(n) for n in ("q", "q_out", "q_t", "qT_out", "s", "s_out"))
        top1, at1, cut, top2, at2 = (signal(n, 2) for n in ("top1", "at1", "cut", "top2", "at2"))
        cand_done, best1, bat1, ccut, best2, bat2 = (signal(n) for n in ("cand", "best1", "bat1", "ccut", "best2", "bat2"))
        atf_done, pair_done, pairf_done, hot_done, sel_done, pick_done = (signal(n) for n in ("atf", "pair", "pairf", "hot", "sel", "pick"))
        E_done, ex_in, ex_out, er_done, gate_done = (signal(n) for n in ("E", "ex_in", "ex_out", "er", "gate"))
        u_in, v_in = [sem(f"u_in{i}") for i in range(SLOTS)], [sem(f"v_in{i}") for i in range(SLOTS)]
        idx_sets = [signal("idx_u"), signal("idx_v")]
        dot_done, gel_done, w_done = signal("dot", K), signal("gel"), signal("w")
        diag_done, v_done = signal("diag", K), signal("v", K)

        block = ctx.enter_context(nc.Block())

        class Turn:

            def __init__(self, tile, head, odd, n):
                self.tile, self.head, self.odd, self.n = tile, head, odd, n
                self.turn = tile * PH + head
                self.col = bass.ds(tile * NEXP + head * K, K) if not isinstance(self.turn, int) else slice(self.turn * K, self.turn * K + K)

            def wide(self, size, first=0, n=None):
                at, n = self.head * size + first, n or size
                return slice(at, at + n) if isinstance(self.head, int) else bass.ds(at, n)

        def is_head(part, head):
            return isinstance(part.head, int) and part.head == head

        def steps(eng, step):
            def tile_steps(tile, before, n):
                for head in range(4):
                    step(lambda lag: Turn(tile, head - lag, (head - lag) % 2, n) if head >= lag else
                         None if before is None else Turn(before, PH + head - lag, (head - lag) % 2, P))
                with eng.Fori(0, (PH - 4) // 2) as two:
                    for odd in range(2):
                        step(lambda lag: Turn(tile, two * 2 + (4 + odd - lag), (odd - lag) % 2, n))

            tile_steps(0, None, P)
            with eng.Fori(0, TILES - 2) as i:
                tile_steps(i + 1, i, P)
            tile_steps(TILES - 1, TILES - 2, NS)
            for over in range(3):
                step(lambda lag: Turn(TILES - 1, PH + over - lag, (over - lag) % 2, NS) if over < lag else None)

        def settle(eng):
            eng.sem_inc(passed[eng.engine], 1)

        def rows(tile, n):
            return bass.ds(tile * P, P) if n == P else slice(SEQ, ROWS)

        @block.sync
        def _(sp):
            for s in signals:
                s.prime(sp)
            sp.dma_start(ident[:], d["ident"]).then_inc(consts_in, 16)
            sp.dma_start(iota[:], d["iota"]).then_inc(consts_in, 16)
            for g in range(2 * PH):
                sp.dma_start(u_rows[:, g // 8, (g % 8) * P:(g % 8 + 1) * P], d["peer_keys"][g // 2, g % 2]).then_inc(keys_in, 16)
            sp.dma_start(wq[:], d["peer_wq"].rearrange("(k p) n -> p k n", p=P)).then_inc(consts_in, 16)

            sp.sem_inc(y_stored, 16)

            def store_y(tile, n):
                sp.wait_ge(y_done.sem, y_done.at(tile))
                y = d["y_prompt"][rows(tile, n), :] if n == P else d["y_sample"]
                sp.dma_start(y, yo[0:n]).then_inc(y_stored, 16)

            def tile_loads(tile, before, n):
                sp.wait_ge(n2_t.sem, n2_t.at(tile, back=1))
                sp.dma_start(n2r[0:n], d["n2"][rows(tile, n), :]).then_inc(n2r_in, 16)
                sp.wait_ge(dot_done.sem, dot_done.at(tile * PH, back=1))
                sp.dma_start(n2u[0:n], d["n2"][rows(tile, n), :]).then_inc(n2u_in, 16)
                sp.wait_ge(h_used.sem, h_used.at(tile, back=1))
                sp.dma_start(h[0:n], d["h"][rows(tile, n), :]).then_inc(h_in, 16)
                if before is not None:
                    store_y(before, P)
                settle(sp)

            tile_loads(0, None, P)
            with sp.Fori(0, TILES - 2) as i:
                tile_loads(i + 1, i, P)
            tile_loads(TILES - 1, TILES - 2, NS)
            store_y(TILES - 1, NS)
            sp.wait_ge(y_stored, 16 * TILES + 16)

        @block.gpsimd
        def _(pool):
            def step(ago):
                parts = ((ago(1), 0, u_rows, dot_done, u_in, "peer_u"), (ago(2), 1, v_rows, v_done, v_in, "peer_v"))
                for turn, which, _, done, _, _ in parts:
                    if turn:
                        pool.wait_ge(E_done.sem, E_done.at(turn.turn))
                        pool.wait_ge(done.sem, done.at(turn.turn, back=2))
                        settle(pool)
                        nc.gpsimd.tensor_copy(idx[0:turn.n, which, turn.odd], E[0:turn.n, turn.col]).then_inc(idx_sets[which].sem, 1)
                        pool.wait_ge(idx_sets[which].sem, idx_sets[which].at(turn.turn))
                for k in range(K):
                    for turn, which, slots, done, arrived, table in parts:
                        if turn:
                            pool.wait_ge(done.sem, done.at(turn.turn, k - SLOTS + 1) if k >= SLOTS else done.at(turn.turn, K - SLOTS + k + 1, back=1))
                            settle(pool)
                            pool.indirect_dma_start(out=slots[0:turn.n, k % SLOTS, :], out_offset=None, in_=d[table],
                                                    in_offset=bass.IndirectOffsetOnAxis(ap=idx[0:turn.n, which, turn.odd, k:k + 1], axis=0))\
                                .then_inc(arrived[k % SLOTS], 16)

            pool.wait_ge(keys_t, 2)
            steps(pool, step)

        @block.scalar
        def _(act):
            for g in range(2):
                act.wait_ge(keys_t, g + 1)
                nc.scalar.copy(keysT[:, 8 * g:8 * g + 8], ps_t[:]).then_inc(keys_out, 1)

            def step(ago):
                sums, exps, dotted, scored = ago(3), ago(1), ago(2), ago(0)
                if sums:
                    turn, n = sums.turn, sums.n
                    act.wait_ge(w_done.sem, w_done.at(turn))
                    for k in range(K):
                        act.wait_ge(v_done.sem, v_done.at(turn, k + 1, back=1))
                        nc.scalar.mul(diag[0:n, k, 0:n], ident[0:n, 0:n], w[0:n, k:k + 1]).then_inc(diag_done.sem, 1)
                if exps:
                    act.wait_ge(ex_in.sem, ex_in.at(exps.turn))
                    nc.scalar.activation(ex[0:exps.n], ex[0:exps.n], ACT.Exp, accum_out=esum[0:exps.n]).then_inc(ex_out.sem, 1)
                if scored:
                    tile, turn, n = scored.tile, scored.turn, scored.n
                    if is_head(scored, 0):
                        act.wait_ge(n2_t.sem, n2_t.at(tile))
                        act.wait_ge(q_done.sem, q_done.at(tile * PH, back=1))
                        nc.scalar.copy(n2T[:, :, 0:n], ps_t[:, :, 0:n]).then_inc(n2T_out.sem, 1)
                    act.wait_ge(q_done.sem, q_done.at(turn))
                    nc.scalar.copy(qh[0:n], ps_q[0:n]).then_inc(q_out.sem, 1)
                    act.wait_ge(q_t.sem, q_t.at(turn))
                    nc.scalar.copy(qhT[:, :, 0:n], ps_qt[:, :, 0:n]).then_inc(qT_out.sem, 1)
                    act.wait_ge(s_done.sem, s_done.at(turn))
                    act.wait_ge(cut.sem, cut.at(turn, back=1))
                    act.wait_ge(at1.sem, at1.at(turn, back=1))
                    nc.scalar.copy(sc[0:n], ps_s[0:n]).then_inc(s_out.sem, 1)
                if dotted:
                    act.wait_ge(dot_done.sem, dot_done.at(dotted.turn))
                    act.wait_ge(w_done.sem, w_done.at(dotted.turn, back=1))
                    nc.scalar.activation(gel[0:dotted.n], dots[0:dotted.n], ACT.Gelu).then_inc(gel_done.sem, 1)
                if sums and is_head(sums, PH - 1):
                    act.wait_ge(y_sum.sem, y_sum.at(sums.tile))
                    act.wait_ge(y_stored, sums.tile * 16 + 16)
                    nc.scalar.copy(yo[0:sums.n], ps_y[0:sums.n]).then_inc(y_done.sem, 1)

            steps(act, step)

        @block.vector
        def _(dve):
            dve.wait_ge(consts_in, 48)

            def route(turn, n, col):
                wait = lambda s, done=None: dve.wait_ge(s.sem, s.at(turn, done))
                wait(s_out)
                settle(dve)
                for c in range(2):
                    nc.vector.max(top[0:n, c, 0:8], sc[0:n, c]).then_inc(top1.sem, 1)
                for c in range(2):
                    wait(top1, c + 1)
                    settle(dve)
                    nc.vector.max_index(top_at[0:n, c, 0:8], top[0:n, c, 0:8], sc[0:n, c]).then_inc(at1.sem, 1)
                    nc.vector.match_replace(sc2[0:n, c], top[0:n, c, 0:8], sc[0:n, c], LOW).then_inc(cut.sem, 1)
                for c in range(2):
                    wait(cut, c + 1)
                    settle(dve)
                    nc.vector.max(top[0:n, c, 8:16], sc2[0:n, c]).then_inc(top2.sem, 1)
                for c in range(2):
                    wait(top2, c + 1)
                    settle(dve)
                    nc.vector.max_index(top_at[0:n, c, 8:16], top[0:n, c, 8:16], sc2[0:n, c]).then_inc(at2.sem, 1)
                nc.vector.tensor_tensor(cand[0:n], top[0:n, 0].unsqueeze(2).to_broadcast([n, K, K]),
                                        top[0:n, 1].unsqueeze(1).to_broadcast([n, K, K]), ALU.add).then_inc(cand_done.sem, 1)
                wait(at2)
                wait(at1)
                nc.vector.tensor_copy(at_f[0:n], top_at[0:n]).then_inc(atf_done.sem, 1)
                wait(cand_done)
                flat = cand[0:n].rearrange("p a b -> p (a b)")
                settle(dve)
                nc.vector.max(best[0:n, 0:8], flat).then_inc(best1.sem, 1)
                wait(best1)
                settle(dve)
                nc.vector.max_index(best_at[0:n, 0:8], best[0:n, 0:8], flat).then_inc(bat1.sem, 1)
                nc.vector.match_replace(cand2[0:n], best[0:n, 0:8], flat, LOW).then_inc(ccut.sem, 1)
                wait(ccut)
                settle(dve)
                nc.vector.max(best[0:n, 8:16], cand2[0:n]).then_inc(best2.sem, 1)
                wait(best2)
                settle(dve)
                nc.vector.max_index(best_at[0:n, 8:16], best[0:n, 8:16], cand2[0:n]).then_inc(bat2.sem, 1)
                dve.wait_ge(gate_done.sem, gate_done.at(turn, back=1))
                nc.vector.tensor_scalar(ex[0:n], best[0:n], best[0:n, 0:1], None, ALU.subtract).then_inc(ex_in.sem, 1)
                wait(bat1)
                wait(bat2)
                nc.vector.tensor_scalar(pair[0:n, 0], best_at[0:n], 4, None, ALU.logical_shift_right)
                nc.vector.tensor_scalar(pair[0:n, 1], best_at[0:n], K - 1, None, ALU.bitwise_and).then_inc(pair_done.sem, 1)
                wait(pair_done)
                nc.vector.tensor_copy(pair_f[0:n], pair[0:n]).then_inc(pairf_done.sem, 1)
                wait(pairf_done)
                nc.vector.tensor_tensor(hot[0:n], pair_f[0:n].rearrange("p c k -> p (c k)").unsqueeze(2).to_broadcast([n, 2 * K, K]),
                                        iota[0:n].unsqueeze(1).to_broadcast([n, 2 * K, K]), ALU.is_equal).then_inc(hot_done.sem, 1)
                wait(hot_done)
                wait(atf_done)
                by_half = hot[0:n].rearrange("p (c k) m -> p c k m", c=2)
                nc.vector.tensor_tensor(by_half, by_half, at_f[0:n].unsqueeze(2).to_broadcast([n, 2, K, K]), ALU.mult).then_inc(sel_done.sem, 1)
                wait(sel_done)
                nc.vector.tensor_reduce(picked[0:n].rearrange("p c k -> p (c k)"), hot[0:n], axis=AX, op=ALU.add).then_inc(pick_done.sem, 1)
                wait(pick_done)
                nc.vector.scalar_tensor_tensor(out=E[0:n, col], in0=picked[0:n, 0], scalar=float(NKEY), in1=picked[0:n, 1],
                                               op0=ALU.mult, op1=ALU.add).then_inc(E_done.sem, 1)
                wait(ex_out)
                nc.vector.reciprocal(erec[0:n], esum[0:n]).then_inc(er_done.sem, 1)
                wait(er_done)
                nc.vector.tensor_scalar(gates[0:n, col], ex[0:n], erec[0:n, 0:1], None, ALU.mult).then_inc(gate_done.sem, 1)

            def step(ago):
                routed, dotted = ago(0), ago(1)
                if routed:
                    route(routed.turn, routed.n, routed.col)
                if dotted:
                    turn, n = dotted.turn, dotted.n
                    if is_head(dotted, 0):
                        dve.wait_ge(n2u_in, dotted.tile * 16 + 16)
                    dve.wait_ge(gel_done.sem, gel_done.at(turn, back=1))
                    for k in range(K):
                        dve.wait_ge(u_in[k % SLOTS], turn * (16 * USES) + 16 * (k // SLOTS + 1))
                        settle(dve)
                        row = u_rows[0:n, k % SLOTS, :]
                        nc.vector.tensor_tensor_reduce(out=row, in0=row, in1=n2u[0:n], scale=1.0, scalar=0.0, op0=ALU.mult,
                                                       op1=ALU.add, accum_out=dots[0:n, k:k + 1]).then_inc(dot_done.sem, 1)
                    dve.wait_ge(gel_done.sem, gel_done.at(turn))
                    dve.wait_ge(gate_done.sem, gate_done.at(turn))
                    dve.wait_ge(diag_done.sem, diag_done.at(turn, back=1))
                    nc.vector.tensor_tensor(w[0:n], gel[0:n], gates[0:n, dotted.col], ALU.mult).then_inc(w_done.sem, 1)

            steps(dve, step)

        @block.tensor
        def _(pe):
            pe.wait_ge(consts_in, 48)
            pe.wait_ge(keys_in, 16 * 2 * PH)
            for g in range(2):
                if g:
                    pe.wait_ge(keys_out, 1)
                for k in range(8):
                    last = nc.tensor.transpose(ps_t[:, k, :], u_rows[:, g, k * P:(k + 1) * P], ident[:])
                last.then_inc(keys_t, 1)
            pe.wait_ge(keys_out, 2)

            def sum_rows(part, ks):
                turn, n = part.turn, part.n
                if is_head(part, 0) and 0 in ks:
                    pe.wait_ge(h_in, part.tile * 16 + 16)
                    pe.wait_ge(y_done.sem, y_done.at(part.tile, back=1))
                    for c in range(2):
                        last = nc.tensor.matmul(ps_y[0:n, 512 * c:512 * c + 512], ident[0:n, 0:n], h[0:n, 512 * c:512 * c + 512],
                                                start=True, stop=False, skip_group_check=True)
                    last.then_inc(h_used.sem, 1)
                for k in ks:
                    pe.wait_ge(diag_done.sem, diag_done.at(turn, k + 1))
                    pe.wait_ge(v_in[k % SLOTS], turn * (16 * USES) + 16 * (k // SLOTS + 1))
                    if n < P:
                        settle(pe)
                    end = is_head(part, PH - 1) and k == K - 1
                    for c in range(2):
                        last = nc.tensor.matmul(ps_y[0:n, 512 * c:512 * c + 512], diag[0:n, k, 0:n],
                                                v_rows[0:n, k % SLOTS, 512 * c:512 * c + 512],
                                                start=False, stop=end, skip_group_check=True)
                    last.then_inc(v_done.sem, 1)
                    if end:
                        pe.wait_ge(v_done.sem, v_done.at(turn))
                        pe.sem_inc(y_sum.sem, 1)

            def step(ago):
                scored, sums = ago(0), ago(3)
                if sums:
                    sum_rows(sums, range(K // 2))
                if scored:
                    tile, turn, n = scored.tile, scored.turn, scored.n
                    if is_head(scored, 0):
                        pe.wait_ge(n2r_in, tile * 16 + 16)
                        settle(pe)
                        for k in range(KD):
                            last = nc.tensor.transpose(ps_t[:, k, 0:n], n2r[0:n, k * P:(k + 1) * P], ident[0:n, 0:n])
                        last.then_inc(n2_t.sem, 1)
                        pe.wait_ge(n2T_out.sem, n2T_out.at(tile))
                    pe.wait_ge(q_out.sem, q_out.at(turn, back=1))
                    for k in range(KD):
                        last = nc.tensor.matmul(ps_q[0:n], n2T[:, k, 0:n], wq[:, k, scored.wide(256)], start=(k == 0), stop=(k == KD - 1))
                    last.then_inc(q_done.sem, 1)
                    pe.wait_ge(q_out.sem, q_out.at(turn))
                    pe.wait_ge(qT_out.sem, qT_out.at(turn, back=1))
                    settle(pe)
                    for c in range(2):
                        last = nc.tensor.transpose(ps_qt[:, c, 0:n], qh[0:n, c * P:(c + 1) * P], ident[0:n, 0:n])
                    last.then_inc(q_t.sem, 1)
                    pe.wait_ge(qT_out.sem, qT_out.at(turn))
                    pe.wait_ge(s_out.sem, s_out.at(turn, back=1))
                    for c in range(2):
                        last = nc.tensor.matmul(ps_s[0:n, c, :], qhT[:, c, 0:n],
                                                keysT[:].rearrange("p g k -> p (g k)")[:, scored.wide(2 * NKEY, c * NKEY, NKEY)], start=True, stop=True)
                    last.then_inc(s_done.sem, 1)
                if sums:
                    sum_rows(sums, range(K // 2, K))

            steps(pe, step)


_INS = ["x_prompt", "x_sample", "mem_prompt", "state_gla",
        "cache_dil_k0", "cache_dil_v0", "cache_dil_k1", "cache_dil_v1", "cache_dil_k2", "cache_dil_v2",
        "cache_mem_k", "cache_mem_v", "ln1_g", "w_in", "gla_wg2", "gla_bg", "gla_onorm_g", "dil_qn_g", "dil_kn_g",
        "mem_norm_g", "w_mem_kv", "mem_qn_g", "mem_kn_g", "w_br_gla", "w_br_dil", "w_br_mem", "w_out", "ln2_g",
        "peer_wq", "peer_keys", "peer_u", "peer_v"]
_OUTS = [("y_prompt", (1, SEQ, D)), ("y_sample", (DEC_B, DEC_T, D)), ("gla_state_p", (1, H, DK, DV))]
_OUTS += [(f"{name}_p", (1, min(wd, SEQ), H, DK)) for name, wd, _ in CACHES]
_OUTS += [("mem_k_p", (1, MEM, H, DK)), ("mem_v_p", (1, MEM, H, DK)), ("gla_state_s", (DEC_B, H, DK, DV))]
_OUTS += [(f"{name}_s", (DEC_B, wd, H, DK)) for name, wd, _ in CACHES]
_SCRATCH = [("z", (ROWS, COLS)), ("zm", (MEM, D)), ("acts", (ROWS, 2 * D)), ("od", (NG, SEQ, 512)), ("lse", (NG, SEQ, H)),
            ("kr", (NG, SEQ, 512)), ("ks", (NG, NS, 512)), ("h", (ROWS, D)), ("n2", (ROWS, D))]


def constants():
    import numpy as np
    f = np.float32
    allow = lambda c: np.where(c, f(0), f(NEG)).astype(f)
    q, k = np.arange(P)[:, None], np.arange(P)[None, :]
    s, t = np.arange(NS)[:, None], np.arange(NS)[None, :]
    pos = np.concatenate([np.arange(SEQ), WINDOWS[-1][0] + np.tile(np.arange(DEC_T), DEC_B)]).astype(f)
    half = DK // 2
    inv = f(10000.0) ** (-np.arange(half, dtype=f) / f(half))
    ang = pos[:, None] * inv.astype(f)[None, :]
    cos, sin = np.cos(ang), np.sin(ang)
    row = np.tile(np.arange(NS), H)[:, None]
    dec = np.zeros((P, NG, P + NS), f)
    dec[:, 0, :P] = allow(k >= row % DEC_T)
    dec[:, 0, P:] = allow((t // DEC_T == row // DEC_T) & (t <= row))
    dec[:, 1:, P:] = allow(t == row)[:, None, :]
    return {
        "ident": np.eye(P, dtype=f),
        "causal": (q <= k).astype(f),
        "mask_own": allow(k <= q), "mask_prev": allow(k >= q), "mask_pair": allow((k <= q) & (k // 64 == q // 64)),
        "rope": np.concatenate([cos, cos, -sin, sin], 1).astype(f),
        "restart": np.tile((np.arange(NS) % DEC_T != 0).astype(f), (P, 1)),
        "own": (s // DEC_T == np.arange(DEC_B)[None, :]).astype(f),
        "own_causal": ((s // DEC_T == t // DEC_T) & (s <= t)).astype(f),
        "dec_mask": dec,
        "iota": np.tile(np.arange(TOPK, dtype=f), (P, 1)),
    }


def build(nc, d):
    d["x"] = (d["x_prompt"].rearrange("b s n -> (b s) n"), d["x_sample"].rearrange("b t n -> (b t) n"))
    d["mem_prompt"] = d["mem_prompt"].rearrange("b m n -> (b m) n")
    d["y_prompt"] = d["y_prompt"].rearrange("b s n -> (b s) n")
    d["y_sample"] = d["y_sample"].rearrange("b t n -> (b t) n")
    d["gla_state_p"] = d["gla_state_p"].rearrange("b h p e -> (b h) p e")
    for name in ("mem_k_p", "mem_v_p", *(f"{c}_p" for c, _, _ in CACHES)):
        d[name] = d[name].rearrange("b m h e -> (b m) (h e)")
    for name in ("cache_mem_k", "cache_mem_v", *(f"{c}_s" for c, _, _ in CACHES), *(f"cache_dil_{kv}{g}" for kv in "kv" for g in range(NG))):
        d[name] = d[name].rearrange("b m h e -> b m (h e)")
    project(nc, d)
    gla(nc, d)
    gla_sample(nc, d)
    for group in range(NG + 1):
        attend(nc, d, group)
    decode(nc, d)
    merge(nc, d)
    experts(nc, d)


def kernel(**inputs):
    import numpy as _np
    import concourse.bacc as _bacc
    from concourse import mybir as _mybir
    from concourse.bass_utils import run_bass_kernel_spmd as _run

    nc = _bacc.Bacc("TRN2", target_bir_lowering=False, num_devices=1)
    arrays, d = {}, {}
    given = {name: _np.ascontiguousarray(inputs[name]) for name in _INS} | constants()
    for name, a in given.items():
        arrays[f"in_{name}"] = a
        d[name] = nc.dram_tensor(f"in_{name}", a.shape, _mybir.dt.from_np(a.dtype), kind="ExternalInput").ap()
    for name, shape in _OUTS:
        d[name] = nc.dram_tensor(f"out_{name}", shape, _mybir.dt.float32, kind="ExternalOutput").ap()
    for name, shape in _SCRATCH:
        d[name] = nc.dram_tensor(f"scratch_{name}", shape, _mybir.dt.float32, kind="Internal").ap()
    build(nc, d)
    r = _run(nc, [arrays], core_ids=[0])
    return tuple(r.results[0][f"out_{name}"] for name, _ in _OUTS)
```
